# Optimizing a Trainium2 kernel written in Bass

```python
import math, functools
import jax, jax.numpy as jnp
from jax import lax
import numpy as np

D_MODEL = 2048
BATCH = 1
SEQ = 256
DEPTH = 1
DEC_BATCH = 8
DEC_SEQ = 1
PAST_LEN = 1024
PAGE_SIZE = 128

N_BRANCH = 4
MIX_W = D_MODEL // N_BRANCH
FOX_HD = 128
FOX_H = MIX_W // FOX_HD
FOX_BLOCK = 128
FOX_BF_INIT = 5.0
S5_GROUP = 16
S5_G = MIX_W // S5_GROUP
S5_P = 64
HG_DK = 128
HG_DV = 128
HG_H = MIX_W // HG_DV
HG_CHUNK = 64
GM_CHUNK = 128
GM_GROUPS = 4
GM_GW = MIX_W // GM_GROUPS
D_FF = ((8 * D_MODEL // 3 + 255) // 256) * 256
DEEPNORM_ALPHA = (2 * DEPTH) ** 0.25
DEEPNORM_BETA = (8 * DEPTH) ** -0.25
LN_EPS = 1e-5
RMS_EPS = 1e-6
IN_SPLITS = (MIX_W, MIX_W, MIX_W, FOX_H, MIX_W, HG_H * HG_DK, HG_H * HG_DK, HG_H * HG_DV, HG_H * HG_DV, MIX_W, MIX_W, N_BRANCH * D_MODEL)
N_IN = sum(IN_SPLITS)

kernel_name = 'hybrid_fox_s5_hgrn2_gmlp_decode_step'

def layer_norm(x, g, b):
    xf = x.astype(jnp.float32)
    mu = jnp.mean(xf, axis=-1, keepdims=True)
    var = jnp.mean(jnp.square(xf - mu), axis=-1, keepdims=True)
    return ((xf - mu) * lax.rsqrt(var + LN_EPS) * g + b).astype(x.dtype)

def split_cols(z):
    bounds = np.cumsum(IN_SPLITS)[:-1].tolist()
    return jnp.split(z, bounds, axis=-1)

def fox_prompt(q, k, v, logf):
    B, L, H, hd = q.shape
    scale = hd ** -0.5
    c = jnp.cumsum(logf, axis=1)
    c_keys = c.transpose(0, 2, 1)
    nb = L // FOX_BLOCK
    q_blocks = q.reshape(B, nb, FOX_BLOCK, H, hd).transpose(1, 0, 2, 3, 4)
    c_blocks = c.reshape(B, nb, FOX_BLOCK, H).transpose(1, 0, 3, 2)
    k_pos = jnp.arange(L)

    def block(args):
        qi, ci, i = args
        q_pos = i * FOX_BLOCK + jnp.arange(FOX_BLOCK)
        s = jnp.einsum('bqhd,bkhd->bhqk', qi, k).astype(jnp.float32) * scale
        s = s + ci[..., None] - c_keys[:, :, None, :]
        s = jnp.where(k_pos[None, :] <= q_pos[:, None], s, -jnp.inf)
        p = jax.nn.softmax(s, axis=-1).astype(v.dtype)
        return jnp.einsum('bhqk,bkhd->bqhd', p, v)

    o = lax.map(block, (q_blocks, c_blocks, jnp.arange(nb)))
    return o.transpose(1, 0, 2, 3, 4).reshape(B, L, H * hd)

def fox_sample(k_past, v_past, logf_past, q, k, v, logf):
    B, L, H, hd = q.shape
    P = k_past.shape[1]
    scale = hd ** -0.5
    lp = logf_past.astype(jnp.float32)
    suffix = lax.cumsum(lp, axis=1, reverse=True) - lp
    c_new = jnp.cumsum(logf, axis=1).transpose(0, 2, 1)
    s_past = jnp.einsum('bqhd,bkhd->bhqk', q, k_past).astype(jnp.float32) * scale
    s_past = s_past + suffix.transpose(0, 2, 1)[:, :, None, :] + c_new[..., None]
    s_new = jnp.einsum('bqhd,bkhd->bhqk', q, k).astype(jnp.float32) * scale
    s_new = s_new + c_new[..., None] - c_new[:, :, None, :]
    causal = jnp.tril(jnp.ones((L, L), dtype=bool))
    s_new = jnp.where(causal, s_new, -jnp.inf)
    p = jax.nn.softmax(jnp.concatenate([s_past, s_new], axis=-1), axis=-1).astype(v.dtype)
    o = jnp.einsum('bhqk,bkhd->bqhd', p[..., :P], v_past) + jnp.einsum('bhqk,bkhd->bqhd', p[..., P:], v)
    return o.reshape(B, L, H * hd)

def s5_mixer(u, lam_re, lam_im, log_dt, b_re, b_im, c_re, c_im, d, w_glu, b_glu, h0_re, h0_im):
    B, L, _ = u.shape
    f32 = jnp.float32
    uf = u.astype(f32).reshape(B, L, S5_G, S5_GROUP)
    dt = jnp.exp(log_dt.astype(f32))[:, None]
    lr, li = lam_re.astype(f32), lam_im.astype(f32)
    mag = jnp.exp(lr * dt)
    ab_re, ab_im = mag * jnp.cos(li * dt), mag * jnp.sin(li * dt)
    den = lr * lr + li * li
    nr, ni = ab_re - 1.0, ab_im
    coef_re = (nr * lr + ni * li) / den
    coef_im = (ni * lr - nr * li) / den
    br, bi = b_re.astype(f32), b_im.astype(f32)
    bb_re = coef_re[..., None] * br - coef_im[..., None] * bi
    bb_im = coef_re[..., None] * bi + coef_im[..., None] * br
    bu_re = jnp.einsum('gph,blgh->blgp', bb_re, uf)
    bu_im = jnp.einsum('gph,blgh->blgp', bb_im, uf)
    a_re = jnp.broadcast_to(ab_re, bu_re.shape)
    a_im = jnp.broadcast_to(ab_im, bu_im.shape)

    def combine(e1, e2):
        a1r, a1i, b1r, b1i = e1
        a2r, a2i, b2r, b2i = e2
        return (a2r * a1r - a2i * a1i, a2r * a1i + a2i * a1r,
                a2r * b1r - a2i * b1i + b2r, a2r * b1i + a2i * b1r + b2i)

    pr, pi_, hr, hi = lax.associative_scan(combine, (a_re, a_im, bu_re, bu_im), axis=1)
    h0r = h0_re.astype(f32)[:, None]
    h0i = h0_im.astype(f32)[:, None]
    hr = hr + pr * h0r - pi_ * h0i
    hi = hi + pr * h0i + pi_ * h0r
    y = jnp.einsum('ghp,blgp->blgh', c_re.astype(f32), hr) - jnp.einsum('ghp,blgp->blgh', c_im.astype(f32), hi)
    y = y.reshape(B, L, -1) + d.astype(f32) * uf.reshape(B, L, -1)
    g = jax.nn.gelu(y)
    out = g * jax.nn.sigmoid(g @ w_glu.astype(f32) + b_glu.astype(f32))
    return out.astype(u.dtype), hr[:, -1], hi[:, -1]

def hgrn2_mixer(q, f_logit, i_in, g, lb, norm_g, s0):
    B, L, H, dk = q.shape
    dv = i_in.shape[-1]
    f32 = jnp.float32
    lbr = lb.astype(f32).reshape(H, dk)
    log_f = jnp.logaddexp(jnp.log(lbr), jnp.log1p(-lbr) + jax.nn.log_sigmoid(f_logit.astype(f32)))
    c = min(HG_CHUNK, L)
    pad = (-L) % c
    n = (L + pad) // c

    def prep(t):
        t = jnp.pad(t, ((0, 0), (0, pad), (0, 0), (0, 0)))
        return t.reshape(B, n, c, H, -1).transpose(1, 0, 3, 2, 4)

    qc, lfc, vc = prep(q.astype(f32)), prep(log_f), prep(i_in.astype(f32))
    mask = jnp.tril(jnp.ones((c, c), dtype=bool))

    def step(S, args):
        qt, lft, vt = args
        kt = -jnp.expm1(lft)
        bc = jnp.cumsum(lft, axis=2)
        diff = bc[:, :, :, None, :] - bc[:, :, None, :, :]
        decay = jnp.exp(jnp.where(mask[:, :, None], diff, -jnp.inf))
        att = jnp.einsum('bhtd,bhtsd,bhsd->bhts', qt, decay, kt)
        o = att @ vt + jnp.einsum('bhtd,bhdv->bhtv', qt * jnp.exp(bc), S)
        bl = bc[:, :, -1]
        S = jnp.exp(bl)[..., None] * S + jnp.einsum('bhsd,bhsv->bhdv', kt * jnp.exp(bl[:, :, None, :] - bc), vt)
        return S, o

    S, o = lax.scan(step, s0.astype(f32), (qc, lfc, vc))
    o = o.transpose(1, 0, 3, 2, 4).reshape(B, n * c, H, dv)[:, :L]
    o = o * lax.rsqrt(jnp.mean(o * o, axis=-1, keepdims=True) + RMS_EPS) * norm_g.astype(f32).reshape(H, dv)
    o = o.reshape(B, L, H * dv) * jax.nn.silu(g.astype(f32))
    return o.astype(q.dtype), S

def gmlp_mixer(u, v, ln_g, ln_b, w_s, b_s):
    B, L, W = u.shape
    vn = layer_norm(v, ln_g, ln_b)
    pad = (-L) % GM_CHUNK
    n = (L + pad) // GM_CHUNK
    vp = jnp.pad(vn, ((0, 0), (0, pad), (0, 0))).reshape(B, n, GM_CHUNK, GM_GROUPS, GM_GW)
    ws = w_s * jnp.tril(jnp.ones((GM_CHUNK, GM_CHUNK), dtype=w_s.dtype))
    mixed = jnp.einsum('gts,bnsgc->bntgc', ws, vp) + b_s.T[None, None, :, :, None]
    mixed = mixed.reshape(B, n * GM_CHUNK, W)[:, :L]
    return u * mixed, vn

def trunk_layer(x, l, W, fox_fn, s5_h0_re, s5_h0_im, hg_s0):
    B, L, _ = x.shape
    z = x @ W['w_in'][l]
    fq, fk, fv, ff, su, hq, hf, hi, hg, gu, gv, gt = split_cols(z)
    fq = fq.reshape(B, L, FOX_H, FOX_HD)
    fk = fk.reshape(B, L, FOX_H, FOX_HD)
    fv = fv.reshape(B, L, FOX_H, FOX_HD)
    logf = jax.nn.log_sigmoid(ff.astype(jnp.float32) + W['fox_bf'][l].astype(jnp.float32))
    o_a = fox_fn(fq, fk, fv, logf)
    o_b, s5_re, s5_im = s5_mixer(su, W['s5_lambda_re'][l], W['s5_lambda_im'][l], W['s5_log_dt'][l],
                                 W['s5_b_re'][l], W['s5_b_im'][l], W['s5_c_re'][l], W['s5_c_im'][l],
                                 W['s5_d'][l], W['s5_w_glu'][l], W['s5_b_glu'][l], s5_h0_re, s5_h0_im)
    lb_all = jnp.cumsum(jax.nn.softmax(W['hgrn_lb'].astype(jnp.float32), axis=0), axis=0)
    lb = lb_all[l] - lb_all[0]
    o_c, hg_state = hgrn2_mixer(hq.reshape(B, L, HG_H, HG_DK), hf.reshape(B, L, HG_H, HG_DK),
                                hi.reshape(B, L, HG_H, HG_DV), hg, lb, W['hgrn_norm_g'][l], hg_s0)
    o_d, v_rows = gmlp_mixer(jax.nn.gelu(gu), jax.nn.gelu(gv), W['gmlp_ln_g'][l], W['gmlp_ln_b'][l],
                             W['gmlp_w_s'][l], W['gmlp_b_s'][l])
    branches = jnp.stack([o_a, o_b, o_c, o_d], axis=2)
    proj = jnp.einsum('blkc,kcd->blkd', branches, W['w_branch'][l])
    gates = jax.nn.sigmoid(gt.reshape(B, L, N_BRANCH, D_MODEL))
    merged = jnp.einsum('blkd,blkd->bld', gates, proj)
    x = layer_norm(DEEPNORM_ALPHA * x + merged @ W['w_out'][l], W['ln1_g'][l], W['ln1_b'][l])
    gate_ff, up_ff = jnp.split(x @ W['w_ffn_up'][l], 2, axis=-1)
    x = layer_norm(DEEPNORM_ALPHA * x + (jax.nn.silu(gate_ff) * up_ff) @ W['w_ffn_down'][l], W['ln2_g'][l], W['ln2_b'][l])
    return x, (fk, fv, logf, s5_re, s5_im, hg_state, v_rows)

def setup_inputs(seed: int = 0) -> dict:
    key = jax.random.key(seed)
    ks = iter(jax.random.split(key, 48))
    f32 = jnp.float32
    nrm = lambda shape, s=1.0: jax.random.normal(next(ks), shape, f32) * s
    n_pages = PAST_LEN // PAGE_SIZE
    n_phys = (DEC_BATCH * n_pages * 5) // 4
    perm = jax.random.permutation(next(ks), n_phys)
    page_table = perm[:DEC_BATCH * n_pages].reshape(DEC_BATCH, n_pages).astype(jnp.int32)
    inp = {}
    inp['x_prompt'] = nrm((BATCH, SEQ, D_MODEL))
    inp['x_sample'] = nrm((DEC_BATCH, DEC_SEQ, D_MODEL))
    inp['cache_k'] = nrm((DEPTH, n_phys, PAGE_SIZE, FOX_H, FOX_HD))
    inp['cache_v'] = nrm((DEPTH, n_phys, PAGE_SIZE, FOX_H, FOX_HD))
    inp['cache_logf'] = jax.nn.log_sigmoid(nrm((DEPTH, n_phys, PAGE_SIZE, FOX_H), 0.5) + 6.0)
    inp['page_table'] = page_table
    inp['state_s5_re'] = nrm((DEPTH, DEC_BATCH, S5_G, S5_P), 0.5)
    inp['state_s5_im'] = nrm((DEPTH, DEC_BATCH, S5_G, S5_P), 0.5)
    inp['state_hgrn'] = nrm((DEPTH, DEC_BATCH, HG_H, HG_DK, HG_DV), 0.5)
    inp['w_in'] = nrm((DEPTH, D_MODEL, N_IN), D_MODEL ** -0.5)
    inp['fox_bf'] = FOX_BF_INIT + nrm((DEPTH, FOX_H), 0.1)
    inp['s5_lambda_re'] = -0.5 + nrm((DEPTH, S5_G, S5_P), 0.01)
    inp['s5_lambda_im'] = jnp.pi * jnp.arange(S5_P, dtype=f32) + nrm((DEPTH, S5_G, S5_P), 0.01)
    inp['s5_log_dt'] = jax.random.uniform(next(ks), (DEPTH, S5_G), f32, math.log(1e-3), math.log(1e-1))
    inp['s5_b_re'] = nrm((DEPTH, S5_G, S5_P, S5_GROUP), (2 * S5_GROUP) ** -0.5)
    inp['s5_b_im'] = nrm((DEPTH, S5_G, S5_P, S5_GROUP), (2 * S5_GROUP) ** -0.5)
    inp['s5_c_re'] = nrm((DEPTH, S5_G, S5_GROUP, S5_P), S5_P ** -0.5)
    inp['s5_c_im'] = nrm((DEPTH, S5_G, S5_GROUP, S5_P), S5_P ** -0.5)
    inp['s5_d'] = nrm((DEPTH, MIX_W))
    inp['s5_w_glu'] = nrm((DEPTH, MIX_W, MIX_W), MIX_W ** -0.5)
    inp['s5_b_glu'] = nrm((DEPTH, MIX_W), 0.01)
    inp['hgrn_lb'] = nrm((DEPTH, HG_H * HG_DK))
    inp['hgrn_norm_g'] = 1.0 + nrm((DEPTH, HG_H * HG_DV), 0.1)
    inp['gmlp_ln_g'] = 1.0 + nrm((DEPTH, MIX_W), 0.1)
    inp['gmlp_ln_b'] = nrm((DEPTH, MIX_W), 0.01)
    inp['gmlp_w_s'] = nrm((DEPTH, GM_GROUPS, GM_CHUNK, GM_CHUNK), GM_CHUNK ** -0.5)
    inp['gmlp_b_s'] = 1.0 + nrm((DEPTH, GM_GROUPS, GM_CHUNK), 0.1)
    inp['w_branch'] = nrm((DEPTH, N_BRANCH, MIX_W, D_MODEL), MIX_W ** -0.5)
    inp['w_out'] = nrm((DEPTH, D_MODEL, D_MODEL), D_MODEL ** -0.5 * DEEPNORM_BETA)
    inp['ln1_g'] = 1.0 + nrm((DEPTH, D_MODEL), 0.1)
    inp['ln1_b'] = nrm((DEPTH, D_MODEL), 0.01)
    inp['w_ffn_up'] = nrm((DEPTH, D_MODEL, 2 * D_FF), D_MODEL ** -0.5)
    inp['w_ffn_down'] = nrm((DEPTH, D_FF, D_MODEL), D_FF ** -0.5 * DEEPNORM_BETA)
    inp['ln2_g'] = 1.0 + nrm((DEPTH, D_MODEL), 0.1)
    inp['ln2_b'] = nrm((DEPTH, D_MODEL), 0.01)
    return inp

def reference(x_prompt, x_sample, cache_k, cache_v, cache_logf, page_table, state_s5_re, state_s5_im, state_hgrn,
              w_in, fox_bf, s5_lambda_re, s5_lambda_im, s5_log_dt, s5_b_re, s5_b_im, s5_c_re, s5_c_im, s5_d,
              s5_w_glu, s5_b_glu, hgrn_lb, hgrn_norm_g, gmlp_ln_g, gmlp_ln_b, gmlp_w_s, gmlp_b_s, w_branch, w_out,
              ln1_g, ln1_b, w_ffn_up, w_ffn_down, ln2_g, ln2_b):
    W = {'w_in': w_in, 'fox_bf': fox_bf, 's5_lambda_re': s5_lambda_re, 's5_lambda_im': s5_lambda_im,
         's5_log_dt': s5_log_dt, 's5_b_re': s5_b_re, 's5_b_im': s5_b_im, 's5_c_re': s5_c_re, 's5_c_im': s5_c_im,
         's5_d': s5_d, 's5_w_glu': s5_w_glu, 's5_b_glu': s5_b_glu, 'hgrn_lb': hgrn_lb, 'hgrn_norm_g': hgrn_norm_g,
         'gmlp_ln_g': gmlp_ln_g, 'gmlp_ln_b': gmlp_ln_b, 'gmlp_w_s': gmlp_w_s, 'gmlp_b_s': gmlp_b_s,
         'w_branch': w_branch, 'w_out': w_out, 'ln1_g': ln1_g, 'ln1_b': ln1_b, 'w_ffn_up': w_ffn_up,
         'w_ffn_down': w_ffn_down, 'ln2_g': ln2_g, 'ln2_b': ln2_b}
    b_p = x_prompt.shape[0]
    b_s = x_sample.shape[0]
    n_past = page_table.shape[1] * cache_k.shape[2]
    s5_zero = jnp.zeros((b_p, S5_G, S5_P), jnp.float32)
    hg_zero = jnp.zeros((b_p, HG_H, HG_DK, HG_DV), jnp.float32)
    y_prompt, y_sample = x_prompt, x_sample
    p_states, s_states = [], []
    for l in range(DEPTH):
        y_prompt, sp = trunk_layer(y_prompt, l, W, fox_prompt, s5_zero, s5_zero, hg_zero)
        k_past = cache_k[l][page_table].reshape(b_s, n_past, FOX_H, FOX_HD)
        v_past = cache_v[l][page_table].reshape(b_s, n_past, FOX_H, FOX_HD)
        lf_past = cache_logf[l][page_table].reshape(b_s, n_past, FOX_H)
        y_sample, ss = trunk_layer(y_sample, l, W, functools.partial(fox_sample, k_past, v_past, lf_past),
                                   state_s5_re[l], state_s5_im[l], state_hgrn[l])
        p_states.append(sp)
        s_states.append(ss)
    fox_k_prompt = jnp.stack([s[0] for s in p_states])
    fox_v_prompt = jnp.stack([s[1] for s in p_states])
    fox_logf_prompt = jnp.stack([s[2] for s in p_states])
    fox_k_sample = jnp.stack([s[0] for s in s_states])
    fox_v_sample = jnp.stack([s[1] for s in s_states])
    fox_logf_sample = jnp.stack([s[2] for s in s_states])
    s5_re_prompt = jnp.stack([s[3] for s in p_states])
    s5_im_prompt = jnp.stack([s[4] for s in p_states])
    s5_re_sample = jnp.stack([s[3] for s in s_states])
    s5_im_sample = jnp.stack([s[4] for s in s_states])
    hgrn_prompt = jnp.stack([s[5] for s in p_states])
    hgrn_sample = jnp.stack([s[5] for s in s_states])
    gmlp_v_sample = jnp.stack([s[6] for s in s_states])
    return (y_prompt, y_sample, fox_k_prompt, fox_v_prompt, fox_logf_prompt, fox_k_sample, fox_v_sample, fox_logf_sample, s5_re_prompt, s5_im_prompt, s5_re_sample, s5_im_sample, hgrn_prompt, hgrn_sample, gmlp_v_sample)


_drawn_inputs = setup_inputs


def setup_inputs(seed=0):
    import zlib

    import numpy as np

    out = dict(_drawn_inputs(seed))
    spreads = {}
    factors = {'cache_k': 4.158,
     'cache_v': 3.267,
     'cache_logf': 31.855,
     's5_lambda_re': 16.145,
     's5_b_glu': 64.0,
     'hgrn_norm_g': 3.127,
     'gmlp_ln_b': 5.773,
     'gmlp_b_s': 3.309,
     'ln1_b': 5.34,
     'ln2_b': 5.753}
    for name, (base, spread) in spreads.items():
        noise = np.random.default_rng([zlib.crc32(name.encode()), seed]).standard_normal(out[name].shape)
        drawn = base * np.exp(spread * noise) if base else spread * noise
        out[name] = __import__('jax').numpy.asarray(drawn.astype(out[name].dtype))
    for name, factor in factors.items():
        out[name] = (out[name] * factor).astype(out[name].dtype)
    return out
```

```python
import math
from contextlib import ExitStack

import concourse.bass as bass
from concourse import mybir
from concourse.alu_op_type import AluOpType as ALU

F32, F32R, I32 = mybir.dt.float32, mybir.dt.float32r, mybir.dt.int32
ACT = mybir.ActivationFunctionType
AX = mybir.AxisListType
ds = bass.ds

P = 128
D_MODEL, SEQ, DEC, MIX, HEADS = 2048, 256, 8, 512, 4
PAST, PAGE = 1024, 128
N_PAGES = PAST // PAGE
D_FF = 5632
TOK = SEQ + DEC
KT = D_MODEL // P
MT = MIX // P
ALPHA = 2.0 ** 0.25
LN_EPS, RMS_EPS = 1e-5, 1e-6
SCALE = P ** -0.5
S5_TILES = 16
ROUND = 12582912.0
PI_ = 3.1415925
NEG = -1.0e30
COLS = 256
RING = 4
CK = 4

FQ, FK, FV, FF = 0, 512, 1024, 1536
SU = FF + HEADS
HQ, HF, HI, HG, GU, GV, GT = (SU + 512 * (n + 1) for n in range(7))

MIXER_COLS = []
for _start in (SU, HF, HI, HQ, FQ, HG, FK, FV):
    MIXER_COLS += [(_start, COLS), (_start + COLS, COLS)]
MIXER_COLS.append((FF, P))
for _start in (GV, GU):
    MIXER_COLS += [(_start, COLS), (_start + COLS, COLS)]

PASSES_A = len(MIXER_COLS)
C_GATE = [PASSES_A * 4]
C_GLU = C_GATE[0] + 32
C_GATE.append(C_GLU + 2)
C_MERGE = [C_GATE[1] + 32, C_GATE[1] + 40]
C_GATE.append(C_MERGE[1] + 8)
C_MERGE.append(C_GATE[2] + 32)
C_GATE.append(C_MERGE[2] + 8)
C_MERGE.append(C_GATE[3] + 32)
C_OUT = C_MERGE[3] + 8
C_UP = C_OUT + 32
UP_STEPS = D_FF // COLS
C_DOWN = C_UP + UP_STEPS * 8
DOWN_CHUNKS = D_FF // P // CK
C_END = C_DOWN + 8 * DOWN_CHUNKS

P_GATE = [PASSES_A]
P_GLU = P_GATE[0] + 8
P_GATE.append(P_GLU + 2)
P_MERGE = [P_GATE[1] + 8, P_GATE[1] + 16]
P_GATE.append(P_MERGE[1] + 8)
P_MERGE.append(P_GATE[2] + 8)
P_GATE.append(P_MERGE[2] + 8)
P_MERGE.append(P_GATE[3] + 8)
P_OUT = P_MERGE[3] + 8
P_UP = P_OUT + 8
P_DOWN = P_UP + 2 * UP_STEPS
C_STATES, C_STATES_OUT, C_STATE_OUT = 19, 43, 87
CACHE_AT = [46, 46] + [52 + 2 * n for n in range(16)] + [110, 112, 115, 118, 122, 125, 129, 132, 136, 138, 140, 142, 144, 146]
C_POOL_END = C_MERGE[0]

MERGE_ORDER = (1, 2, 3, 0)
S5_AT, S5_GAP = 12, 4
H_AT, H_GAP = 48, 4
HGRN_LEVELS = (64, 32, 16, 8, 4, 2, 1)
NL = len(HGRN_LEVELS)

PRODUCTS = [("x", n, (4 + n % 4,)) for n in range(KT)]
PRODUCTS += [("vecs", 0, (6,)), ("s5_h0", 0, (5,)), ("s5_lam", 0, (4,)), ("s5_ct", 0, (7,)), ("s5_ct", 1, (5,)),
             ("g_ws", 0, (6,)), ("s5_bt", 0, (4,)), ("s5_bt", 1, (5,)), ("s5_bus", 0, (4, 5, 6, 7))]


H_SMP = 5


def _s5_products():
    out = []
    for b in range(8):
        out.append(("s5_bu", b, (4, 5)))
        if b == H_SMP + 1:
            out.append(("h_os", 0, (7,)))
        if b:
            out.append(("s5_y", b - 1, (6 + (b - 1) // 2 % 2,)))
        if b == H_SMP:
            out += [("h_vs", 0, (4,))] + [("h_vb", n, (4 + n % 2,)) for n in range(8)]
    return out + [("s5_y", 7, (7,))]


PRODUCTS += _s5_products()
PRODUCTS += [("s5_out", 0, (4,))] + [("s5_outs", n, (5 + n % 2,)) for n in range(8)]
PRODUCTS += [("h_ost", 0, (7,))] + [("h_v", c, (4 + c,)) for c in range(2)] + [("f_tok", 0, (7,))]
for _n in range(NL + 1):
    PRODUCTS += [("f_qb", _n, (6 + _n % 2,)), ("h_att", _n, (4, 5))]
PRODUCTS += [("h_kd", 0, (4, 5)), ("h_s", 0, (6,)), ("h_o", 0, (4, 5)), ("h_last", 0, (7,))]
PRODUCTS += [("h_ms", 0, (4, 5, 6, 7))]
PRODUCTS += [("g_mu", 0, (4,)), ("g_var", 0, (5,))] + [("g_tok", c, (6 + c % 2,)) for c in range(3)]
PRODUCTS += [("g_mix", n, (4 + n,)) for n in range(2)] + [("g_ms", 0, (6,))]
PRODUCTS += [("f_lf", 0, (6,)), ("f_suf", 0, (7,))]
PRODUCTS += [("f_suft", 0, (6,)), ("f_new", 0, (5,)), ("f_sct", 0, (6, 7)), ("f_pt", 0, (4,)), ("f_pn", 0, (5,))]
PRODUCTS += [("f_tok", n, (4 + n % 2,)) for n in range(1, 7)]
PRODUCTS += [("f_s", 0, (4, 5)), ("f_p", 0, (7,)), ("f_o", 0, (4,)), ("f_s", 1, (4, 5)), ("f_p", 1, (7, 4)),
             ("f_o", 1, (5,)), ("f_os", 0, (6,)), ("f_ost", 0, (7,))]
PRODUCTS += [("l_mu", 0, (4,)), ("l_var", 0, (5,)), ("l_mu", 1, (6,)), ("l_var", 1, (7,))]
PRODUCTS += [("y", n, (4 + n % 4,)) for n in range(12)]


def said(text):
    out = []
    for word in text.split():
        word, _, times = word.partition("*")
        name, _, by = word.partition(":")
        out += [(name, int(by or 1))] * int(times or 1)
    return out


TOLD = {
    "act": said("""
        a_dt vecs_lnv empty_vecs vecs_ready a_mag a_sin empty_s5_h0 h0_ready empty_s5_lam lam_ready
        empty_s5_ct*2 empty_g_ws a_table empty_s5_bt*2 s5_bt_ready s5_staged a_table empty_s5_bus bus_ready
        a_table*4 a_smp empty_h_vs h_vs_tok a_table*2 empty_h_os h_os_tok gh_done empty_s5_out
        empty_s5_outs*8 a_ln empty_h_ost empty_h_v*2 empty_f_tok f_qtok a_decay*9 empty_h_kd h_kdt empty_h_s
        h_s0 empty_h_o h_sq h_rstd bh2_done g_sq g_rstd empty_g_tok*3 g_tokens bh3_done a_lf empty_f_lf
        empty_f_sct f_exp empty_f_pt f_ptt empty_f_tok*5 f_vtok empty_f_tok f_pexp empty_f_p f_pt_sb f_pexp
        empty_f_p f_pt_sb gh_done empty_f_os f_ostok bh0_done empty_y y_copied empty_y y_copied empty_y
        y_copied empty_y y_copied empty_y y_copied empty_y y_copied empty_y y_copied empty_y y_copied
        empty_y y_copied empty_y y_copied empty_y y_copied empty_y y_copied"""),
    "dve": said("""
        empty_x*16 d_lrdt d_turns s5_par s5_cd s5_bd d_angle*2 s5_hs empty_s5_bu s5_h d_angle empty_s5_bu
        s5_h d_angle empty_s5_y:2 empty_s5_bu s5_h d_angle empty_s5_bu s5_h d_angle empty_s5_y:2 empty_s5_bu
        s5_h d_angle empty_s5_bu s5_h d_angle empty_h_vb*8 h_smp_done:2 empty_s5_y:2 empty_s5_bu s5_h
        empty_s5_bu s5_h s5_sf empty_s5_y:2 s5_yd g_split d_lf d_dif*2 h_qe d_dif kv_free empty_h_att
        empty_f_qb kv_free h_qe d_dif kv_free empty_h_att empty_f_qb kv_free h_qe d_dif kv_free empty_h_att
        empty_f_qb kv_free h_qe d_dif kv_free empty_h_att empty_f_qb kv_free h_qe d_dif kv_free empty_h_att
        empty_f_qb kv_free h_qe d_dif kv_free empty_h_att empty_f_qb kv_free h_qe d_dif kv_free empty_h_att
        empty_f_qb kv_free empty_h_att h_att_done h_kd kv_free empty_f_qb kv_free empty_h_last empty_h_ms
        h_var h_out branch2 h_done:2 empty_g_mu g_cent empty_g_var g_rec g_vn empty_g_mix*2 empty_g_ms
        g_mixed branch3 g_done f_lf f_rc empty_f_suf f_suf_in f_qk empty_f_suft f_sc empty_f_new f_max
        f_prob f_tok_free empty_f_pn f_cum kv_free*2 f_vsum empty_f_s f_pmax kv_free f_prompt kv_free f_vsum
        empty_f_o kv_free*2 f_vsum empty_f_s f_pmax kv_free f_prompt kv_free f_vsum empty_f_o glu_done
        kv_free*2 f_vsum kv_free*2 f_vsum kv_free*2 f_vsum*2 branch1 empty_f_ost f_out branch0 sums*2
        merged*2 sums merged sums merged pre0 empty_l_mu centred0*4 empty_l_var var0 x1_f32*4 pre1
        empty_l_mu centred1*4 empty_l_var var1 y_ready*4"""),
    "pool": said("""
        ident_ready consts_ready"""),
}


def before(name, index):
    at = [p[:2] for p in PRODUCTS].index((name, index))
    out = []
    for bank in PRODUCTS[at][2]:
        for n in range(at - 1, -1, -1):
            if bank in PRODUCTS[n][2]:
                if PRODUCTS[n][:2] not in out:
                    out.append(PRODUCTS[n][:2])
                break
    return out


def banks(name, index):
    return [p[2] for p in PRODUCTS if p[:2] == (name, index)][0]


class Steps:

    def __init__(self, engine, sem, tell=None):
        self.engine, self.sem, self.n, self.tell_ = engine, sem, 0, tell

    def do(self, instruction):
        self.n += 1
        instruction.then_inc(self.sem, 1)

    def settle(self):
        self.engine.wait_ge(self.sem, self.n)

    def then(self, instruction):
        self.do(instruction)
        self.settle()

    def tell(self, name):
        self.settle()
        self.tell_(self.engine, name)


def trunk(nc, A, O):
    ctx = ExitStack()
    sems = {}

    def sem(name):
        if name not in sems:
            sems[name] = ctx.enter_context(nc.semaphore(name))
        return sems[name]

    def made(name, count):
        return sem("made"), [p[:2] for p in PRODUCTS].index((name, count - 1)) + 1

    said = {}

    def tell(engine, name, by=1):
        who = "act" if engine is nc.scalar else "dve" if engine is nc.vector else "pool"
        said.setdefault(who, []).append((name, by))
        assert TOLD[who][len(said[who]) - 1] == (name, by), (who, len(said[who]), name)
        engine.sem_inc(sem(who + "_told"), 1)

    def told(name, count):
        for who, names in TOLD.items():
            total = 0
            for n, (other, by) in enumerate(names):
                if other == name:
                    total += by
                    if total >= count:
                        return sem(who + "_told"), n + 1
            assert not total, (name, count)
        return sem(name), count

    base = (nc.sbuf_base + 31) // 32 * 32
    ZB = MT * TOK * 4
    XB = KT * TOK * 4
    CB = CK * COLS * 4
    at_raw, at_hi, at_lo = 0, RING * CB, 2 * RING * CB
    at_xh = 3 * RING * CB
    at_xl = at_xh + XB
    at_g = at_xl + XB
    at_z = at_g + 2 * XB
    at_kv = at_z + 13 * ZB
    at_fix = at_kv + 2 * 4 * MIX * 4

    def place(name, shape, dt, off):
        return nc.alloc_sbuf_tensor_at(name, shape, dt, offset=base + off)

    raw = place("w_raw", [P, RING, CK, COLS], F32, at_raw)
    w_hi = place("w_hi", [P, RING, CK, COLS], F32R, at_hi)
    w_lo = place("w_lo", [P, RING, CK, COLS], F32R, at_lo)
    xh = place("xh", [P, KT, TOK], F32R, at_xh)
    xl = place("xl", [P, KT, TOK], F32R, at_xl)
    gates = place("gates", [P, 32, TOK], F32, at_g)

    zslot = {}

    def z(name, slot, dt=F32):
        zslot[name] = place(name, [P, MT, TOK], dt, at_z + slot * ZB)
        return zslot[name]

    gh1, gl1 = z("gh1", 0, F32R), z("gl1", 1, F32R)
    hq, hi_ = z("hq", 2), z("hi", 3)
    bh2, bl2 = z("bh2", 2, F32R), z("bl2", 3, F32R)
    fk, fv = z("fk", 4), z("fv", 5)
    bh0, bl0 = z("bh0", 4, F32R), z("bl0", 5, F32R)
    gv, kt_ = z("gv", 6), z("kt", 7)
    bh3, bl3 = z("bh3", 6, F32R), z("bl3", 7, F32R)
    su, hf, fq, gu, hg = (z(n, 8 + i) for i, n in enumerate(("su", "hf", "fq", "gu", "hg")))
    bh, bl = [bh0, gh1, bh2, bh3], [bl0, gl1, bl2, bl3]
    mh = place("mh", [P, KT, TOK], F32R, at_z + 8 * ZB)
    ml = place("ml", [P, KT, TOK], F32R, at_z + 12 * ZB)
    kv = place("kv", [P, 2, 4, MIX], F32, at_kv)

    at_keep = (nc.sbuf_usable_end - base) // 32 * 32 - 2 * P * 4 - 4 * KT * 4
    ident = place("ident", [P, P], F32, at_keep)
    ones = place("ones", [P, P], F32, at_keep + P * 4)
    lnv = place("lnv", [P, 4, KT], F32, at_keep + 2 * P * 4)

    off = [at_fix]

    def fix(name, shape, dt=F32):
        n = 4
        for s in shape[1:]:
            n *= s
        t = place(name, shape, dt, off[0])
        off[0] += (n + 31) // 32 * 32
        assert off[0] <= at_keep
        return t

    level_mask = fix("level_mask", [P, NL + 1, P], I32)
    causal = fix("causal", [P, P])
    ws_t = fix("ws_t", [P, MT, P])
    lam_t = fix("lam_t", [P, 6, S5_TILES])
    h0 = fix("h0", [P, 2, S5_TILES, DEC])
    v_tok = fix("v_tok", [P, 2, MIX])
    t8 = fix("t8", [DEC, 2, MIX])
    sc = fix("sc", [P, N_PAGES, 32])
    small = fix("small", [P, 64])
    vecs = fix("vecs", [P, 5, MT])
    bs_row = fix("bs_row", [1, MT, P])
    ws00 = fix("ws00", [1, MT])
    lf_t = fix("lf_t", [HEADS, TOK])
    q8 = place("q8", [DEC, MIX], F32, off[0])
    cum = fix("cum", [HEADS, 2, SEQ])
    bf = fix("bf", [HEADS, 1])
    eye8 = fix("eye8", [P, DEC, DEC])
    hos = place("hos", [P, 32], F32, at_g + 33280)
    pt = fix("pt", [1, DEC * N_PAGES], I32)
    pt_col = fix("pt_col", [DEC * N_PAGES, 1], I32)
    par = place("par", [P, 4], F32, at_g + 33536)
    sf = place("sf", [P, 2, S5_TILES], F32, at_g + 33408)
    osmp = place("osmp", [P, 32], F32, at_fix + 1280)

    x_nat = place("x_nat", [P, 2, D_MODEL], F32, at_g)
    xs_nat = place("xs_nat", [DEC, D_MODEL], F32, at_g + 2 * D_MODEL * 4)
    h0_nat = place("h0_nat", [DEC, 2, D_MODEL], F32, at_z + 9 * ZB)
    bn = place("bn", [P, 2, S5_TILES, 16], F32, at_kv)
    cn = place("cn", [P, 2, MT, 64], F32, at_kv + 2048)
    bd = place("bd", [P, 2, S5_TILES, 2, 16], F32, at_kv + 4096)
    cd = place("cd", [P, 2, MT, 2, 64], F32, at_kv + 8192)
    sp = place("sp", [S5_TILES, 16, P], F32, at_z + 0 * ZB)
    dt2 = place("dt2", [S5_TILES, 2], F32, at_z + 1 * ZB + 4096)
    ws_nat = place("ws_nat", [P, MT, P], F32, at_kv + 12288)
    vec_nat = place("vec_nat", [4 * KT + 5 * MT, P], F32, at_kv + 14336)
    g0 = at_g
    bt = place("bt", [P, 2, MT, P], F32, g0)
    ct = place("ct", [P, 2, MT, P], F32, g0 + 4096)
    er = place("er", [P, 2, 2, SEQ], F32, g0 + 8192)
    ei = place("ei", [P, 2, 2, SEQ], F32, g0 + 12288)
    tab = place("tab", [P, 2, SEQ], F32, g0 + 16384)
    rnd = place("rnd", [P, 2, SEQ], F32, g0 + 18432)
    gr = place("gr", [P, 2, SEQ], F32, g0 + 20480)
    gi = place("gi", [P, 2, SEQ], F32, g0 + 22528)
    hr = place("hr", [P, 2, SEQ], F32, g0 + 24576)
    hm = place("hm", [P, 2, SEQ], F32, g0 + 26624)
    bus = place("bus", [P, 2, S5_TILES, DEC], F32, g0 + 28672)
    hs = place("hs", [P, 2, S5_TILES, DEC], F32, g0 + 29696)
    iota_t = place("iota_t", [P, SEQ], F32, g0 + 30720)
    qm = place("qm", [P, HEADS, DEC, DEC], F32, g0 + 31744)
    bc = place("bc", [P, 8, P], F32, g0)
    att = place("att", [P, 8, P], F32, g0 + 4096)
    s_prev = place("s_prev", [P, 2, HEADS, P], F32, g0 + 8192)
    qb_h = place("qb_h", [P, HEADS, P], F32, g0 + 12288)
    dif = place("dif", [P, 2, 8, P], F32, g0 + 16896)
    qe = place("qe", [P, 8, P], F32, g0 + 25088)
    ke = place("ke", [P, 8, P], F32, g0 + 29184)
    s_smp = place("s_smp", [P, 32, P], F32, at_kv)
    k_tok = place("k_tok", [P, 2, MIX], F32, at_z + 12 * ZB)
    lfp = place("lfp", [DEC * N_PAGES, PAGE, HEADS], F32, at_z + 9 * ZB)
    rc = place("rc", [DEC * N_PAGES, PAGE, HEADS], F32, at_z + 9 * ZB + 2048)
    tri = place("tri", [64, 64], F32, at_fix)
    ptt = place("ptt", [P, N_PAGES, 32], F32, at_fix + 256)
    ps_row = place("ps_row", [32, PAST], F32, g0 + 24 * TOK * 4)
    s_sb = place("s_sb", [P, HEADS, SEQ], F32, g0 + 24 * TOK * 4)
    pt_sb = place("pt_sb", [P, 2, HEADS, P], F32, g0 + 28 * TOK * 4)
    lnt = place("lnt", [P, MT, TOK], F32, g0 + 16896)
    gsq, sgl = z("gsq", 12), z("sgl", 12)
    vacc = place("vacc", [P, 2, MIX], F32, at_z + 11 * ZB)
    xp = place("xp", [P, KT, TOK], F32, at_g)
    sq = place("sq", [P, KT, TOK], F32, at_g + XB)
    sg = place("sg", [P, 2, TOK], F32, at_g)
    hx = place("hx", [P, 2, TOK], F32, at_g + 2112)
    hh = place("hh", [P, D_FF // P, TOK], F32R, at_g + 4224)
    hl = place("hl", [P, D_FF // P, TOK], F32R, at_g + 4224 + (D_FF // P) * TOK * 4)
    yp = place("yp", [P, KT, TOK], F32, at_g + 4224 + 2 * (D_FF // P) * TOK * 4)
    sq2 = place("sq2", [P, KT, TOK], F32, at_g + 4224)
    y_tok = place("y_tok", [P, 2, D_MODEL], F32, at_g + 4224 + XB)
    ys_tok = place("ys_tok", [DEC, D_MODEL], F32, at_g + 4224 + XB + 2 * D_MODEL * 4)
    mu_r = place("mu_r", [P, 2, TOK], F32, at_g + 4224 + 2 * (D_FF // P) * TOK * 4 + XB)

    PS = nc.alloc_psum_tensor("ps", [P, 8, 512], F32)

    rows = lambda ap: ap.rearrange("(k p) c -> p k c", p=P)

    def claim(pe, name, index=0):
        for other, n in before(name, index):
            pe.wait_ge(*told("empty_" + other, n + 1))
        return banks(name, index)

    def lo_done(engine, n):
        if n < C_POOL_END:
            engine.wait_ge(*told("lo_pool", n + 1))
        else:
            engine.wait_ge(*told("lo_dve", n - C_POOL_END + 1))

    block = ctx.enter_context(nc.Block())

    @block.sync
    def _(sp):
        def load_chunk(n, slot, src, cols=COLS, freed=None):
            if freed is None and n >= RING:
                lo_done(sp, n - RING)
            elif freed is not None:
                sp.wait_ge(*told("lo_dve", freed))
            sp.dma_start(raw[:, slot, :, 0:cols], src).then_inc(sem(f"raw{slot}"), 16)

        w_in = A["w_in"][0]

        def load_pass(c0, col, cols=COLS):
            for kc in range(4):
                load_chunk(c0 + kc, (c0 + kc) % RING,
                           rows(w_in[kc * 512:(kc + 1) * 512, col:col + cols]), cols)

        sp.dma_start(x_nat[:, :, :], A["x_prompt"][0].rearrange("(n p) d -> p n d", p=P)).then_inc(sem("x_loaded"), 16)
        sp.dma_start(xs_nat[:, :], A["x_sample"].rearrange("b o d -> (b o) d")).then_inc(sem("x_loaded"), 16)
        kv_loads = [0]

        def load_cache(cache, n):
            pages = [sp.value_load(pt[0:1, (n % 16) * 4 + j:(n % 16) * 4 + j + 1], min_val=0,
                                   max_val=cache.shape[1] - 1) for j in range(4)]
            if n == 0:
                sp.wait_ge(sem("h_store"), 16)
            if n >= 2:
                sp.wait_ge(*told("kv_free", n - 1))
            for j, page in enumerate(pages):
                src = cache[0][ds(page, 1)].rearrange("o s h d -> (o s) (h d)")
                sp.dma_start(kv[:, n % 2, j, :], src).then_inc(sem(f"kv{n % 2}"), 16)

        hgrn_out = O["hgrn_sample"][0].rearrange("b h k v -> k (b h) v")

        def load_caches(n0, n1):
            for n in range(n0, n1):
                load_cache(A["cache_k"] if n < 16 else A["cache_v"], n)

        caches = [0]

        def load_due(n):
            due = sum(n >= at for at in CACHE_AT)
            load_caches(caches[0], due)
            caches[0] = due

        for p in range(PASSES_A):
            for kc in range(4):
                n, (col, cols) = 4 * p + kc, MIXER_COLS[p]
                load_chunk(n, n % RING, rows(w_in[kc * 512:(kc + 1) * 512, col:col + cols]), cols)
                if n == C_STATES:
                    sp.wait_ge(*told("s5_staged", 1))
                    for b in range(DEC):
                        sp.dma_start(s_smp[:, 4 * b:4 * b + 4, :],
                                     A["state_hgrn"][0, b].rearrange("h k v -> k h v")).then_inc(sem("s_smp"), 16)
                if n == C_STATES_OUT:
                    sp.wait_ge(*told("h_smp_done", 1))
                    sp.wait_ge(*made("h_os", 1))
                    sp.dma_start(hgrn_out, s_smp[:, :, :]).then_inc(sem("h_store"), 16)
                    sp.wait_ge(*told("consts_loaded", 16 * 5))
                load_due(n)

        def gate_passes(dg):
            for k in range(4):
                for half in range(2):
                    for kc in range(4):
                        n = C_GATE[dg] + 8 * k + 4 * half + kc
                        col = GT + k * D_MODEL + dg * 512 + half * COLS
                        load_chunk(n, n % RING, rows(w_in[kc * 512:(kc + 1) * 512, col:col + COLS]))
                        load_due(n)
                        if n == C_STATE_OUT:
                            sp.wait_ge(*told("h_done", 1))
                            sp.dma_start(O["hgrn_prompt"][0, 0].rearrange("h k v -> k h v"),
                                         s_prev[:, 1, :, :]).then_inc(sem("h_store"), 16)

        gate_passes(0)
        load_chunk(C_GLU, C_GLU % RING, rows(A["s5_w_glu"][0][:, 0:COLS]))
        load_chunk(C_GLU + 1, (C_GLU + 1) % RING, rows(A["s5_w_glu"][0][:, COLS:2 * COLS]))
        gate_passes(1)

        def load_merge(dg):
            for m, k in enumerate(MERGE_ORDER):
                for half in range(2):
                    n = C_MERGE[dg] + 2 * m + half
                    load_chunk(n, n % RING, rows(A["w_branch"][0, k][:, dg * 512 + half * COLS:dg * 512 + (half + 1) * COLS]))

        def load_gates(dg):
            base_c = C_GATE[dg]
            with nc.sync.Fori(0, 4) as k:
                for j in range(8):
                    n = base_c + j
                    src = w_in[(j % 4) * 512:(j % 4 + 1) * 512, ds(k * D_MODEL + (GT + dg * 512 + (j // 4) * COLS), COLS)]
                    load_chunk(None, n % RING, rows(src), freed=k * 8 + (n - RING - C_POOL_END + 1))

        def load_square(w, c0, count, tiles):
            with nc.sync.Fori(0, count) as i:
                for j in range(2 * tiles):
                    n = c0 + j
                    src = w[(j % tiles) * 512:(j % tiles + 1) * 512, ds(i * (2 * COLS) + (j // tiles) * COLS, COLS)]
                    load_chunk(None, n % RING, rows(src), freed=i * (2 * tiles) + (n - RING - C_POOL_END + 1))

        load_merge(0)
        load_merge(1)
        for dg in (2, 3):
            load_gates(dg)
            load_merge(dg)
        load_square(A["w_out"][0], C_OUT, 4, 4)
        w_up = A["w_ffn_up"][0]
        with nc.sync.Fori(0, UP_STEPS) as i:
            for j in range(8):
                n = C_UP + j
                src = w_up[(j % 4) * 512:(j % 4 + 1) * 512, ds(i * COLS + (j // 4) * D_FF, COLS)]
                load_chunk(None, n % RING, rows(src), freed=i * 8 + (n - RING - C_POOL_END + 1))
        w_down = A["w_ffn_down"][0]
        with nc.sync.Fori(0, 2) as i:
            for j in range(4 * DOWN_CHUNKS):
                n = C_DOWN + j
                ps, kc = j // DOWN_CHUNKS, j % DOWN_CHUNKS
                src = w_down[kc * 512:(kc + 1) * 512, ds(i * (4 * COLS) + ps * COLS, COLS)]
                load_chunk(None, n % RING, rows(src), freed=i * (4 * DOWN_CHUNKS) + (n - RING - C_POOL_END + 1))
        for half in range(4):
            sp.wait_ge(*told("y_copied", 3 * half + 3))
            c = slice(half * 512, half * 512 + 512)
            sp.dma_start(O["y_prompt"][0].rearrange("(n p) d -> p n d", p=P)[:, :, c], y_tok[:, :, c]).then_inc(sem("stored"), 16)
            sp.dma_start(O["y_sample"].rearrange("b o d -> (b o) d")[:, c], ys_tok[:, c]).then_inc(sem("stored"), 16)
        sp.wait_ge(*told("stored", 16 * 8))
        sp.wait_ge(*told("h_store", 16 * 2))

    @block.gpsimd
    def _(pool):
        steps = Steps(pool, sem("pool_steps"), tell)
        steps.do(pool.memset(ident[:, :], 0.0))
        steps.then(pool.memset(ones[:, :], 1.0))
        steps.then(pool.affine_select(out=ident[:, :], in_=ident[:, :], compare_op=ALU.not_equal, fill=1.0, base=0,
                                      pattern=[[-1, P]], channel_multiplier=1))
        tell(pool, "ident_ready")
        steps.do(pool.iota(iota_t[:, :], [[1, SEQ]], base=0, channel_multiplier=0,
                           allow_small_or_imprecise_dtypes=True))
        steps.do(pool.iota(small[:, 0:1].bitcast(I32), [[0, 1]], base=0, channel_multiplier=1))
        steps.do(pool.iota(level_mask[:, 0, :], [[1, P]], base=0, channel_multiplier=0))
        steps.do(pool.iota(level_mask[:, 1, :], [[0, P]], base=0, channel_multiplier=1))
        steps.do(pool.memset(bd[:, :, :, :, :], 0.0))
        steps.then(pool.memset(eye8[:, :, :], 0.0))
        steps.do(pool.affine_select(out=eye8[:, :, :], in_=eye8[:, :, :], compare_op=ALU.not_equal, fill=1.0, base=0,
                                    pattern=[[1, DEC], [-1, DEC]], channel_multiplier=0))
        pool.wait_ge(*told("mix_loaded", 16 * 10))
        steps.do(pool.affine_select(out=ws_nat[:, :, :], in_=ws_nat[:, :, :], compare_op=ALU.is_ge, fill=0.0, base=0,
                                    pattern=[[0, MT], [-1, P]], channel_multiplier=1))
        steps.then(pool.memset(causal[:, :], 0.0))
        steps.do(pool.affine_select(out=causal[:, :], in_=causal[:, :], compare_op=ALU.is_ge, fill=NEG, base=0,
                                    pattern=[[-1, P]], channel_multiplier=1))
        steps.tell("consts_ready")

        def low_parts(c0, c1):
            with nc.gpsimd.Fori(0, (c1 - c0) // RING) as i:
                for j in range(RING):
                    n = c0 + j
                    pool.wait_ge(*told("hi_done", i * RING + (n + 1)))
                    pool.tensor_tensor(w_lo[:, j, :, :], raw[:, j, :, :], w_hi[:, j, :, :],
                                       ALU.subtract).then_inc(sem("lo_pool"), 1)

        low_parts(0, 88)
        pool.wait_ge(*told("h_done", 1))
        steps.then(pool.memset(tri[:, :], 1.0))
        steps.then(pool.affine_select(out=tri[:, :], in_=tri[:, :], compare_op=ALU.is_gt, fill=0.0, base=0,
                                      pattern=[[-1, 64]], channel_multiplier=1))
        steps.then(pool.affine_select(out=tri[:, :].rearrange("k (b p) -> k b p", p=8),
                                      in_=tri[:, :].rearrange("k (b p) -> k b p", p=8), compare_op=ALU.is_ge,
                                      fill=0.0, base=7, pattern=[[8, 8], [0, 8]], channel_multiplier=-1))
        pool.wait_ge(*told("consts_loaded", 16 * 5))
        table = A["cache_logf"][0].rearrange("n s h -> n (s h)")
        pool.indirect_dma_start(out=lfp[:, :, :].rearrange("r s h -> r (s h)"), out_offset=None, in_=table,
                                in_offset=bass.IndirectOffsetOnAxis(ap=pt_col[:, 0:1], axis=0)).then_inc(sem("lfp"), 16)
        low_parts(88, 148)
        for n in (148, 149):
            pool.wait_ge(*told("hi_done", n + 1))
            pool.tensor_tensor(w_lo[:, n % RING, :, :], raw[:, n % RING, :, :], w_hi[:, n % RING, :, :],
                               ALU.subtract).then_inc(sem("lo_pool"), 1)


    targets = []
    for name in ("su", "hf", "hi", "hq", "fq", "hg", "fk", "fv"):
        targets += [(name, 0), (name, 1)]
    targets.append(("ff", 0))
    for name in ("gv", "gu"):
        targets += [(name, 0), (name, 1)]
    where = dict(su=su, hf=hf, hq=hq, hi=hi_, hg=hg, fq=fq, fk=fk, fv=fv, gv=gv, gu=gu)
    functions = dict(gv=ACT.Gelu_apprx_tanh, gu=ACT.Gelu_apprx_tanh, hg=ACT.Silu)

    def projected(engine, name):
        for p in range(PASSES_A):
            if targets[p][0] == name:
                engine.wait_ge(*told(f"evac{p % 2}", p // 2 + 1))

    BANK = lambda p: 2 * (p % 2)

    @block.tensor
    def _(pe):
        def products(slot, bank, right_h, right_l, k0, first, last, cols=COLS):
            for kk in range(CK):
                rh, rl = right_h[:, k0 + kk, :], right_l[:, k0 + kk, :]
                for half in range(cols // P):
                    out = PS[:, bank + half, 0:TOK]
                    c = slice(half * P, half * P + P)
                    nc.tensor.matmul(out, w_hi[:, slot, kk, c], rh, start=(first and kk == 0), stop=False)
                    nc.tensor.matmul(out, w_hi[:, slot, kk, c], rl, start=False, stop=False)
                    ins = nc.tensor.matmul(out, w_lo[:, slot, kk, c], rh, start=False, stop=(last and kk == CK - 1))
            ins.then_inc(sem("used"), 1)

        done = [0]

        def chunk(p, kc, chunks, right_h, right_l, cols=COLS):
            n = done[0]
            if kc == 0 and p >= 2:
                pe.wait_ge(*told(f"evac{p % 2}", p // 2))
            lo_done(pe, n)
            products(n % RING, BANK(p), right_h, right_l, CK * kc, kc == 0, kc == chunks - 1, cols)
            done[0] += 1

        def weights(upto):
            while done[0] < upto:
                n = done[0]
                if n < C_GATE[0]:
                    p = n // 4
                    chunk(p, n % 4, 4, xh, xl, MIXER_COLS[p][1])
                elif n < C_GLU:
                    chunk(P_GATE[0] + (n - C_GATE[0]) // 4, (n - C_GATE[0]) % 4, 4, xh, xl)
                elif n < C_GATE[1]:
                    if n == C_GLU:
                        pe.wait_ge(*told("g_split", 1))
                    chunk(P_GLU + n - C_GLU, 0, 1, gh1, gl1)
                else:
                    chunk(P_GATE[1] + (n - C_GATE[1]) // 4, (n - C_GATE[1]) % 4, 4, xh, xl)

        def transposes(name, index, parts):
            bank = claim(pe, name, index)[0]
            for col, src in parts:
                p, f = src.shape[0], src.shape[-1]
                ins = nc.tensor.transpose(PS[0:f, bank + col // 512, col % 512:col % 512 + p], src, ident[0:p, 0:p])
            ins.then_inc(sem("made"), 1)

        pe.wait_ge(*told("ident_ready", 1))
        pe.wait_ge(*told("x_loaded", 32))
        for k in range(KT):
            c = slice(k * P, k * P + P)
            transposes("x", k, [(0, x_nat[:, 0, c]), (P, x_nat[:, 1, c]), (SEQ, xs_nat[:, c])])

        pe.wait_ge(*told("mix_loaded", 16 * 10))
        transposes("vecs", 0, [(0, vec_nat[:, :])])
        pe.wait_ge(*told("s5_loaded", 16 * 9))
        transposes("s5_h0", 0, [(128 * r + 8 * i, h0_nat[:, r, i * P:i * P + P]) for r in range(2) for i in range(S5_TILES)])
        pe.wait_ge(*told("s5_par", 1))
        transposes("s5_lam", 0, [(16 * k, sp[:, 2 + k, :]) for k in range(6)])
        pe.wait_ge(*told("x_split", KT))
        weights(2)
        pe.wait_ge(*told("s5_cd", 1))
        for r in range(2):
            transposes("s5_ct", r, [(P * q, cd[:, r, q, :, :].rearrange("p a b -> p (a b)")) for q in range(MT)])
        pe.wait_ge(*told("consts_ready", 1))
        transposes("g_ws", 0, [(P * g, ws_nat[:, g, :]) for g in range(MT)])
        weights(5)
        pe.wait_ge(*told("s5_bd", 1))
        for r in range(2):
            transposes("s5_bt", r, [(P * q, bd[:, r, 4 * q:4 * q + 4, :, :].rearrange("p i g h -> p (i g h)"))
                                    for q in range(MT)])
        weights(12)

        def s5_input(i, r):
            rows_ = slice(32 * (i % 4), 32 * (i % 4) + 32)
            return bt[rows_, r, i // 4, :], su[rows_, i // 4, :]

        projected(pe, "su")
        pe.wait_ge(*told("s5_bt_ready", 1))
        bank = claim(pe, "s5_bus")[0]
        for r in range(2):
            for i in range(S5_TILES):
                b, u = s5_input(i, r)
                col = (4 * r + i // 4) * DEC
                ins = nc.tensor.matmul(PS[:, bank + i % 4, col:col + DEC], b, u[:, SEQ:TOK], start=True, stop=True)
        ins.then_inc(sem("made"), 1)

        def s5_bu(b):
            bank = claim(pe, "s5_bu", b)[0]
            for t in range(2):
                for r in range(2):
                    w, u = s5_input(2 * b + t, r)
                    ins = nc.tensor.matmul(PS[:, bank + t, r * SEQ:r * SEQ + SEQ], w, u[:, 0:SEQ], start=True, stop=True)
            ins.then_inc(sem("made"), 1)

        def s5_y(b):
            bank = claim(pe, "s5_y", b)[0] if b % 2 == 0 else banks("s5_y", b)[0]
            pe.wait_ge(*told("s5_h", b + 1))
            pe.wait_ge(*told("s5_hs", 1))
            for t in range(2):
                i = 2 * b + t
                q, j = i // 4, i % 4
                out = PS[32 * j:32 * j + 32, bank, :]
                for (lo, n), st in (((0, SEQ), (hr[:, t, :], hm[:, t, :])), ((SEQ, DEC), (hs[:, 0, i, :], hs[:, 1, i, :]))):
                    for r in range(2):
                        ins = nc.tensor.matmul(out[:, lo:lo + n], ct[:, r, q, 32 * j:32 * j + 32], st[r],
                                               start=(r == 0), stop=(r == 1), tile_position=(0, 32 * j))
            ins.then_inc(sem("made"), 1)

        s5_bu(0)
        for b in range(1, 8):
            weights(S5_AT + S5_GAP * b - 2)
            s5_bu(b)
            if b == H_SMP + 1:
                bank = claim(pe, "h_os")[0]
                pe.wait_ge(*told("h_smp_done", 1))
                for h in range(HEADS):
                    for n in range(DEC):
                        ins = nc.tensor.matmul(PS[0:DEC, bank, h * P:h * P + P], qm[:, h, n, :], s_smp[:, 4 * n + h, :],
                                               start=(n == 0), stop=(n == DEC - 1))
                ins.then_inc(sem("made"), 1)
            weights(S5_AT + S5_GAP * b + 1)
            s5_y(b - 1)
            if b == H_SMP:
                projected(pe, "hi")
                transposes("h_vs", 0, [(P * h, hi_[:, h, SEQ:TOK]) for h in range(HEADS)])
                pe.wait_ge(*told("h_vs_tok", 1))
                for n in range(DEC):
                    bank = claim(pe, "h_vb", n)[0]
                    nc.tensor.matmul(PS[:, bank, :], ident[0:DEC, n:n + 1].to_broadcast([DEC, P]), t8[:, 0, :],
                                     start=True, stop=True).then_inc(sem("made"), 1)
        weights(S5_AT + S5_GAP * 8)
        s5_y(7)
        weights(S5_AT + S5_GAP * 8 + 1)
        bank = claim(pe, "s5_out")[0]
        pe.wait_ge(*told("s5_sf", 1))
        for r in range(2):
            ins = nc.tensor.transpose(PS[0:S5_TILES, bank, r * P:r * P + P], sf[:, r, :], ident[:, :])
        ins.then_inc(sem("made"), 1)
        for n in range(8):
            transposes("s5_outs", n, [(P * i, hs[:, n // 4, 4 * (n % 4) + i, :]) for i in range(4)])

        pe.wait_ge(*told("h_os_tok", 1))
        transposes("h_ost", 0, [(P * h, q8[:, h * P:h * P + P]) for h in range(HEADS)])
        for c in range(2):
            transposes("h_v", c, [(P * h, hi_[:, h, c * P:c * P + P]) for h in range(HEADS)])
        projected(pe, "fq")
        transposes("f_tok", 0, [(P * h, fq[:, h, SEQ:TOK]) for h in range(HEADS)])
        for n in range(NL + 1):
            weights(H_AT + H_GAP * n)
            bank = claim(pe, "f_qb", n)[0]
            if n == 0:
                pe.wait_ge(*told("f_qtok", 1))
            nc.tensor.matmul(PS[:, bank, :], ident[0:DEC, n:n + 1].to_broadcast([DEC, P]), q8[:, :],
                             start=True, stop=True).then_inc(sem("made"), 1)
            bank = claim(pe, "h_att", n)[0]
            if n < NL:
                pe.wait_ge(*told("h_qe", n + 1))
            for hc in range(8):
                h, c = hc // 2, hc % 2
                t = slice(c * P, c * P + P)
                keys, queries = (ke[:, hc, :], qe[:, hc, :]) if n < NL else (kt_[:, h, t], hq[:, h, t])
                ins = nc.tensor.matmul(PS[:, bank + hc // 4, (hc % 4) * P:(hc % 4) * P + P], keys, queries,
                                       start=True, stop=True)
            ins.then_inc(sem("made"), 1)
        weights(77)
        pe.wait_ge(*told("h_kd", 1))
        transposes("h_kd", 0, [(P * hc, qe[:, hc, :]) for hc in range(8)])
        weights(78)
        pe.wait_ge(*told("h_kdt", 1))

        def h_state(c):
            bank = claim(pe, ("h_s", "h_last")[c])[0]
            for h in range(HEADS):
                ins = nc.tensor.matmul(PS[:, bank, h * P:h * P + P], ke[:, 2 * h + c, :],
                                       v_tok[:, c, h * P:h * P + P], start=True, stop=True)
            ins.then_inc(sem("made"), 1)

        h_state(0)
        weights(79)
        bank = claim(pe, "h_o")[0]
        pe.wait_ge(*told("h_s0", 1))
        pe.wait_ge(*told("h_att_done", 1))
        for h in range(HEADS):
            out = PS[:, bank + h // 2, (h % 2) * SEQ:(h % 2) * SEQ + SEQ]
            v = slice(h * P, h * P + P)
            nc.tensor.matmul(out[:, 0:P], v_tok[:, 0, v], att[:, 2 * h, :], start=True, stop=True)
            nc.tensor.matmul(out[:, P:SEQ], v_tok[:, 1, v], att[:, 2 * h + 1, :], start=True, stop=False)
            ins = nc.tensor.matmul(out[:, P:SEQ], s_prev[:, 0, h, :], qb_h[:, h, :], start=False, stop=True)
        ins.then_inc(sem("made"), 1)
        h_state(1)
        weights(80)
        weights(81)
        bank = claim(pe, "h_ms")[0]
        pe.wait_ge(*told("h_sq", 1))
        for h in range(HEADS):
            ins = nc.tensor.matmul(PS[:, bank + h, 0:TOK], ones[:, :], lnt[:, h, :], start=True, stop=True)
        ins.then_inc(sem("made"), 1)

        def sums(name, index, src, tiles):
            bank = claim(pe, name, index)[0]
            for t in range(tiles):
                ins = nc.tensor.matmul(PS[:, bank, 0:TOK], ones[:, :], src[:, t, :], start=(t == 0), stop=(t == tiles - 1))
            ins.then_inc(sem("made"), 1)

        weights(88)
        projected(pe, "gv")
        sums("g_mu", 0, gv, MT)
        weights(90)
        pe.wait_ge(*told("g_sq", 1))
        sums("g_var", 0, gsq, MT)
        weights(92)
        pe.wait_ge(*told("g_vn", 1))
        for c in range(2):
            transposes("g_tok", c, [(P * g, gv[:, g, c * P:c * P + P]) for g in range(MT)])
        transposes("g_tok", 2, [(P * g, gv[:, g, SEQ:TOK]) for g in range(MT)])
        weights(94)
        pe.wait_ge(*told("g_tokens", 1))
        for n in range(2):
            bank = claim(pe, "g_mix", n)[0]
            for g in range(MT):
                out = PS[:, bank, g * P:g * P + P]
                nc.tensor.matmul(out, v_tok[:, n, g * P:g * P + P], ws_t[:, g, :], start=True, stop=False)
                ins = nc.tensor.matmul(out, ones[0:1, :], bs_row[0:1, g, :], start=False, stop=True)
            ins.then_inc(sem("made"), 1)
        bank = claim(pe, "g_ms")[0]
        pe.wait_ge(*told("consts_loaded", 16 * 5))
        nc.tensor.matmul(PS[:, bank, 0:MT], ones[0:1, :], ws00[0:1, :], start=True, stop=True)
        nc.tensor.matmul(PS[:, bank, MT:2 * MT], ones[0:1, :], bs_row[0:1, :, 0], start=True,
                         stop=True).then_inc(sem("made"), 1)

        weights(95)
        pe.wait_ge(*told("f_lf", 1))
        transposes("f_lf", 0, [(0, lf_t[:, 0:P]), (4, lf_t[:, P:SEQ]), (8, lf_t[:, SEQ:TOK])])
        bank = claim(pe, "f_suf")[0]
        pe.wait_ge(*told("f_rc", 1))
        nc.tensor.matmul(PS[0:64, bank, 0:HEADS], tri[:, :], rc[:, 0, :], start=True, stop=True).then_inc(sem("made"), 1)
        weights(97)
        bank = claim(pe, "f_suft")[0]
        pe.wait_ge(*told("f_suf_in", 1))
        for h in range(HEADS):
            ins = nc.tensor.transpose(PS[:, bank, h * 64:h * 64 + 64], rc[:, :, h], ident[0:64, 0:64])
        ins.then_inc(sem("made"), 1)
        bank = claim(pe, "f_new")[0]
        pe.wait_ge(*told("f_qk", 1))
        nc.tensor.matmul(PS[0:32, bank, 0:1], small[:, 8:40], ones[:, 0:1], start=True, stop=True)
        nc.tensor.matmul(PS[0:32, bank, 1:2], cum[:, 1, 0:32], ones[0:HEADS, 0:1], start=True,
                         stop=True).then_inc(sem("made"), 1)
        bank = claim(pe, "f_sct")[0]
        pe.wait_ge(*told("f_sc", 1))
        for pg in range(N_PAGES):
            ins = nc.tensor.transpose(PS[0:32, bank + pg // 4, (pg % 4) * P:(pg % 4) * P + P], sc[:, pg, :], ident[:, :])
        ins.then_inc(sem("made"), 1)
        weights(100)
        bank = claim(pe, "f_pt")[0]
        pe.wait_ge(*told("f_prob", 1))
        for pg in range(N_PAGES):
            ins = nc.tensor.transpose(PS[:, bank, pg * 32:pg * 32 + 32], ps_row[:, pg * P:pg * P + P], ident[0:32, 0:32])
        ins.then_inc(sem("made"), 1)
        bank = claim(pe, "f_pn")[0]
        nc.tensor.matmul(PS[:, bank, 0:32], ones[0:32, :], small[0:32, 0:32], start=True, stop=True).then_inc(sem("made"), 1)
        for n in range(1, 7):
            src, c = (fk, fv)[(n - 1) // 3], (n - 1) % 3
            t = slice(c * P, c * P + P) if c < 2 else slice(SEQ, TOK)
            transposes("f_tok", n, [(P * h, src[:, h, t]) for h in range(HEADS)])
        used_values = [0]

        def values(upto):
            while used_values[0] < upto:
                b = used_values[0]
                bank = claim(pe, "f_os")[0] if b == 0 else banks("f_os", 0)[0]
                pe.wait_ge(*told("f_vsum", b + 1))
                ins = nc.tensor.matmul(PS[0:DEC, bank, :], eye8[:, b, :], vacc[:, b % 2, :], start=(b == 0), stop=(b == 7))
                ins.then_inc(sem("values_used" if b < 7 else "made"), 1)
                used_values[0] += 1

        pe.wait_ge(*told("f_cum", 1))
        for i in range(2):
            weights(104 + 16 * i)
            values(2 * i)
            bank = claim(pe, "f_s", i)[0]
            t, keys = slice(i * P, i * P + P), (i + 1) * P
            for h in range(HEADS):
                out = PS[:, bank + h // 2, (h % 2) * SEQ:(h % 2) * SEQ + keys]
                nc.tensor.matmul(out, fq[:, h, t], fk[:, h, 0:keys], start=True, stop=False)
                nc.tensor.matmul(out, cum[:, 0, t], ident[0:HEADS, h:h + 1].to_broadcast([HEADS, keys]),
                                 start=False, stop=False)
                ins = nc.tensor.matmul(out, ident[0:HEADS, h:h + 1].to_broadcast([HEADS, P]), cum[:, 1, 0:keys],
                                       start=False, stop=True)
            ins.then_inc(sem("made"), 1)
            weights(109 + 16 * i)
            values(2 * i + 1)
            pbanks = claim(pe, "f_p", i)
            pe.wait_ge(*told("f_prompt", i + 1))
            for kb in range(i + 1):
                for h in range(HEADS):
                    ins = nc.tensor.transpose(PS[:, pbanks[kb], h * P:h * P + P], s_sb[:, h, kb * P:kb * P + P], ident[:, :])
            ins.then_inc(sem("made"), 1)
            weights(114 + 16 * i)
            bank = claim(pe, "f_o", i)[0]
            pe.wait_ge(*told("f_pt_sb", i + 1))
            for h in range(HEADS):
                for kb in range(i + 1):
                    ins = nc.tensor.matmul(PS[:, bank, h * P:h * P + P], v_tok[:, kb, h * P:h * P + P],
                                           pt_sb[:, kb, h, :], start=(kb == 0), stop=(kb == i))
            ins.then_inc(sem("made"), 1)
        for b in range(3, 8):
            weights(135 + 2 * (b - 3))
            values(b + 1)
        weights(148)
        pe.wait_ge(*told("f_ostok", 1))
        transposes("f_ost", 0, [(P * h, t8[:, 0, h * P:h * P + P]) for h in range(HEADS)])
        weights(150)

        def merge(dg):
            for m, k in enumerate(MERGE_ORDER):
                if dg == 0:
                    pe.wait_ge(*told(f"branch{k}", 1))
                for half in range(2):
                    chunk(P_MERGE[dg] + 2 * m + half, 0, 1, bh[k], bl[k])

        def loop(c0, p0, turns, chunks_of, right_h, right_l, passes):
            per = passes * chunks_of
            with nc.tensor.Fori(0, turns) as i:
                for j in range(per):
                    n, p, kc = c0 + j, p0 + j // chunks_of, j % chunks_of
                    if kc == 0:
                        pe.wait_ge(*told(f"evac{p % 2}", i * (passes // 2) + p // 2))
                    pe.wait_ge(*told("lo_dve", i * per + (n - C_POOL_END + 1)))
                    products(n % RING, BANK(p), right_h, right_l, CK * kc, kc == 0, kc == chunks_of - 1)
            done[0] = c0 + turns * per

        merge(0)
        merge(1)
        for dg in (2, 3):
            loop(C_GATE[dg], P_GATE[dg], 4, 4, xh, xl, 2)
            merge(dg)
        pe.wait_ge(*told("merged", 4))
        loop(C_OUT, P_OUT, 4, 4, mh, ml, 2)

        def layer_sums(n, src, squares):
            pe.wait_ge(*told(f"pre{n}", 1))
            sums("l_mu", n, src, KT)
            bank = claim(pe, "l_var", n)[0]
            for t in range(KT):
                if t % 4 == 0:
                    pe.wait_ge(*told(f"sq{n}", t // 4 + 1))
                ins = nc.tensor.matmul(PS[:, bank, 0:TOK], ones[:, :], squares[:, t, :], start=(t == 0), stop=(t == KT - 1))
            ins.then_inc(sem("made"), 1)

        layer_sums(0, xp, sq)
        pe.wait_ge(*told("x1_ready", 4))
        loop(C_UP, P_UP, UP_STEPS, 4, xh, xl, 2)
        pe.wait_ge(*told("hl_done", UP_STEPS))
        loop(C_DOWN, P_DOWN, 2, DOWN_CHUNKS, hh, hl, 4)
        layer_sums(1, yp, sq2)
        for t4 in range(4):
            pe.wait_ge(*told("y_ready", t4 + 1))
            for c in range(3):
                t = slice(c * P, c * P + P) if c < 2 else slice(SEQ, TOK)
                transposes("y", 3 * t4 + c, [(P * j, yp[:, 4 * t4 + j, t]) for j in range(4)])

    @block.scalar
    def _(act):
        steps = Steps(act, sem("act_steps"), tell)
        A_ = nc.scalar.activation

        def load(dst, src, name):
            act.dma_start(dst, src, allow_slow_non_contiguous=True).then_inc(sem(name), 16)

        load(sp[:, 0, :], A["s5_lambda_re"][0].rearrange("(i g) p -> i (g p)", g=2), "s5_loaded")
        load(sp[:, 1, :], A["s5_lambda_im"][0].rearrange("(i g) p -> i (g p)", g=2), "s5_loaded")
        load(dt2[:, :], A["s5_log_dt"][0].rearrange("(i g) -> i g", g=2), "s5_loaded")
        for r, part in enumerate(("re", "im")):
            load(cn[:, r, :, :], A[f"s5_c_{part}"][0].rearrange("(q g) h p -> (g h) q p", g=8), "s5_loaded")
            load(bn[:, r, :, :], A[f"s5_b_{part}"][0].rearrange("(i g) p h -> (g p) i h", g=2), "s5_loaded")
            load(h0_nat[:, r, :], A[f"state_s5_{part}"][0].rearrange("b g p -> b (g p)"), "s5_loaded")
        load(ws_nat[:, :, :], A["gmlp_w_s"][0].rearrange("g t s -> t g s"), "mix_loaded")
        for n, name in enumerate(("ln1_g", "ln1_b", "ln2_g", "ln2_b")):
            load(vec_nat[n * KT:(n + 1) * KT, :], A[name][0].rearrange("(t p) -> t p", p=P), "mix_loaded")
        for n, name in enumerate(("s5_d", "s5_b_glu", "hgrn_norm_g", "gmlp_ln_g", "gmlp_ln_b")):
            load(vec_nat[4 * KT + n * MT:4 * KT + (n + 1) * MT, :], A[name][0].rearrange("(t p) -> t p", p=P), "mix_loaded")
        load(bs_row[:, :, :], A["gmlp_b_s"], "consts_loaded")
        load(ws00[:, :], A["gmlp_w_s"][:, :, 0, 0], "consts_loaded")
        load(bf[:, :], A["fox_bf"][0].rearrange("(h o) -> h o", o=1), "consts_loaded")
        load(pt[:, :], A["page_table"].rearrange("(o b) n -> o (b n)", o=1), "consts_loaded")
        load(pt_col[:, :], A["page_table"].rearrange("b (n o) -> (b n) o", o=1), "consts_loaded")

        for k in range(KT):
            act.wait_ge(*made("x", k + 1))
            A_(xh[:, k, :], PS[:, 4 + k % 4, 0:TOK], ACT.Copy).then_inc(sem("xh_done"), 1)

        done = [0]

        def split(n, slot, turn, used):
            act.wait_ge(*told(f"raw{slot}", turn))
            if used is not None:
                act.wait_ge(*told("used", used))
            A_(w_hi[:, slot, :, :], raw[:, slot, :, :], ACT.Copy).then_inc(sem("hi_done"), 1)

        def high(n):
            split(n, n % RING, 16 * (n // RING + 1), n - RING + 1 if n >= RING else None)
            done[0] = n + 1

        def evacuate(p):
            src = PS[:, BANK(p):BANK(p) + 2, 0:TOK]
            if p < PASSES_A:
                act.wait_ge(*told("used", 4 * p + 4))
                name, half = targets[p]
                if name == "ff":
                    ins = A_(lf_t[:, :], PS[0:HEADS, BANK(p), 0:TOK], ACT.Copy)
                else:
                    ins = A_(where[name][:, 2 * half:2 * half + 2, :], src, functions.get(name, ACT.Copy))
            else:
                dg = 0 if p < P_GLU else 1
                m = p - P_GATE[dg]
                act.wait_ge(*told("used", C_GATE[dg] + 4 * m + 4))
                if m == 0 and dg == 0:
                    act.wait_ge(*told("h_store", 32))
                    act.wait_ge(*told("h_done", 1))
                if m == 4 and dg == 1:
                    act.wait_ge(*made("f_o", 2))
                ins = A_(gates[:, 16 * dg + 2 * m:16 * dg + 2 * m + 2, :], src, ACT.Sigmoid)
            ins.then_inc(sem(f"evac{p % 2}"), 1)

        evacuated = [0]

        def weights(upto):
            while done[0] < upto:
                high(done[0])
                behind = done[0] - RING
                p = evacuated[0]
                end = 4 * p + 4 if p < P_GLU else C_GATE[1] + 4 * (p - P_GATE[1]) + 4
                if p < P_GLU or p >= P_GATE[1]:
                    if behind >= end and p < P_MERGE[0]:
                        evacuate(p)
                        evacuated[0] += 1
                elif behind >= C_GLU + 2:
                    glu_gate()
                    evacuated[0] += 2

        def glu_gate():
            act.wait_ge(*told("g_done", 1))
            act.wait_ge(sem("fox_stored"), 16 * 6)
            for half in range(2):
                p = P_GLU + half
                act.wait_ge(*told("used", C_GLU + half + 1))
                for t in range(2):
                    ins = A_(sgl[:, 2 * half + t, :], PS[:, BANK(p) + t, 0:TOK], ACT.Sigmoid,
                             bias=vecs[:, 1, 2 * half + t:2 * half + t + 1])
                ins.then_inc(sem(f"evac{p % 2}"), 1)

        def copied(name, index, dst, src, ready=None, release=1):
            act.wait_ge(*made(name, index + 1))
            steps.then(A_(dst, src, ACT.Copy))
            tell(act, "empty_" + name, release)
            if ready:
                tell(act, ready, 1)

        act.wait_ge(*told("s5_loaded", 16 * 9))
        steps.then(A_(dt2[:, :], dt2[:, :], ACT.Exp))
        tell(act, "a_dt", 1)
        weights(2)
        act.wait_ge(*made("vecs", 1))
        steps.do(A_(lnv[:, :, :].rearrange("p a b -> p (a b)"), PS[:, 6, 0:4 * KT], ACT.Copy))
        steps.tell("vecs_lnv")
        copied("vecs", 0, vecs[:, :, :].rearrange("p a b -> p (a b)"), PS[:, 6, 4 * KT:4 * KT + 5 * MT], "vecs_ready")
        act.wait_ge(*told("d_lrdt", 1))
        steps.then(A_(sp[:, 2, :], sp[:, 8, :], ACT.Exp))
        tell(act, "a_mag", 1)
        act.wait_ge(*told("d_turns", 1))
        steps.do(A_(sp[:, 9, :], sp[:, 3, :], ACT.Sin, scale=PI_))
        steps.do(A_(sp[:, 10, :], sp[:, 3, :], ACT.Sin, scale=2 * PI_))
        steps.tell("a_sin")
        copied("s5_h0", 0, h0[:, :, :, :].rearrange("p r i b -> p (r i b)"), PS[:, 5, 0:256], "h0_ready")
        copied("s5_lam", 0, lam_t[:, :, :].rearrange("p k i -> p (k i)"), PS[:, 4, 0:96], "lam_ready")
        weights(4)
        for r in range(2):
            copied("s5_ct", r, ct[:, r, :, :].rearrange("p q c -> p (q c)"), PS[:, (7, 5)[r], :])
        copied("g_ws", 0, ws_t[:, :, :].rearrange("p q c -> p (q c)"), PS[:, 6, :])

        def s5_table(b):
            act.wait_ge(*told("d_angle", b + 1))
            steps.do(A_(er[:, b % 2, :, :], tab[:, :, :], ACT.Sin, scale=PI_))
            steps.then(A_(ei[:, b % 2, :, :], tab[:, :, :], ACT.Sin, scale=2 * PI_))
            steps.then(A_(er[:, b % 2, :, :], er[:, b % 2, :, :], ACT.Square))
            tell(act, "a_table", 1)

        s5_table(0)
        weights(7)
        for r in range(2):
            copied("s5_bt", r, bt[:, r, :, :].rearrange("p q c -> p (q c)"), PS[:, 4 + r, :])
        tell(act, "s5_bt_ready", 1)
        tell(act, "s5_staged", 1)
        weights(13)
        s5_table(1)
        weights(16)
        copied("s5_bus", 0, bus[:, :, :, :].rearrange("p r (q j) b -> p j (r q) b", j=4),
               PS[:, 4:8, 0:64].rearrange("p j (m b) -> p j m b", b=DEC), "bus_ready")
        for b in range(2, 8):
            weights(S5_AT + S5_GAP * b)
            s5_table(b)
            if b == H_SMP:
                weights(S5_AT + S5_GAP * b + 2)
                projected(act, "hf")
                steps.do(A_(kt_[:, :, :], hf[:, :, :], ACT.Sigmoid, scale=-1.0))
                steps.then(A_(small[:, 8:40].rearrange("p (h b) -> p h b", h=HEADS), hf[:, :, SEQ:TOK], ACT.Sigmoid))
                tell(act, "a_smp", 1)
                copied("h_vs", 0, t8[:, 0, :], PS[0:DEC, 4, :], "h_vs_tok")
        copied("h_os", 0, q8[:, :], PS[0:DEC, 7, :], "h_os_tok")
        weights(S5_AT + S5_GAP * 8 + 4)
        act.wait_ge(*told("s5_yd", 1))
        steps.then(A_(su[:, :, :], su[:, :, :], ACT.Gelu_apprx_tanh))
        steps.then(A_(gh1[:, :, :], su[:, :, :], ACT.Copy))
        tell(act, "gh_done", 1)
        so = sc[0:S5_TILES, :, :].rearrange("i a b -> i (a b)")
        copied("s5_out", 0, so, PS[0:S5_TILES, 4, 0:256])
        for r, part in enumerate(("re", "im")):
            act.dma_start(O[f"s5_{part}_prompt"][0, 0].rearrange("(i g) p -> i (g p)", g=2),
                          so[:, r * P:(r + 1) * P]).then_inc(sem("so_stored"), 16)
        for n in range(8):
            if n == 0:
                act.wait_ge(*made("h_vb", 8))
            if n >= 2:
                act.wait_ge(*told(f"t8_stored{n % 2}", 16 * (n // 2)))
            copied("s5_outs", n, t8[:, n % 2, :], PS[0:DEC, 5 + n % 2, :])
            part = ("re", "im")[n // 4]
            out = O[f"s5_{part}_sample"][0].rearrange("b g p -> b (g p)")[:, (n % 4) * 512:(n % 4 + 1) * 512]
            act.dma_start(out, t8[:, n % 2, :]).then_inc(sem(f"t8_stored{n % 2}"), 16)
        steps.then(A_(lnt[:, :, :], hf[:, :, :], ACT.Abs))
        steps.then(A_(lnt[:, :, :], lnt[:, :, :], ACT.Exp, scale=-1.0))
        steps.then(A_(lnt[:, :, :], lnt[:, :, :], ACT.Ln, bias=1.0))
        tell(act, "a_ln", 1)
        copied("h_ost", 0, hos[:, :].rearrange("p (h b) -> p h b", h=HEADS),
               PS[:, 7, :].rearrange("p (h b) -> p h b", h=HEADS)[:, :, 0:DEC])
        for c in range(2):
            copied("h_v", c, v_tok[:, c, :], PS[:, 4 + c, :])
        copied("f_tok", 0, q8[:, :], PS[0:DEC, 7, :], "f_qtok")
        for n in range(NL + 2):
            if n < NL:
                act.wait_ge(*told("d_dif", n + 1))
                d = dif[:, n % 2, :, :]
                steps.then(A_(d, d, ACT.Abs))
                steps.then(A_(d, d, ACT.Exp, scale=-1.0))
                tell(act, "a_decay", 1)
            elif n == NL:
                act.wait_ge(*told("d_dif", NL + 1))
                steps.then(A_(dif[:, NL % 2, :, :], bc[:, :, :], ACT.Exp))
                tell(act, "a_decay", 1)
            else:
                act.wait_ge(*told("d_dif", NL + 2))
                d = dif[:, (NL + 1) % 2, :, :]
                steps.then(A_(d, d, ACT.Exp))
                tell(act, "a_decay", 1)
            weights(min(H_AT + H_GAP * n + 3, 80))
        copied("h_kd", 0, ke[:, :, :].rearrange("p (a b) c -> p a (b c)", a=2), PS[:, 4:6, :], "h_kdt")
        weights(82)
        copied("h_s", 0, s_prev[:, 0, :, :].rearrange("p h v -> p (h v)"), PS[:, 6, :], "h_s0")
        weights(83)
        act.wait_ge(*made("h_o", 1))
        for pair in range(2):
            steps.do(A_(hf[:, 2 * pair:2 * pair + 2, 0:SEQ], PS[:, 4 + pair, :].rearrange("p (h t) -> p h t", h=2), ACT.Copy))
        steps.tell("empty_" + "h_o")
        weights(84)
        steps.then(A_(hf[:, :, SEQ:TOK], hos[:, :].rearrange("p (h b) -> p h b", h=HEADS), ACT.Copy))
        steps.then(A_(lnt[:, :, :], hf[:, :, :], ACT.Square))
        tell(act, "h_sq", 1)
        weights(85)
        act.wait_ge(*told("h_var", 1))
        steps.then(A_(lnt[:, :, :], lnt[:, :, :], ACT.Sqrt))
        tell(act, "h_rstd", 1)
        weights(86)
        act.wait_ge(*told("h_out", 1))
        steps.then(A_(bh2[:, :, :], hf[:, :, :], ACT.Copy))
        tell(act, "bh2_done", 1)
        weights(93)
        act.wait_ge(*told("g_cent", 1))
        steps.then(A_(gsq[:, :, :], gv[:, :, :], ACT.Square))
        tell(act, "g_sq", 1)
        weights(95)
        act.wait_ge(*told("g_rec", 1))
        steps.then(A_(gsq[:, 0, :], gsq[:, 0, :], ACT.Sqrt))
        tell(act, "g_rstd", 1)
        weights(96)
        for c in range(2):
            copied("g_tok", c, v_tok[:, c, :], PS[:, 6 + c, :])
        act.wait_ge(*told("t8_stored1", 16 * 4))
        copied("g_tok", 2, t8[:, 1, :], PS[0:DEC, 6, :], "g_tokens")
        act.dma_start(O["gmlp_v_sample"][0].rearrange("b o c -> (b o) c"), t8[:, 1, :]).then_inc(sem("t8_stored1"), 16)
        weights(99)
        act.wait_ge(*told("g_mixed", 1))
        steps.then(A_(bh3[:, :, :], gu[:, :, :], ACT.Copy))
        tell(act, "bh3_done", 1)
        projected(act, "ff")
        ab = cum[:, :, :].rearrange("h a t -> h (a t)")[:, 0:TOK]
        steps.then(A_(ab, lf_t[:, :], ACT.Abs, bias=bf[:, 0:1]))
        steps.then(A_(ab, ab, ACT.Exp, scale=-1.0))
        steps.then(A_(ab, ab, ACT.Ln, bias=1.0))
        tell(act, "a_lf", 1)
        act.wait_ge(*made("f_lf", 1))
        steps.do(A_(small[:, 40:48], PS[:, 6, 0:8], ACT.Copy))
        steps.then(A_(small[0:DEC, 48:52], PS[0:DEC, 6, 8:12], ACT.Copy))
        tell(act, "empty_" + "f_lf", 1)
        act.dma_start(O["fox_logf_prompt"][0, 0].rearrange("(n p) h -> p n h", p=P),
                      small[:, 40:48].rearrange("p (n h) -> p n h", n=2)).then_inc(sem("fox_stored"), 16)
        act.dma_start(O["fox_logf_sample"][0].rearrange("b o h -> (b o) h"), small[0:DEC, 48:52]).then_inc(sem("fox_stored"), 16)
        weights(102)
        act.wait_ge(*told("f_max", 1))
        steps.do(A_(ps_row[:, :].rearrange("r (a c) -> r a c", a=2), PS[0:32, 6:8, :], ACT.Exp, bias=small[0:32, 56:57],
                    accum_out=small[0:32, 57:58]))
        steps.then(A_(small[0:32, 58:59], small[0:32, 54:55], ACT.Exp, bias=small[0:32, 55:56]))
        tell(act, "empty_" + "f_sct", 1)
        tell(act, "f_exp", 1)
        weights(103)
        copied("f_pt", 0, ptt[:, :, :].rearrange("p a b -> p (a b)"), PS[:, 4, 0:256], "f_ptt")
        act.wait_ge(*told("f_tok_free", 1))
        for n in range(1, 7):
            name, c = ("fox_k", "fox_v")[(n - 1) // 3], (n - 1) % 3
            buf = (k_tok, v_tok)[(n - 1) // 3]
            bank = 4 + n % 2
            if c < 2:
                copied("f_tok", n, buf[:, c, :], PS[:, bank, :], "f_vtok" if n == 5 else None)
                out = O[name + "_prompt"][0, 0].rearrange("(n p) h d -> n p (h d)", p=P)[c]
                act.dma_start(out, buf[:, c, :]).then_inc(sem("fox_stored"), 16)
            else:
                act.wait_ge(*told("t8_stored1", 16 * (5 if n == 3 else 6)))
                copied("f_tok", n, t8[:, 1, :], PS[0:DEC, bank, :])
                act.dma_start(O[name + "_sample"][0].rearrange("b o h d -> (b o) (h d)"),
                              t8[:, 1, :]).then_inc(sem("t8_stored1"), 16)
        for i in range(2):
            weights(107 + 16 * i)
            act.wait_ge(*told("f_pmax", i + 1))
            keys = (i + 1) * P
            for h in range(HEADS):
                steps.do(A_(s_sb[:, h, 0:keys], s_sb[:, h, 0:keys], ACT.Exp, scale=SCALE, bias=small[:, 4 + h:5 + h],
                            accum_out=small[:, h:h + 1]))
            steps.tell("f_pexp")
            weights(111 + 16 * i)
            act.wait_ge(*made("f_p", i + 1))
            pb = banks("f_p", i)
            for kb in range(i + 1):
                steps.do(A_(pt_sb[:, kb, :, :].rearrange("p h t -> p (h t)"), PS[:, pb[kb], :], ACT.Copy))
            steps.settle()
            tell(act, "empty_" + "f_p", 1)
            tell(act, "f_pt_sb", 1)
        weights(136)
        act.wait_ge(*told("glu_done", 1))
        steps.then(A_(gh1[:, :, :], su[:, :, :], ACT.Copy))
        tell(act, "gh_done", 1)
        weights(150)
        copied("f_os", 0, t8[:, 0, :], PS[0:DEC, 6, :], "f_ostok")
        weights(154)
        act.wait_ge(*told("f_out", 1))
        steps.then(A_(bh0[:, :, :], fq[:, :, :], ACT.Copy))
        tell(act, "bh0_done", 1)

        def merged(dg):
            act.wait_ge(*told("sums", dg + 1))
            A_(mh[:, 4 * dg:4 * dg + 4, :], gates[:, (dg % 2) * 16:(dg % 2) * 16 + 4, :], ACT.Copy).then_inc(sem("mh_done"), 1)

        def highs(n0, n1):
            for n in range(n0, n1):
                high(n)

        def loop_highs(c0, i, per, j0, j1):
            for j in range(j0, j1):
                n = c0 + j
                split(None, n % RING, i * (4 * per) + 16 * (n // RING + 1), i * per + (n - RING + 1))

        highs(154, C_MERGE[1] + 6)
        merged(0)
        highs(C_MERGE[1] + 6, C_GATE[2])
        for dg in (2, 3):
            c0, p0 = C_GATE[dg], P_GATE[dg]

            def gate_pass(i, m):
                p = p0 + m
                act.wait_ge(*told("used", i * 8 + (c0 + 4 * m + 4)))
                dst = gates[:, ds(i * 4 + ((dg % 2) * 16 + 2 * m), 2), :]
                A_(dst, PS[:, BANK(p):BANK(p) + 2, 0:TOK], ACT.Sigmoid).then_inc(sem(f"evac{p % 2}"), 1)

            highs(c0, c0 + 4)
            merged(dg - 1)
            highs(c0 + 4, c0 + 8)
            act.wait_ge(*told("ml_done", dg - 1))
            act.wait_ge(*told("used", c0 + 4))
            A_(gates[:, (dg % 2) * 16:(dg % 2) * 16 + 2, :], PS[:, BANK(p0):BANK(p0) + 2, 0:TOK],
               ACT.Sigmoid).then_inc(sem(f"evac{p0 % 2}"), 1)
            with nc.scalar.Fori(1, 4) as i:
                loop_highs(c0, i, 8, 0, 4)
                gate_pass(i - 1, 1)
                loop_highs(c0, i, 8, 4, 8)
                gate_pass(i, 0)
            highs(C_MERGE[dg], C_MERGE[dg] + 4)
            act.wait_ge(*told("used", C_MERGE[dg]))
            A_(gates[:, (dg % 2) * 16 + 14:(dg % 2) * 16 + 16, :], PS[:, BANK(p0 + 7):BANK(p0 + 7) + 2, 0:TOK],
               ACT.Sigmoid).then_inc(sem(f"evac{(p0 + 7) % 2}"), 1)
            highs(C_MERGE[dg] + 4, C_MERGE[dg] + 8)
        highs(C_OUT, C_OUT + 4)
        merged(3)
        highs(C_OUT + 4, C_OUT + 8)
        with nc.scalar.Fori(1, 4) as i:
            loop_highs(C_OUT, i, 8, 0, 8)
        highs(C_UP, C_UP + 4)

        def squares(n, src, dst):
            for t4 in range(4):
                act.wait_ge(*told(f"centred{n}", t4 + 1))
                A_(dst[:, 4 * t4:4 * t4 + 4, :], src[:, 4 * t4:4 * t4 + 4, :], ACT.Square).then_inc(sem(f"sq{n}"), 1)
            act.wait_ge(*told(f"var{n}", 1))
            A_(mu_r[:, 1, :], mu_r[:, 1, :], ACT.Sqrt).then_inc(sem(f"rstd{n}"), 1)

        squares(0, xp, sq)
        for t4 in range(4):
            act.wait_ge(*told("x1_f32", t4 + 1))
            A_(xh[:, 4 * t4:4 * t4 + 4, :], xp[:, 4 * t4:4 * t4 + 4, :], ACT.Copy).then_inc(sem("x1_hi"), 1)

        bank_g, bank_u = BANK(P_UP), BANK(P_UP + 1)

        def silu(i):
            act.wait_ge(*told("used", i * 8 + (C_UP + 4)))
            A_(sg[:, :, :], PS[:, bank_g:bank_g + 2, 0:TOK], ACT.Silu).then_inc(sem(f"evac{P_UP % 2}"), 1)

        def h_high(i):
            act.wait_ge(sem(f"evac{(P_UP + 1) % 2}"), i + ((P_UP + 1) // 2 + 1))
            A_(hh[:, ds(i * 2, 2), :], hx[:, :, :], ACT.Copy).then_inc(sem("hh_done"), 1)

        highs(C_UP + 4, C_UP + 8)
        silu(0)
        with nc.scalar.Fori(1, UP_STEPS) as i:
            loop_highs(C_UP, i, 8, 0, 6)
            h_high(i - 1)
            loop_highs(C_UP, i, 8, 6, 8)
            silu(i)
        highs(C_DOWN, C_DOWN + 4)
        act.wait_ge(sem(f"evac{(P_UP + 1) % 2}"), (UP_STEPS - 1) + ((P_UP + 1) // 2 + 1))
        A_(hh[:, 2 * UP_STEPS - 2:2 * UP_STEPS, :], hx[:, :, :], ACT.Copy).then_inc(sem("hh_done"), 1)
        highs(C_DOWN + 4, C_DOWN + 44)
        with nc.scalar.Fori(1, 2) as i:
            loop_highs(C_DOWN, i, 44, 0, 44)
        squares(1, yp, sq2)
        for n in range(12):
            act.wait_ge(*made("y", n + 1))
            t4, c = n // 3, n % 3
            dst = y_tok[:, c, t4 * 512:(t4 + 1) * 512] if c < 2 else ys_tok[:, t4 * 512:(t4 + 1) * 512]
            src = PS[:, 4 + n % 4, :] if c < 2 else PS[0:DEC, 4 + n % 4, :]
            steps.then(A_(dst, src, ACT.Copy))
            tell(act, "empty_" + "y", 1)
            tell(act, "y_copied", 1)
        act.wait_ge(*told("so_stored", 32))
        act.wait_ge(*told("t8_stored0", 16 * 4))
        act.wait_ge(*told("t8_stored1", 16 * 7))
        act.wait_ge(*told("fox_stored", 16 * 6))

    @block.vector
    def _(dve):
        V = nc.vector
        steps = Steps(dve, sem("dve_steps"), tell)
        do, then = steps.do, steps.then

        for k in range(KT):
            dve.wait_ge(*told("xh_done", k + 1))
            V.tensor_tensor(xl[:, k, :], PS[:, 4 + k % 4, 0:TOK], xh[:, k, :], ALU.subtract).then_inc(sem("x_split"), 1)
            dve.wait_ge(*told("x_split", k + 1))
            tell(dve, "empty_" + "x", 1)

        S = lambda n: sp[:, n, :]
        dve.wait_ge(*told("a_dt", 1))
        step = dt2[:, :].unsqueeze(2).to_broadcast([S5_TILES, 2, 64])
        g2 = lambda n: sp[:, n, :].rearrange("i (g p) -> i g p", g=2)
        do(V.tensor_tensor(g2(8), g2(0), step, ALU.mult))
        steps.tell("d_lrdt")
        then(V.tensor_tensor(g2(3), g2(1), step, ALU.mult))
        then(V.tensor_scalar(S(3), S(3), 1.0 / (2 * math.pi), None, ALU.mult))
        then(V.tensor_scalar(S(11), S(3), ROUND, ROUND, ALU.add, ALU.subtract))
        then(V.tensor_tensor(S(3), S(3), S(11), ALU.subtract))
        dve.wait_ge(*told("a_mag", 1))
        tell(dve, "d_turns", 1)
        do(V.tensor_tensor(S(12), S(0), S(0), ALU.mult))
        then(V.tensor_tensor(S(13), S(1), S(1), ALU.mult))
        then(V.tensor_tensor(S(12), S(12), S(13), ALU.add))
        do(V.reciprocal(S(12), S(12)))
        dve.wait_ge(*told("a_sin", 1))
        then(V.tensor_tensor(S(9), S(9), S(9), ALU.mult))
        then(V.tensor_scalar(S(9), S(9), -2.0, 1.0, ALU.mult, ALU.add))
        do(V.tensor_tensor(S(4), S(2), S(9), ALU.mult))
        then(V.tensor_tensor(S(5), S(2), S(10), ALU.mult))
        then(V.tensor_scalar(S(9), S(4), 1.0, None, ALU.subtract))
        do(V.tensor_tensor(S(13), S(9), S(0), ALU.mult))
        do(V.tensor_tensor(S(14), S(5), S(1), ALU.mult))
        do(V.tensor_tensor(S(15), S(5), S(0), ALU.mult))
        then(V.tensor_tensor(S(11), S(9), S(1), ALU.mult))
        do(V.tensor_tensor(S(13), S(13), S(14), ALU.add))
        then(V.tensor_tensor(S(15), S(15), S(11), ALU.subtract))
        do(V.tensor_tensor(S(6), S(13), S(12), ALU.mult))
        do(V.tensor_tensor(S(7), S(15), S(12), ALU.mult))
        steps.tell("s5_par")
        dve.wait_ge(*told("consts_ready", 1))
        parity = small[:, 1:2].bitcast(I32)
        then(V.tensor_scalar(parity, small[:, 0:1].bitcast(I32), 4, 1, ALU.arith_shift_right, ALU.bitwise_and))
        then(V.tensor_copy(par[:, 1:2], parity))
        then(V.tensor_scalar(par[:, 0:1], par[:, 1:2], -1.0, 1.0, ALU.mult, ALU.add))
        dve.wait_ge(*told("s5_loaded", 16 * 9))
        for r in range(2):
            for g in range(2):
                do(V.tensor_scalar(cd[:, r, :, g, :], cn[:, r, :, :], par[:, g:g + 1], (1.0, -1.0)[r], ALU.mult, ALU.mult))
        steps.tell("s5_cd")
        t_s, s_s = level_mask[:, 0, :], level_mask[:, 1, :]
        then(V.tensor_tensor(level_mask[:, 2, :], t_s, s_s, ALU.bitwise_xor))
        then(V.tensor_tensor(level_mask[:, 3, :], t_s, s_s, ALU.is_gt))
        then(V.tensor_tensor(level_mask[:, NL, :], level_mask[:, 2, :], level_mask[:, 3, :], ALU.mult))
        for n, b in enumerate(HGRN_LEVELS):
            do(V.tensor_scalar(level_mask[:, n, :], level_mask[:, NL, :], b, None, ALU.is_ge))
        steps.settle()
        for n in range(NL - 1, 0, -1):
            then(V.tensor_tensor(level_mask[:, n, :], level_mask[:, n, :], level_mask[:, n - 1, :], ALU.subtract))
        then(V.tensor_copy(level_mask[:, NL, :], ident[:, :]))
        dve.wait_ge(*told("lam_ready", 1))
        co = [lam_t[:, 4 + r, :].unsqueeze(2).to_broadcast([P, S5_TILES, 16]) for r in range(2)]
        t1 = tab[:, 0, :].rearrange("p (i h) -> p i h", h=16)
        t2 = tab[:, 1, :].rearrange("p (i h) -> p i h", h=16)
        for r in range(2):
            do(V.tensor_tensor(t1, bn[:, r, :, :], co[0], ALU.mult))
            then(V.tensor_tensor(t2, bn[:, 1 - r, :, :], co[1], ALU.mult))
            for g in range(2):
                half = slice(64 * g, 64 * g + 64)
                do(V.tensor_tensor(bd[half, r, :, g, :], t1[half], t2[half], (ALU.subtract, ALU.add)[r]))
            steps.settle()
        tell(dve, "s5_bd", 1)

        def s5_angle(b):
            if b:
                dve.wait_ge(*told("a_table", b))
            turns = lam_t[:, 1, 2 * b:2 * b + 2].unsqueeze(2).to_broadcast([P, 2, SEQ])
            then(V.tensor_tensor(tab[:, :, :], iota_t[:, :].unsqueeze(1).to_broadcast([P, 2, SEQ]), turns, ALU.mult))
            then(V.tensor_scalar(rnd[:, :, :], tab[:, :, :], ROUND, ROUND, ALU.add, ALU.subtract))
            then(V.tensor_tensor(tab[:, :, :], tab[:, :, :], rnd[:, :, :], ALU.subtract))
            tell(dve, "d_angle", 1)

        s5_angle(0)
        s5_angle(1)
        dve.wait_ge(*told("bus_ready", 1))
        dve.wait_ge(*told("h0_ready", 1))
        ab = [lam_t[:, 2 + r, :].unsqueeze(2).to_broadcast([P, S5_TILES, DEC]) for r in range(2)]
        t1 = gr[:, 0, 0:P].rearrange("p (i b) -> p i b", b=DEC)
        t2 = gr[:, 0, P:2 * P].rearrange("p (i b) -> p i b", b=DEC)
        for r in range(2):
            do(V.tensor_tensor(t1, h0[:, r, :, :], ab[0], ALU.mult))
            then(V.tensor_tensor(t2, h0[:, 1 - r, :, :], ab[1], ALU.mult))
            then(V.tensor_tensor(t1, t1, t2, (ALU.subtract, ALU.add)[r]))
            then(V.tensor_tensor(hs[:, r, :, :], t1, bus[:, r, :, :], ALU.add))
        tell(dve, "s5_hs", 1)
        dve.wait_ge(*told("vecs_ready", 1))
        projected(dve, "su")
        def h_samples():
            dve.wait_ge(*told("s_smp", 16 * DEC))
            dve.wait_ge(*told("a_smp", 1))
            projected(dve, "hq")
            do(V.tensor_tensor(qm[:, :, :, :], hq[:, :, SEQ:TOK].unsqueeze(3).to_broadcast([P, HEADS, DEC, DEC]),
                               eye8[:, :, :].unsqueeze(1).to_broadcast([P, HEADS, DEC, DEC]), ALU.mult))
            states = s_smp[:, :, :].rearrange("p (b h) v -> p b h v", h=HEADS)
            for h in range(HEADS):
                do(V.tensor_tensor(states[:, :, h, :], states[:, :, h, :],
                                   small[:, 8 + 8 * h:16 + 8 * h].unsqueeze(2).to_broadcast([P, DEC, P]), ALU.mult))
            steps.settle()
            for b in range(DEC):
                dve.wait_ge(*made("h_vb", b + 1))
                for h in range(HEADS):
                    do(V.scalar_tensor_tensor(s_smp[:, 4 * b + h, :], PS[:, 4 + b % 2, h * P:h * P + P],
                                              kt_[:, h, SEQ + b:SEQ + b + 1], s_smp[:, 4 * b + h, :], ALU.mult, ALU.add))
                steps.settle()
                tell(dve, "empty_" + "h_vb", 1)
            tell(dve, "h_smp_done", 2)

        for b in range(8):
            dve.wait_ge(*told("a_table", b + 1))
            c_, s_ = er[:, b % 2, :, :], ei[:, b % 2, :, :]
            then(V.tensor_scalar(c_, c_, -2.0, 1.0, ALU.mult, ALU.add))
            dve.wait_ge(*made("s5_bu", b + 1))
            br, bi = PS[:, 4:6, 0:SEQ], PS[:, 4:6, SEQ:2 * SEQ]
            if b:
                dve.wait_ge(*made("s5_y", b))
            t1, t2 = rnd[:, :, :], hm[:, :, :]
            do(V.tensor_tensor(gr[:, :, :], c_, br, ALU.mult))
            do(V.tensor_tensor(t1, s_, bi, ALU.mult))
            do(V.tensor_tensor(gi[:, :, :], c_, bi, ALU.mult))
            then(V.tensor_tensor(t2, s_, br, ALU.mult))
            tell(dve, "empty_" + "s5_bu", 1)
            do(V.tensor_tensor(gr[:, :, :], gr[:, :, :], t1, ALU.add))
            then(V.tensor_tensor(gi[:, :, :], gi[:, :, :], t2, ALU.subtract))
            for t in range(2):
                mag = lam_t[:, 0, 2 * b + t:2 * b + t + 1].to_broadcast([P, SEQ])
                do(V.tensor_tensor_scan(gr[:, t, :], mag, gr[:, t, :], 0.0, ALU.mult, ALU.add))
                do(V.tensor_tensor_scan(gi[:, t, :], mag, gi[:, t, :], 0.0, ALU.mult, ALU.add))
            steps.settle()
            do(V.tensor_tensor(hr[:, :, :], c_, gr[:, :, :], ALU.mult))
            do(V.tensor_tensor(t1, s_, gi[:, :, :], ALU.mult))
            do(V.tensor_tensor(gi[:, :, :], c_, gi[:, :, :], ALU.mult))
            then(V.tensor_tensor(gr[:, :, :], s_, gr[:, :, :], ALU.mult))
            do(V.tensor_tensor(hr[:, :, :], hr[:, :, :], t1, ALU.subtract))
            then(V.tensor_tensor(hm[:, :, :], gi[:, :, :], gr[:, :, :], ALU.add))
            tell(dve, "s5_h", 1)
            do(V.tensor_copy(sf[:, 0, 2 * b:2 * b + 2], hr[:, :, SEQ - 1]))
            do(V.tensor_copy(sf[:, 1, 2 * b:2 * b + 2], hm[:, :, SEQ - 1]))
            if b + 2 < 8:
                s5_angle(b + 2)
            if b == H_SMP:
                h_samples()
            if b % 2 == 1:
                q = b // 2
                if b == 7:
                    steps.tell("s5_sf")
                dve.wait_ge(*made("s5_y", b + 1))
                then(V.scalar_tensor_tensor(su[:, q, :], su[:, q, :], vecs[:, 0, q:q + 1], PS[:, 6 + q % 2, 0:TOK],
                                            ALU.mult, ALU.add))
                tell(dve, "empty_" + "s5_y", 2)
        tell(dve, "s5_yd", 1)
        dve.wait_ge(*told("gh_done", 1))
        then(V.tensor_tensor(gl1[:, :, :], su[:, :, :], gh1[:, :, :], ALU.subtract))
        tell(dve, "g_split", 1)

        dve.wait_ge(*told("a_ln", 1))
        do(V.tensor_scalar(hf[:, :, :], hf[:, :, :], 0.0, None, ALU.min))
        steps.settle()
        then(V.tensor_tensor(hf[:, :, :], hf[:, :, :], lnt[:, :, :], ALU.subtract))
        tell(dve, "d_lf", 1)
        for hc in range(8):
            h, c = hc // 2, hc % 2
            do(V.tensor_tensor_scan(bc[:, hc, :], ones[:, :], hf[:, h, c * P:c * P + P], 0.0, ALU.mult, ALU.add))
        then(V.memset(att[:, :, :], 0.0))
        projected(dve, "hq")
        heads = lambda t: t.rearrange("p (h c) s -> p h (c s)", h=HEADS)

        def h_dif(n):
            if n < NL:
                b = HGRN_LEVELS[n]
                v = bc[:, :, :].rearrange("p a (m c) -> p (a m) c", c=2 * b)
                d = dif[:, n % 2, :, :].rearrange("p a (m c) -> p (a m) c", c=2 * b)
                then(V.tensor_tensor(d, v, v[:, :, b - 1:b].to_broadcast([P, 8 * P // (2 * b), 2 * b]), ALU.subtract))
            elif n == NL + 1:
                then(V.tensor_tensor(dif[:, n % 2, :, :], bc[:, :, P - 1:P].to_broadcast([P, 8, P]), bc[:, :, :], ALU.subtract))
            tell(dve, "d_dif", 1)

        def keys_half(n):
            b = n // 2
            if n % 2 == 0:
                dve.wait_ge(*made("f_qb", b + 1))
            dve.wait_ge(sem(f"kv{n % 2}"), 64 * (n // 2 + 1))
            half = kv[:, n % 2, :, :]
            then(V.tensor_tensor(half, half, PS[:, 6 + b % 2, :].unsqueeze(1).to_broadcast([P, 4, MIX]), ALU.mult))
            if n % 2 == 1:
                tell(dve, "empty_" + "f_qb", 1)
            then(V.tensor_reduce(sc[:, 4 * (n % 2):4 * (n % 2) + 4, 4 * b:4 * b + 4],
                                 half.rearrange("p j (h d) -> p j h d", h=HEADS), AX.X, ALU.add))
            tell(dve, "kv_free", 1)

        h_dif(0)
        h_dif(1)
        for n in range(NL):
            dve.wait_ge(*told("a_decay", n + 1))
            if n:
                dve.wait_ge(*made("h_att", n))
            d = heads(dif[:, n % 2, :, :])
            do(V.tensor_tensor(heads(qe[:, :, :]), d, hq[:, :, 0:SEQ], ALU.mult))
            then(V.tensor_tensor(heads(ke[:, :, :]), d, kt_[:, :, 0:SEQ], ALU.mult))
            tell(dve, "h_qe", 1)
            h_dif(n + 2)
            if n == 0:
                dve.wait_ge(sem("so_stored"), 32)
            keys_half(2 * n)
            dve.wait_ge(*made("h_att", n + 1))
            bank = banks("h_att", n)[0]
            for part in range(2):
                mask = level_mask[:, n, :].unsqueeze(1).to_broadcast([P, 4, P])
                data = PS[:, bank + part, :].rearrange("p (a t) -> p a t", a=4)
                do(V.copy_predicated(att[:, 4 * part:4 * part + 4, :], mask, data))
            steps.settle()
            tell(dve, "empty_" + "h_att", 1)
            keys_half(2 * n + 1)
        dve.wait_ge(*told("a_decay", NL + 1))
        eb = dif[:, NL % 2, :, :]
        do(V.tensor_tensor(qb_h[:, :, :], eb.rearrange("p (h c) s -> p h c s", h=HEADS)[:, :, 1, :], hq[:, :, P:SEQ], ALU.mult))
        do(V.tensor_copy(small[:, 2:6], eb.rearrange("p (h c) s -> p h c s", h=HEADS)[:, :, 1, P - 1]))
        dve.wait_ge(*made("h_att", NL + 1))
        bank = banks("h_att", NL)[0]
        for part in range(2):
            mask = level_mask[:, NL, :].unsqueeze(1).to_broadcast([P, 4, P])
            do(V.copy_predicated(att[:, 4 * part:4 * part + 4, :], mask, PS[:, bank + part, :].rearrange("p (a t) -> p a t", a=4)))
        steps.settle()
        tell(dve, "empty_" + "h_att", 1)
        tell(dve, "h_att_done", 1)
        dve.wait_ge(*told("a_decay", NL + 2))
        then(V.tensor_tensor(heads(qe[:, :, :]), heads(dif[:, (NL + 1) % 2, :, :]), kt_[:, :, 0:SEQ], ALU.mult))
        tell(dve, "h_kd", 1)
        keys_half(14)
        keys_half(15)
        dve.wait_ge(*told("h_s0", 1))
        dve.wait_ge(*made("h_last", 1))
        for h in range(HEADS):
            do(V.scalar_tensor_tensor(s_prev[:, 1, h, :], s_prev[:, 0, h, :], small[:, 2 + h:3 + h],
                                      PS[:, 7, h * P:h * P + P], ALU.mult, ALU.add))
        steps.settle()
        tell(dve, "empty_" + "h_last", 1)
        dve.wait_ge(*made("h_ms", 1))
        then(V.tensor_scalar(lnt[:, :, :], PS[:, 4:8, 0:TOK], 1.0 / P, RMS_EPS, ALU.mult, ALU.add))
        tell(dve, "empty_" + "h_ms", 1)
        then(V.reciprocal(lnt[:, :, :], lnt[:, :, :]))
        tell(dve, "h_var", 1)
        projected(dve, "hg")
        dve.wait_ge(*told("h_rstd", 1))
        then(V.tensor_tensor(hf[:, :, :], hf[:, :, :], lnt[:, :, :], ALU.mult))
        then(V.tensor_tensor(hf[:, :, :], hf[:, :, :], vecs[:, 2, :].unsqueeze(2).to_broadcast([P, MT, TOK]), ALU.mult))
        then(V.tensor_tensor(hf[:, :, :], hf[:, :, :], hg[:, :, :], ALU.mult))
        tell(dve, "h_out", 1)
        dve.wait_ge(*told("bh2_done", 1))
        then(V.tensor_tensor(bl2[:, :, :], hf[:, :, :], bh2[:, :, :], ALU.subtract))
        tell(dve, "branch2", 1)
        tell(dve, "h_done", 2)

        projected(dve, "gv")
        projected(dve, "gu")
        dve.wait_ge(*made("g_mu", 1))
        then(V.tensor_scalar(gsq[:, 0, :], PS[:, 4, 0:TOK], 1.0 / MIX, None, ALU.mult))
        tell(dve, "empty_" + "g_mu", 1)
        then(V.tensor_tensor(gv[:, :, :], gv[:, :, :], gsq[:, 0:1, :].to_broadcast([P, MT, TOK]), ALU.subtract))
        tell(dve, "g_cent", 1)
        dve.wait_ge(*made("g_var", 1))
        then(V.tensor_scalar(gsq[:, 0, :], PS[:, 5, 0:TOK], 1.0 / MIX, LN_EPS, ALU.mult, ALU.add))
        tell(dve, "empty_" + "g_var", 1)
        then(V.reciprocal(gsq[:, 0, :], gsq[:, 0, :]))
        tell(dve, "g_rec", 1)
        dve.wait_ge(*told("g_rstd", 1))
        then(V.tensor_tensor(gv[:, :, :], gv[:, :, :], gsq[:, 0:1, :].to_broadcast([P, MT, TOK]), ALU.mult))
        for t in range(MT):
            do(V.tensor_scalar(gv[:, t, :], gv[:, t, :], vecs[:, 3, t:t + 1], vecs[:, 4, t:t + 1], ALU.mult, ALU.add))
        steps.tell("g_vn")
        for n in range(2):
            dve.wait_ge(*made("g_mix", n + 1))
            then(V.tensor_tensor(gu[:, :, n * P:n * P + P], gu[:, :, n * P:n * P + P],
                                 PS[:, 4 + n, :].rearrange("p (g t) -> p g t", g=MT), ALU.mult))
            tell(dve, "empty_" + "g_mix", 1)
        dve.wait_ge(*made("g_ms", 1))
        t1 = gsq[:, 1, 0:32].rearrange("p (g b) -> p g b", g=MT)
        then(V.tensor_tensor(t1, gv[:, :, SEQ:TOK], PS[:, 6, 0:MT].unsqueeze(2).to_broadcast([P, MT, DEC]), ALU.mult))
        then(V.tensor_tensor(t1, t1, PS[:, 6, MT:2 * MT].unsqueeze(2).to_broadcast([P, MT, DEC]), ALU.add))
        tell(dve, "empty_" + "g_ms", 1)
        then(V.tensor_tensor(gu[:, :, SEQ:TOK], gu[:, :, SEQ:TOK], t1, ALU.mult))
        tell(dve, "g_mixed", 1)
        dve.wait_ge(*told("bh3_done", 1))
        then(V.tensor_tensor(bl3[:, :, :], gu[:, :, :], bh3[:, :, :], ALU.subtract))
        tell(dve, "branch3", 1)
        tell(dve, "g_done", 1)

        dve.wait_ge(*told("a_lf", 1))
        ab = cum[:, :, :].rearrange("h a t -> h (a t)")[:, 0:TOK]
        then(V.tensor_scalar(lf_t[:, :], lf_t[:, :], bf[:, 0:1], 0.0, ALU.add, ALU.min))
        then(V.tensor_tensor(lf_t[:, :], lf_t[:, :], ab, ALU.subtract))
        tell(dve, "f_lf", 1)
        dve.wait_ge(*told("lfp", 16))
        for h in range(HEADS):
            do(V.tensor_tensor_scan(rc[:, ::-1, h], ones[0:64, :], lfp[:, ::-1, h], 0.0, ALU.mult, ALU.add))
        steps.tell("f_rc")
        dve.wait_ge(*made("f_suf", 1))
        then(V.tensor_tensor(rc[:, :, :], rc[:, :, :], lfp[:, :, :], ALU.subtract))
        then(V.tensor_tensor(rc[:, :, :], rc[:, :, :], PS[0:64, 7, 0:HEADS].unsqueeze(1).to_broadcast([64, PAGE, HEADS]), ALU.add))
        tell(dve, "empty_" + "f_suf", 1)
        tell(dve, "f_suf_in", 1)
        projected(dve, "fq")
        projected(dve, "fk")
        do(V.tensor_tensor(small[:, 8:40].rearrange("p (b h) -> p h b", h=HEADS), fq[:, :, SEQ:TOK], fk[:, :, SEQ:TOK], ALU.mult))
        do(V.tensor_tensor(cum[:, 1, 0:32].rearrange("k (b h) -> k b h", h=HEADS),
                           lf_t[:, SEQ:TOK].unsqueeze(2).to_broadcast([HEADS, DEC, HEADS]),
                           ident[0:HEADS, 0:HEADS].unsqueeze(1).to_broadcast([HEADS, DEC, HEADS]), ALU.mult))
        steps.tell("f_qk")
        then(V.tensor_scalar(sc[:, :, :], sc[:, :, :], SCALE, None, ALU.mult))
        dve.wait_ge(*made("f_suft", 1))
        for h in range(HEADS):
            do(V.tensor_tensor(sc[:, :, h::HEADS], sc[:, :, h::HEADS],
                               PS[:, 6, h * 64:h * 64 + 64].rearrange("p (b g) -> p g b", g=N_PAGES), ALU.add))
        steps.settle()
        tell(dve, "empty_" + "f_suft", 1)
        tell(dve, "f_sc", 1)
        col = lambda n: small[0:32, n:n + 1]
        dve.wait_ge(*made("f_new", 1))
        do(V.tensor_scalar(col(54), PS[0:32, 5, 0:1], SCALE, None, ALU.mult))
        then(V.tensor_copy(col(53), PS[0:32, 5, 1:2]))
        tell(dve, "empty_" + "f_new", 1)
        dve.wait_ge(*made("f_sct", 1))
        then(V.tensor_reduce(col(60), PS[0:32, 6:8, :], AX.XY, ALU.max))
        then(V.tensor_tensor(col(60), col(60), col(53), ALU.add))
        then(V.tensor_tensor(col(60), col(60), col(54), ALU.max))
        do(V.tensor_tensor(col(56), col(53), col(60), ALU.subtract))
        then(V.tensor_scalar(col(55), col(60), -1.0, None, ALU.mult))
        tell(dve, "f_max", 1)
        dve.wait_ge(*told("f_exp", 1))
        then(V.tensor_tensor(col(60), col(57), col(58), ALU.add))
        then(V.reciprocal(col(60), col(60)))
        do(V.tensor_scalar(ps_row[:, :], ps_row[:, :], col(60), None, ALU.mult))
        then(V.tensor_tensor(col(58), col(58), col(60), ALU.mult))
        then(V.tensor_scalar(small[0:32, 0:32], ident[0:32, 0:32], col(58), None, ALU.mult))
        tell(dve, "f_prob", 1)
        tell(dve, "f_tok_free", 1)
        projected(dve, "fv")
        dve.wait_ge(*made("f_pn", 1))
        new = osmp[:, :].rearrange("p (h b) -> p h b", h=HEADS)
        dve.wait_ge(*made("f_pt", 1))
        then(V.tensor_tensor(new, fv[:, :, SEQ:TOK], PS[:, 5, 0:32].rearrange("p (b h) -> p h b", h=HEADS), ALU.mult))
        tell(dve, "empty_" + "f_pn", 1)
        then(V.tensor_tensor_scan(cum[:, 0, :], ones[0:HEADS, 0:1].to_broadcast([HEADS, SEQ]),
                                  lf_t[:, 0:SEQ], 0.0, ALU.mult, ALU.add))
        do(V.tensor_scalar(cum[:, 1, :], cum[:, 0, :], -1.0 / SCALE, None, ALU.mult))
        steps.settle()
        then(V.tensor_scalar(cum[:, 0, :], cum[:, 0, :], 1.0 / SCALE, None, ALU.mult))
        tell(dve, "f_cum", 1)

        def values_half(n):
            b, half = n // 2, n % 2
            if n == 0:
                dve.wait_ge(*told("f_ptt", 1))
            dve.wait_ge(sem(f"kv{half}"), 64 * (8 + b + 1))
            v = kv[:, half, :, :]
            w = ptt[:, 4 * half:4 * half + 4, 4 * b:4 * b + 4].unsqueeze(3).to_broadcast([P, 4, HEADS, P])
            vh = v.rearrange("p j (h d) -> p j h d", h=HEADS)
            then(V.tensor_tensor(vh, vh, w, ALU.mult))
            then(V.tensor_tensor(v[:, 0:2, :], v[:, 0:2, :], v[:, 2:4, :], ALU.add))
            acc = vacc[:, b % 2, :]
            if half == 0:
                if b >= 2:
                    dve.wait_ge(sem("values_used"), b - 1)
                then(V.tensor_tensor(acc, v[:, 0, :], v[:, 1, :], ALU.add))
            else:
                then(V.tensor_tensor(v[:, 0, :], v[:, 0, :], v[:, 1, :], ALU.add))
                then(V.tensor_tensor(acc, acc, v[:, 0, :], ALU.add))
            if n < 14:
                tell(dve, "kv_free", 1)
            if half:
                tell(dve, "f_vsum", 1)

        for i in range(2):
            keys = (i + 1) * P
            values_half(4 * i)
            values_half(4 * i + 1)
            dve.wait_ge(*made("f_s", i + 1))
            b0 = banks("f_s", i)[0]
            src = lambda a, c: PS[:, b0:b0 + 2, :].rearrange("p n (h k) -> p (n h) k", h=2)[:, :, a:c]
            if i:
                dve.wait_ge(*made("f_p", 1))
                do(V.tensor_copy(s_sb[:, :, 0:P], src(0, P)))
            else:
                dve.wait_ge(*made("f_pt", 1))
            then(V.tensor_tensor(s_sb[:, :, keys - P:keys], src(keys - P, keys),
                                 causal[:, :].unsqueeze(1).to_broadcast([P, HEADS, P]), ALU.add))
            tell(dve, "empty_" + "f_s", 1)
            then(V.tensor_reduce(small[:, 8:12], s_sb[:, :, 0:keys], AX.X, ALU.max))
            then(V.tensor_scalar(small[:, 4:8], small[:, 8:12], -SCALE, None, ALU.mult))
            tell(dve, "f_pmax", 1)
            values_half(4 * i + 2)
            dve.wait_ge(*told("f_pexp", i + 1))
            then(V.reciprocal(small[:, 0:4], small[:, 0:4]))
            then(V.tensor_tensor(s_sb[:, :, 0:keys], s_sb[:, :, 0:keys],
                                 small[:, 0:4].unsqueeze(2).to_broadcast([P, HEADS, keys]), ALU.mult))
            tell(dve, "f_prompt", 1)
            values_half(4 * i + 3)
            dve.wait_ge(*made("f_o", i + 1))
            then(V.tensor_copy(fq[:, :, i * P:i * P + P], PS[:, banks("f_o", i)[0], :].rearrange("p (h t) -> p h t", h=HEADS)))
            tell(dve, "empty_" + "f_o", 1)
        dve.wait_ge(*told(f"evac{P_GLU % 2}", P_GLU // 2 + 1))
        dve.wait_ge(sem(f"evac{(P_GLU + 1) % 2}"), (P_GLU + 1) // 2 + 1)
        then(V.tensor_tensor(su[:, :, :], su[:, :, :], sgl[:, :, :], ALU.mult))
        tell(dve, "glu_done", 1)
        for n in range(8, 16):
            values_half(n)
        dve.wait_ge(*told("gh_done", 2))
        then(V.tensor_tensor(gl1[:, :, :], su[:, :, :], gh1[:, :, :], ALU.subtract))
        tell(dve, "branch1", 1)
        dve.wait_ge(*made("f_ost", 1))
        then(V.tensor_tensor(fq[:, :, SEQ:TOK], PS[:, 7, :].rearrange("p (h b) -> p h b", h=HEADS)[:, :, 0:DEC],
                             osmp[:, :].rearrange("p (h b) -> p h b", h=HEADS), ALU.add))
        tell(dve, "empty_" + "f_ost", 1)
        tell(dve, "f_out", 1)

        done = [C_POOL_END]

        def low(n, slot, count):
            dve.wait_ge(*told("hi_done", count))
            V.tensor_tensor(w_lo[:, slot, :, :], raw[:, slot, :, :], w_hi[:, slot, :, :], ALU.subtract).then_inc(sem("lo_dve"), 1)

        def lows(n0, n1):
            for n in range(n0, n1):
                low(n, n % RING, n + 1)

        def loop_lows(c0, i, per, j0, j1):
            for j in range(j0, j1):
                low(None, (c0 + j) % RING, i * per + (c0 + j + 1))

        lows(150, 154)
        dve.wait_ge(*told("bh0_done", 1))
        then(V.tensor_tensor(bl0[:, :, :], fq[:, :, :], bh0[:, :, :], ALU.subtract))
        tell(dve, "branch0", 1)

        def merge(dg):
            g0 = (dg % 2) * 16
            last_gate = P_GATE[dg] + 7
            dve.wait_ge(*told(f"evac{last_gate % 2}", last_gate // 2 + 1))
            dve.wait_ge(sem(f"evac{(last_gate - 1) % 2}"), (last_gate - 1) // 2 + 1)
            for m in range(8):
                k, half = MERGE_ORDER[m // 2], m % 2
                p, n = P_MERGE[dg] + m, C_MERGE[dg] + m
                dve.wait_ge(*told("used", n + 1))
                g = gates[:, g0 + 4 * k + 2 * half:g0 + 4 * k + 2 * half + 2, :]
                V.tensor_tensor(g, g, PS[:, BANK(p):BANK(p) + 2, 0:TOK], ALU.mult).then_inc(sem(f"evac{p % 2}"), 1)
                if m < 7:
                    lows(n + RING, n + RING + 1)
            for par_ in range(2):
                p = P_MERGE[dg] + 6 + par_
                dve.wait_ge(*told(f"evac{p % 2}", p // 2 + 1))
            G = lambda k: gates[:, g0 + 4 * k:g0 + 4 * k + 4, :]
            then(V.tensor_tensor(G(0), G(0), G(1), ALU.add))
            lows(C_MERGE[dg] + 7 + RING, C_MERGE[dg] + 8 + RING)
            then(V.tensor_tensor(G(2), G(2), G(3), ALU.add))
            then(V.tensor_tensor(G(0), G(0), G(2), ALU.add))
            tell(dve, "sums", 1)

        def merged_low(dg):
            dve.wait_ge(*told("mh_done", dg + 1))
            V.tensor_tensor(ml[:, 4 * dg:4 * dg + 4, :], gates[:, (dg % 2) * 16:(dg % 2) * 16 + 4, :],
                            mh[:, 4 * dg:4 * dg + 4, :], ALU.subtract).then_inc(sem("ml_done"), 1)
            dve.wait_ge(*told("ml_done", dg + 1))
            tell(dve, "merged", 1)

        dve.wait_ge(*told("t8_stored1", 16 * 7))
        dve.wait_ge(*told("fox_stored", 16 * 6))
        merge(0)
        merge(1)
        merged_low(0)
        for dg in (2, 3):
            c0 = C_GATE[dg]
            lows(c0 + 4, c0 + 6)
            merged_low(dg - 1)
            lows(c0 + 6, c0 + 8)
            with nc.vector.Fori(1, 4) as i:
                loop_lows(c0, i, 8, 0, 8)
            lows(C_MERGE[dg], C_MERGE[dg] + 4)
            merge(dg)
        merged_low(3)
        lows(C_OUT + 4, C_OUT + 6)

        def out_pass(c0, p0, dst, i, m, per, passes):
            tiles = ds(i * (2 * passes) + 2 * m, 2)
            p = p0 + m
            dve.wait_ge(*told("used", i * (passes * per) + (c0 + per * (m + 1))))
            V.scalar_tensor_tensor(dst[:, tiles, :], xl[:, tiles, :], ALPHA, PS[:, BANK(p):BANK(p) + 2, 0:TOK],
                                   ALU.mult, ALU.add).then_inc(sem(f"evac{p % 2}"), 1)
            dve.wait_ge(*told(f"evac{p % 2}", i * (passes // 2) + (p // 2 + 1)))
            V.scalar_tensor_tensor(dst[:, tiles, :], xh[:, tiles, :], ALPHA, dst[:, tiles, :],
                                   ALU.mult, ALU.add).then_inc(sem("res_done"), 1)

        lows(C_OUT + 6, C_OUT + 7)
        out_pass(C_OUT, P_OUT, xp, 0, 0, 4, 2)
        lows(C_OUT + 7, C_OUT + 8)
        with nc.vector.Fori(1, 4) as i:
            loop_lows(C_OUT, i, 8, 0, 3)
            out_pass(C_OUT, P_OUT, xp, i - 1, 1, 4, 2)
            loop_lows(C_OUT, i, 8, 3, 7)
            out_pass(C_OUT, P_OUT, xp, i, 0, 4, 2)
            loop_lows(C_OUT, i, 8, 7, 8)
        lows(C_UP, C_UP + 3)
        out_pass(C_OUT, P_OUT, xp, 3, 1, 4, 2)
        lows(C_UP + 3, C_UP + 4)

        def layer_norm(n, src, finish):
            dve.wait_ge(*told("res_done", 8 * (n + 1)))
            tell(dve, f"pre{n}", 1)
            dve.wait_ge(*made("l_mu", n + 1))
            then(V.tensor_scalar(mu_r[:, 0, :], PS[:, 4 + 2 * n, 0:TOK], 1.0 / D_MODEL, None, ALU.mult))
            tell(dve, "empty_" + "l_mu", 1)
            part = lambda t4: src[:, 4 * t4:4 * t4 + 4, :]
            spread = lambda r: mu_r[:, r:r + 1, :].to_broadcast([P, 4, TOK])
            for t4 in range(4):
                then(V.tensor_tensor(part(t4), part(t4), spread(0), ALU.subtract))
                tell(dve, f"centred{n}", 1)
            dve.wait_ge(*made("l_var", n + 1))
            then(V.tensor_scalar(mu_r[:, 1, :], PS[:, 5 + 2 * n, 0:TOK], 1.0 / D_MODEL, LN_EPS, ALU.mult, ALU.add))
            tell(dve, "empty_" + "l_var", 1)
            then(V.reciprocal(mu_r[:, 1, :], mu_r[:, 1, :]))
            tell(dve, f"var{n}", 1)
            dve.wait_ge(*told(f"rstd{n}", 1))
            for t4 in range(4):
                then(V.tensor_tensor(part(t4), part(t4), spread(1), ALU.mult))
                for t in range(4 * t4, 4 * t4 + 4):
                    do(V.tensor_scalar(src[:, t, :], src[:, t, :], lnv[:, 2 * n, t:t + 1], lnv[:, 2 * n + 1, t:t + 1],
                                       ALU.mult, ALU.add))
                steps.settle()
                finish(t4)

        layer_norm(0, xp, lambda t4: tell(dve, "x1_f32", 1))
        for t4 in range(4):
            dve.wait_ge(*told("x1_hi", t4 + 1))
            c = slice(4 * t4, 4 * t4 + 4)
            V.tensor_tensor(xl[:, c, :], xp[:, c, :], xh[:, c, :], ALU.subtract).then_inc(sem("x1_ready"), 1)
        dve.wait_ge(*told("x1_ready", 4))

        pg, pu = P_UP, P_UP + 1

        def h_product(i, hh_count):
            dve.wait_ge(*told("used", i * 8 + (C_UP + 8)))
            dve.wait_ge(*told(f"evac{pg % 2}", i + (pg // 2 + 1)))
            if hh_count is not None:
                dve.wait_ge(*told("hl_done", hh_count))
            V.tensor_tensor(hx[:, :, :], sg[:, :, :], PS[:, BANK(pu):BANK(pu) + 2, 0:TOK], ALU.mult).then_inc(sem(f"evac{pu % 2}"), 1)

        def h_low(i):
            dve.wait_ge(*told("hh_done", i + 1))
            V.tensor_tensor(hl[:, ds(i * 2, 2), :], hx[:, :, :], hh[:, ds(i * 2, 2), :], ALU.subtract).then_inc(sem("hl_done"), 1)

        lows(C_UP + 4, C_UP + 8)
        loop_lows(C_UP, 1, 8, 0, 3)
        h_product(0, None)
        loop_lows(C_UP, 1, 8, 3, 7)
        h_low(0)
        loop_lows(C_UP, 1, 8, 7, 8)
        with nc.vector.Fori(2, UP_STEPS) as i:
            loop_lows(C_UP, i, 8, 0, 3)
            h_product(i - 1, i - 1)
            loop_lows(C_UP, i, 8, 3, 7)
            h_low(i - 1)
            loop_lows(C_UP, i, 8, 7, 8)
        lows(C_DOWN, C_DOWN + 3)
        h_product(UP_STEPS - 1, UP_STEPS - 1)
        lows(C_DOWN + 3, C_DOWN + 4)
        h_low(UP_STEPS - 1)

        def down_turn(i, last):
            for m in range(4):
                a, b = 11 * m, 11 * m + 11
                loop_lows(C_DOWN, i, 44, a + (4 if (m == 0) else 3), b)
                if last and m == 3:
                    out_pass(C_DOWN, P_DOWN, yp, i, m, 11, 4)
                    break
                if m == 3:
                    loop_lows(C_DOWN, i + 1, 44, 0, 3)
                    out_pass(C_DOWN, P_DOWN, yp, i, m, 11, 4)
                    loop_lows(C_DOWN, i + 1, 44, 3, 4)
                else:
                    loop_lows(C_DOWN, i, 44, b, b + 3)
                    out_pass(C_DOWN, P_DOWN, yp, i, m, 11, 4)

        down_turn(0, False)
        down_turn(1, True)
        layer_norm(1, yp, lambda t4: tell(dve, "y_ready", 1))

    ctx.close()


_INS = ("x_prompt x_sample cache_k cache_v cache_logf page_table state_s5_re state_s5_im state_hgrn w_in fox_bf "
        "s5_lambda_re s5_lambda_im s5_log_dt s5_b_re s5_b_im s5_c_re s5_c_im s5_d s5_w_glu s5_b_glu hgrn_lb "
        "hgrn_norm_g gmlp_ln_g gmlp_ln_b gmlp_w_s gmlp_b_s w_branch w_out ln1_g ln1_b w_ffn_up w_ffn_down ln2_g "
        "ln2_b").split()
_OUTS = {
    "y_prompt": (1, SEQ, D_MODEL), "y_sample": (DEC, 1, D_MODEL),
    "fox_k_prompt": (1, 1, SEQ, HEADS, P), "fox_v_prompt": (1, 1, SEQ, HEADS, P), "fox_logf_prompt": (1, 1, SEQ, HEADS),
    "fox_k_sample": (1, DEC, 1, HEADS, P), "fox_v_sample": (1, DEC, 1, HEADS, P), "fox_logf_sample": (1, DEC, 1, HEADS),
    "s5_re_prompt": (1, 1, 32, 64), "s5_im_prompt": (1, 1, 32, 64), "s5_re_sample": (1, DEC, 32, 64),
    "s5_im_sample": (1, DEC, 32, 64), "hgrn_prompt": (1, 1, HEADS, P, P), "hgrn_sample": (1, DEC, HEADS, P, P),
    "gmlp_v_sample": (1, DEC, 1, MIX),
}


def kernel(**inputs):
    import numpy as np
    import concourse.bacc as bacc
    from concourse.bass_utils import run_bass_kernel_spmd

    nc = bacc.Bacc("TRN2", target_bir_lowering=False, num_devices=1)
    arrays, A = {}, {}
    for name in _INS:
        a = np.ascontiguousarray(inputs[name])
        arrays["in_" + name] = a
        A[name] = nc.dram_tensor("in_" + name, a.shape, mybir.dt.from_np(a.dtype), kind="ExternalInput").ap()
    O = {name: nc.dram_tensor("out_" + name, shape, F32, kind="ExternalOutput").ap() for name, shape in _OUTS.items()}
    trunk(nc, A, O)
    r = run_bass_kernel_spmd(nc, [arrays], core_ids=[0])
    return tuple(r.results[0]["out_" + name] for name in _OUTS)
```

```python
import math
from contextlib import ExitStack

import concourse.bass as bass
from concourse import mybir
from concourse.alu_op_type import AluOpType as ALU

F32, F32R, I32 = mybir.dt.float32, mybir.dt.float32r, mybir.dt.int32
ACT = mybir.ActivationFunctionType
AX = mybir.AxisListType
ds = bass.ds

P = 128
D_MODEL, SEQ, DEC, MIX, HEADS = 2048, 256, 8, 512, 4
PAST, PAGE = 1024, 128
N_PAGES = PAST // PAGE
D_FF = 5632
TOK = SEQ + DEC
KT = D_MODEL // P
MT = MIX // P
ALPHA = 2.0 ** 0.25
LN_EPS, RMS_EPS = 1e-5, 1e-6
SCALE = P ** -0.5
S5_TILES = 16
LN2_HIGH = 0.693359375
LN2_LOW = -2.12194440e-4
ROUND = 12582912.0
PI_ = 3.1415925
NEG = -1.0e30
COLS = 256
RING = 4
CK = 4

FQ, FK, FV, FF = 0, 512, 1024, 1536
SU = FF + HEADS
HQ, HF, HI, HG, GU, GV, GT = (SU + 512 * (n + 1) for n in range(7))

MIXER_COLS = []
for _start in (SU, HF, HI, HQ, FQ, HG, FK, FV):
    MIXER_COLS += [(_start, COLS), (_start + COLS, COLS)]
MIXER_COLS.append((FF, P))
for _start in (GV, GU):
    MIXER_COLS += [(_start, COLS), (_start + COLS, COLS)]

PASSES_A = len(MIXER_COLS)
C_GATE = [PASSES_A * 4]
C_GLU = C_GATE[0] + 32
C_GATE.append(C_GLU + 2)
C_MERGE = [C_GATE[1] + 32, C_GATE[1] + 40]
C_GATE.append(C_MERGE[1] + 8)
C_MERGE.append(C_GATE[2] + 32)
C_GATE.append(C_MERGE[2] + 8)
C_MERGE.append(C_GATE[3] + 32)
C_OUT = C_MERGE[3] + 8
C_UP = C_OUT + 32
UP_STEPS = D_FF // COLS
C_DOWN = C_UP + UP_STEPS * 8
DOWN_CHUNKS = D_FF // P // CK

P_GATE = [PASSES_A]
P_GLU = P_GATE[0] + 8
P_GATE.append(P_GLU + 2)
P_MERGE = [P_GATE[1] + 8, P_GATE[1] + 16]
P_GATE.append(P_MERGE[1] + 8)
P_MERGE.append(P_GATE[2] + 8)
P_GATE.append(P_MERGE[2] + 8)
P_MERGE.append(P_GATE[3] + 8)
P_OUT = P_MERGE[3] + 8
P_UP = P_OUT + 8
P_DOWN = P_UP + 2 * UP_STEPS
S5_AT = [12, 15, 19, 23, 27, 31, 34, 37, 40]
OUTS_AT = S5_AT[8] + 1
H_AT, H_GAP = 46, 4
H_END = H_AT + 7 * H_GAP
C_STATES, C_STATES_OUT, C_STATE_OUT = 19, 42, 91
CACHE_AT = [44, 44] + [H_AT + 6 + 2 * n for n in range(16)] + [110, 112, 115, 118, 122, 125, 129, 132, 136, 138, 140, 142, 144, 146]
VALUES_AT = [137, 139, 142, 144, 147]
C_POOL_END = C_MERGE[0]

MERGE_ORDER = (1, 2, 3, 0)
LN_PARTS = [0, 2, 4, 8, 12]
HGRN_LEVELS = (64, 32, 16, 8, 4, 2, 1)
NL = len(HGRN_LEVELS)

PRODUCTS = [("x", n, (4 + n % 4,)) for n in range(KT)]
PRODUCTS += [("s5_h0", 0, (5,)), ("vecs", 0, (6,)), ("s5_lam", 0, (4,)), ("s5_ct", 0, (7,)), ("s5_ct", 1, (5,)),
             ("g_ws", 0, (6,)), ("s5_bt", 0, (4,)), ("s5_bt", 1, (5,)), ("s5_bus", 0, (4, 5, 6, 7))]


H_SMP = 5


def _s5_products():
    out = []
    for b in range(8):
        out.append(("s5_bu", b, (4, 5)))
        if b == H_SMP + 1:
            out.append(("h_os", 0, (7,)))
        if b:
            out.append(("s5_y", b - 1, (6 + (b - 1) // 2 % 2,)))
        if b == H_SMP:
            out += [("h_vs", 0, (7,))] + [("h_vb", n, (4 + n % 2,)) for n in range(8)]
    return out + [("s5_y", 7, (7,))]


PRODUCTS += _s5_products()
PRODUCTS += [("s5_out", 0, (4,))] + [("s5_outs", 0, (5,))]
PRODUCTS += [("h_ost", 0, (7,))] + [("h_v", c, (4 + c,)) for c in range(2)] + [("f_tok", 0, (6,))]
for _n in range(NL + 1):
    PRODUCTS += [("f_qb", _n, (6 + _n % 2,)), ("h_att", _n, (4, 5))]
PRODUCTS += [("h_kd", 0, (4, 5)), ("h_s", 0, (6,)), ("h_o", 0, (4, 5)), ("h_last", 0, (7,))]
PRODUCTS += [("h_ms", 0, (4, 5, 6, 7))]
PRODUCTS += [("g_mu", 0, (4,)), ("g_var", 0, (5,))] + [("g_tok", c, (6 + c % 2,)) for c in range(3)]
PRODUCTS += [("g_mix", n, (4 + n,)) for n in range(2)] + [("g_ms", 0, (6,))]
PRODUCTS += [("f_lf", 0, (6,)), ("f_suf", 0, (7,))]
PRODUCTS += [("f_suft", 0, (6,)), ("f_new", 0, (5,)), ("f_sct", 0, (6, 7)), ("f_pt", 0, (4,)), ("f_pn", 0, (5,))]
PRODUCTS += [("f_tok", n, (4 + n % 2,)) for n in range(1, 7)]
PRODUCTS += [("f_s", 0, (4, 5)), ("f_p", 0, (7,)), ("f_o", 0, (4,)), ("f_s", 1, (4, 5)), ("f_p", 1, (7, 4)),
             ("f_o", 1, (5,)), ("f_os", 0, (6,)), ("f_ost", 0, (7,))]
PRODUCTS += [("l_mu", 0, (4,)), ("l_var", 0, (5,)), ("l_mu", 1, (6,)), ("l_var", 1, (7,))]
PRODUCTS += [("y", n, (4 + n % 4,)) for n in range(12)]


def said(text):
    out = []
    for word in text.split():
        word, _, times = word.partition("*")
        name, _, by = word.partition(":")
        out += [(name, int(by or 1))] * int(times or 1)
    return out


TOLD = {
    "act": said("""
        vecs_lnv empty_vecs vecs_ready a_sin empty_s5_h0 h0_ready empty_s5_lam lam_ready empty_s5_ct*2
        empty_g_ws empty_s5_bt*2 s5_bt_ready s5_staged a_table*2 empty_s5_bus bus_ready a_table*3 a_smp
        a_table empty_h_vs h_vs_tok a_table*2 empty_h_os h_os_tok gh_done empty_s5_out empty_s5_outs a_ln
        empty_h_ost empty_h_v*2 empty_f_tok f_qtok a_decay*9 empty_h_kd h_kdt empty_h_s h_s0 empty_h_o h_sq
        h_rstd bh2_done a_lf g_sq g_rstd empty_g_tok*3 g_tokens bh3_done empty_f_lf empty_f_sct f_exp
        empty_f_pt f_ptt empty_f_tok*5 f_vtok empty_f_tok f_pexp empty_f_p f_pt_sb f_pexp empty_f_p f_pt_sb
        gh_done empty_f_os f_ostok bh0_done empty_y y_copied empty_y y_copied empty_y y_copied empty_y
        y_copied empty_y y_copied empty_y y_copied empty_y y_copied empty_y y_copied empty_y y_copied
        empty_y y_copied empty_y y_copied empty_y y_copied"""),
    "dve": said("""
        empty_x*16 d_turns s5_par s5_cd s5_bd d_angle*2 s5_hs empty_s5_bu s5_h d_angle empty_s5_bu s5_h
        d_angle empty_s5_bu s5_h d_angle empty_s5_y:2 empty_s5_bu s5_h d_angle empty_s5_bu s5_h d_angle
        empty_s5_y:2 empty_s5_bu s5_h d_angle empty_h_vb*8 h_smp_done empty_s5_bu s5_h empty_s5_y:2
        empty_s5_bu s5_h s5_sf empty_s5_y:2 s5_yd g_split d_lf d_dif*2 h_qe kv_free empty_h_att empty_f_qb
        kv_free h_qe kv_free empty_h_att empty_f_qb kv_free h_qe kv_free empty_h_att empty_f_qb kv_free h_qe
        kv_free empty_h_att empty_f_qb kv_free h_qe kv_free empty_h_att empty_f_qb kv_free h_qe kv_free
        empty_h_att empty_f_qb kv_free h_qe d_dif kv_free empty_h_att empty_f_qb kv_free empty_h_att
        h_att_done h_kd kv_free empty_f_qb kv_free empty_h_last empty_h_ms h_var h_out branch2 h_done:2
        empty_g_mu g_cent f_lf empty_g_var g_rec g_vn empty_g_mix*2 empty_g_ms g_mixed branch3 g_done f_rc
        empty_f_suf f_suf_in f_qk empty_f_suft f_sc empty_f_new f_max f_prob f_tok_free empty_f_pn f_cum
        kv_free*2 f_vsum empty_f_s f_pmax kv_free f_prompt kv_free f_vsum empty_f_o kv_free*2 f_vsum
        empty_f_s f_pmax kv_free f_prompt kv_free f_vsum empty_f_o glu_done kv_free*2 f_vsum kv_free*2
        f_vsum kv_free*2 f_vsum*2 branch1 empty_f_ost f_out branch0 sums*2 merged*2 sums merged sums merged
        empty_l_mu centred0*5 empty_l_var x1_norm*4 empty_l_mu centred1*5 empty_l_var y_ready*4"""),
    "pool": said("""
        ident_ready consts_ready mlp_ready p_dif*5"""),
}


def before(name, index):
    at = [p[:2] for p in PRODUCTS].index((name, index))
    out = []
    for bank in PRODUCTS[at][2]:
        for n in range(at - 1, -1, -1):
            if bank in PRODUCTS[n][2]:
                if PRODUCTS[n][:2] not in out:
                    out.append(PRODUCTS[n][:2])
                break
    return out


def banks(name, index):
    return [p[2] for p in PRODUCTS if p[:2] == (name, index)][0]


class Steps:

    def __init__(self, engine, sem, tell=None):
        self.engine, self.sem, self.n, self.tell_ = engine, sem, 0, tell

    def do(self, instruction):
        self.n += 1
        instruction.then_inc(self.sem, 1)

    def settle(self):
        self.engine.wait_ge(self.sem, self.n)

    def then(self, instruction):
        self.do(instruction)
        self.settle()

    def tell(self, name):
        self.settle()
        self.tell_(self.engine, name)


def trunk(nc, A, O):
    ctx = ExitStack()
    sems = {}

    def sem(name):
        if name not in sems:
            sems[name] = ctx.enter_context(nc.semaphore(name))
        return sems[name]

    def made(name, count):
        return sem("made"), [p[:2] for p in PRODUCTS].index((name, count - 1)) + 1

    so_far = {}

    def tell(engine, name, by=1):
        who = "act" if engine is nc.scalar else "dve" if engine is nc.vector else "pool"
        so_far.setdefault(who, []).append((name, by))
        assert TOLD[who][len(so_far[who]) - 1] == (name, by), (who, len(so_far[who]), name)
        engine.sem_inc(sem(who + "_told"), 1)

    def told(name, count):
        for who, names in TOLD.items():
            total = 0
            for n, (other, by) in enumerate(names):
                if other == name:
                    total += by
                    if total >= count:
                        return sem(who + "_told"), n + 1
            assert not total, (name, count)
        return sem(name), count

    base = (nc.sbuf_base + 31) // 32 * 32
    ZB = MT * TOK * 4
    XB = KT * TOK * 4
    CB = CK * COLS * 4
    at_raw, at_hi, at_lo = 0, RING * CB, 2 * RING * CB
    at_xh = 3 * RING * CB
    at_xl = at_xh + XB
    at_g = at_xl + XB
    at_z = at_g + 2 * XB
    at_kv = at_z + 13 * ZB
    at_fix = at_kv + 2 * 4 * MIX * 4

    def place(name, shape, dt, off):
        return nc.alloc_sbuf_tensor_at(name, shape, dt, offset=base + off)

    raw = place("w_raw", [P, RING, CK, COLS], F32, at_raw)
    w_hi = place("w_hi", [P, RING, CK, COLS], F32R, at_hi)
    w_lo = place("w_lo", [P, RING, CK, COLS], F32R, at_lo)
    xh = place("xh", [P, KT, TOK], F32R, at_xh)
    xl = place("xl", [P, KT, TOK], F32R, at_xl)
    gates = place("gates", [P, 32, TOK], F32, at_g)

    def z(name, slot, dt=F32):
        return place(name, [P, MT, TOK], dt, at_z + slot * ZB)

    gh1, gl1 = z("gh1", 0, F32R), z("gl1", 1, F32R)
    hq, hi_ = z("hq", 2), z("hi", 3)
    bh2, bl2 = z("bh2", 2, F32R), z("bl2", 3, F32R)
    fk, fv = z("fk", 4), z("fv", 5)
    bh0, bl0 = z("bh0", 4, F32R), z("bl0", 5, F32R)
    gv, kt_ = z("gv", 6), z("kt", 7)
    bh3, bl3 = z("bh3", 6, F32R), z("bl3", 7, F32R)
    su, hf, fq, gu, hg = (z(n, 8 + i) for i, n in enumerate(("su", "hf", "fq", "gu", "hg")))
    bh, bl = [bh0, gh1, bh2, bh3], [bl0, gl1, bl2, bl3]
    mh = place("mh", [P, KT, TOK], F32R, at_z + 8 * ZB)
    ml = place("ml", [P, KT, TOK], F32R, at_z + 12 * ZB)
    kv = place("kv", [P, 2, 4, MIX], F32, at_kv)

    at_keep = (nc.sbuf_usable_end - base) // 32 * 32 - 2 * P * 4 - 4 * KT * 4
    ident = place("ident", [P, P], F32, at_keep)
    ones = place("ones", [P, P], F32, at_keep + P * 4)
    lnv = place("lnv", [P, 4, KT], F32, at_keep + 2 * P * 4)

    off = [at_fix]

    def fix(name, shape, dt=F32):
        n = 4
        for s in shape[1:]:
            n *= s
        t = place(name, shape, dt, off[0])
        off[0] += (n + 31) // 32 * 32
        assert off[0] <= at_keep
        return t

    level_mask = fix("level_mask", [P, NL + 1, P], I32)
    causal = fix("causal", [P, P])
    ws_t = fix("ws_t", [P, MT, P])
    lam_t = fix("lam_t", [P, 6, S5_TILES])
    h0 = fix("h0", [P, 2, S5_TILES, DEC])
    v_tok = fix("v_tok", [P, 2, MIX])
    s5o = place("s5o", [P, 2, P], F32, off[0] + MIX * 4)
    t8 = fix("t8", [DEC, 2, MIX])
    sc = fix("sc", [P, N_PAGES, 32])
    small = fix("small", [P, 64])
    vecs = fix("vecs", [P, 5, MT])
    bs_row = fix("bs_row", [1, MT, P])
    ws00 = fix("ws00", [1, MT])
    lf_t = fix("lf_t", [HEADS, TOK])
    q8 = place("q8", [DEC, MIX], F32, off[0])
    ho = place("ho", [32, MIX], F32, off[0])
    cum = fix("cum", [HEADS, 2, SEQ])
    bf = fix("bf", [HEADS, 1])
    eye8 = fix("eye8", [P, DEC, DEC])
    hos = place("hos", [P, 32], F32, at_g + 33280)
    pt = fix("pt", [1, DEC * N_PAGES], I32)
    pt_col = fix("pt_col", [DEC * N_PAGES, 1], I32)
    par = place("par", [P, 4], F32, at_g + 33536)
    sf = place("sf", [P, 2, S5_TILES], F32, at_g + 33408)
    osmp = place("osmp", [P, 32], F32, at_fix + 1280)

    x_nat = place("x_nat", [P, 2, D_MODEL], F32, at_g)
    xs_nat = place("xs_nat", [DEC, D_MODEL], F32, at_g + 2 * D_MODEL * 4)
    h0_nat = place("h0_nat", [P, 2, P], F32, at_z + 9 * ZB)
    bn = place("bn", [P, 2, S5_TILES, 16], F32, at_kv)
    cn = place("cn", [P, 2, MT, 64], F32, at_kv + 2048)
    bd = place("bd", [P, 2, S5_TILES, 2, 16], F32, at_kv + 4096)
    cd = place("cd", [P, 2, MT, 2, 64], F32, at_kv + 8192)
    s5p = place("s5p", [S5_TILES, 16, P], F32, at_z + 0 * ZB)
    dt2 = place("dt2", [S5_TILES, 2], F32, at_z + 1 * ZB + 4096)
    ws_nat = place("ws_nat", [P, MT, P], F32, at_kv + 12288)
    vec_nat = place("vec_nat", [4 * KT + 5 * MT, P], F32, at_kv + 14336)
    g0 = at_g
    bt = place("bt", [P, 2, MT, P], F32, g0)
    ct = place("ct", [P, 2, MT, P], F32, g0 + 4096)
    er = place("er", [P, 2, 2, SEQ], F32, g0 + 8192)
    ei = place("ei", [P, 2, 2, SEQ], F32, g0 + 12288)
    tab = place("tab", [P, 2, SEQ], F32, g0 + 16384)
    rnd = place("rnd", [P, 2, SEQ], F32, g0 + 18432)
    gr = place("gr", [P, 2, SEQ], F32, g0 + 20480)
    gi = place("gi", [P, 2, SEQ], F32, g0 + 22528)
    hr = place("hr", [P, 2, TOK], F32, at_z + 11 * ZB + 1024)
    tmp2 = place("tmp2", [P, 2, SEQ], F32, g0 + 24576)
    hm = place("hm", [P, 2, TOK], F32, g0 + 26624)
    bus = place("bus", [P, 2, S5_TILES, DEC], F32, g0 + 28672)
    hs = place("hs", [P, 2, DEC, S5_TILES], F32, g0 + 29696)
    iota16 = place("iota16", [P, 16], F32, g0 + 33568)
    rot_a = place("rot_a", [P, S5_TILES, 16], F32, g0 + 30720)
    rot_b = place("rot_b", [P, S5_TILES, 16], F32, at_z + 11 * ZB)
    qm = place("qm", [P, DEC, HEADS, DEC], F32, g0 + 31744)
    bc = place("bc", [P, 8, P], F32, g0)
    att = place("att", [P, 8, P], F32, g0 + 4096)
    s_prev = place("s_prev", [P, 2, HEADS, P], F32, g0 + 8192)
    qb_h = place("qb_h", [P, HEADS, P], F32, g0 + 12288)
    dif = place("dif", [P, 2, 8, P], F32, g0 + 16896)
    qe = place("qe", [P, 8, P], F32, g0 + 25088)
    ke = place("ke", [P, 8, P], F32, g0 + 29184)
    s_smp = place("s_smp", [P, 32, P], F32, at_kv)
    k_tok = place("k_tok", [P, 2, MIX], F32, at_z + 12 * ZB)
    lfp = place("lfp", [DEC * N_PAGES, PAGE, HEADS], F32, at_z + 9 * ZB)
    rc = place("rc", [DEC * N_PAGES, PAGE, HEADS], F32, at_z + 9 * ZB + 2048)
    tri = place("tri", [64, 64], F32, at_fix)
    ptt = place("ptt", [P, N_PAGES, 32], F32, at_fix + 256)
    ps_row = place("ps_row", [32, PAST], F32, g0 + 24 * TOK * 4)
    s_sb = place("s_sb", [P, HEADS, SEQ], F32, g0 + 24 * TOK * 4)
    pt_sb = place("pt_sb", [P, 2, HEADS, P], F32, g0 + 28 * TOK * 4)
    lnt = place("lnt", [P, MT, TOK], F32, g0 + 16896)
    gsq, sgl = z("gsq", 12), z("sgl", 12)
    vacc = place("vacc", [P, 2, MIX], F32, at_z + 11 * ZB)
    xp = place("xp", [P, KT, TOK], F32, at_g)
    sq = place("sq", [P, KT, TOK], F32, at_g + XB)
    acc0 = place("acc0", [P, 2, TOK], F32, at_g + XB + 14 * TOK * 4)
    acc1 = place("acc1", [P, 2, TOK], F32, at_g)
    sg = place("sg", [P, 2, TOK], F32, at_g)
    hx = place("hx", [P, 2, TOK], F32, at_g + 2112)
    hh = place("hh", [P, D_FF // P, TOK], F32R, at_g + 4224)
    hl = place("hl", [P, D_FF // P, TOK], F32R, at_g + 4224 + (D_FF // P) * TOK * 4)
    yp = place("yp", [P, KT, TOK], F32, at_g + 4224 + 2 * (D_FF // P) * TOK * 4)
    sq2 = place("sq2", [P, KT, TOK], F32, at_g + 4224)
    y_tok = place("y_tok", [P, 2, D_MODEL], F32, at_g + 4224 + XB)
    ys_tok = place("ys_tok", [DEC, D_MODEL], F32, at_g + 4224 + XB + 2 * D_MODEL * 4)
    mu_r = place("mu_r", [P, 2, TOK], F32, at_g + 4224 + 2 * (D_FF // P) * TOK * 4 + XB)

    PS = nc.alloc_psum_tensor("ps", [P, 8, 512], F32)

    rows = lambda ap: ap.rearrange("(k p) c -> p k c", p=P)

    def claim(pe, name, index=0):
        for other, n in before(name, index):
            pe.wait_ge(*told("empty_" + other, n + 1))
        return banks(name, index)

    def lo_done(engine, n):
        if n < C_POOL_END:
            engine.wait_ge(*told("lo_pool", n + 1))
        else:
            engine.wait_ge(*told("lo_dve", n - C_POOL_END + 1))

    def distances(n):
        if n == NL + 1:
            return dif[:, n % 2, :, :], bc[:, :, P - 1:P].to_broadcast([P, 8, P]), bc[:, :, :]
        b = HGRN_LEVELS[n]
        v = bc[:, :, :].rearrange("p a (m c) -> p (a m) c", c=2 * b)
        d = dif[:, n % 2, :, :].rearrange("p a (m c) -> p (a m) c", c=2 * b)
        return d, v, v[:, :, b - 1:b].to_broadcast([P, 8 * P // (2 * b), 2 * b])

    block = ctx.enter_context(nc.Block())

    @block.sync
    def _(sp):
        def load_chunk(n, slot, src, cols=COLS, freed=None):
            if freed is None and n >= RING:
                lo_done(sp, n - RING)
            elif freed is not None:
                sp.wait_ge(*told("lo_dve", freed))
            sp.dma_start(raw[:, slot, :, 0:cols], src).then_inc(sem(f"raw{slot}"), 16)

        w_in = A["w_in"][0]

        sp.dma_start(xs_nat[:, :], A["x_sample"].rearrange("b o d -> (b o) d")).then_inc(sem("xs_loaded"), 16)
        for q in range(4):
            c = slice(q * 512, q * 512 + 512)
            sp.dma_start(x_nat[:, :, c], A["x_prompt"][0].rearrange("(n p) d -> p n d", p=P)[:, :, c]).then_inc(sem(f"x_loaded{q}"), 16)

        def load(dst, src, name):
            sp.dma_start(dst, src, allow_slow_non_contiguous=True).then_inc(sem(name), 16)

        load(s5p[:, 0, :], A["s5_lambda_re"][0].rearrange("(i g) p -> i (g p)", g=2), "s5_loaded")
        load(s5p[:, 1, :], A["s5_lambda_im"][0].rearrange("(i g) p -> i (g p)", g=2), "s5_loaded")
        load(dt2[:, :], A["s5_log_dt"][0].rearrange("(i g) -> i g", g=2), "s5_loaded")
        for r, part in enumerate(("re", "im")):
            load(cn[:, r, :, :], A[f"s5_c_{part}"][0].rearrange("(q g) h p -> (g h) q p", g=8), "s5_loaded")
            load(bn[:, r, :, :], A[f"s5_b_{part}"][0].rearrange("(i g) p h -> (g p) i h", g=2), "s5_loaded")
            load(h0_nat[:, r, :], A[f"state_s5_{part}"][0].rearrange("b (i g) p -> (b i) (g p)", g=2), "s5_loaded")

        def load_rest():
            load(ws_nat[:, :, :], A["gmlp_w_s"][0].rearrange("g t s -> t g s"), "mix_loaded")
            for n, name in enumerate(("ln1_g", "ln1_b", "ln2_g", "ln2_b")):
                load(vec_nat[n * KT:(n + 1) * KT, :], A[name][0].rearrange("(t p) -> t p", p=P), "mix_loaded")
            for n, name in enumerate(("s5_d", "s5_b_glu", "hgrn_norm_g", "gmlp_ln_g", "gmlp_ln_b")):
                load(vec_nat[4 * KT + n * MT:4 * KT + (n + 1) * MT, :], A[name][0].rearrange("(t p) -> t p", p=P), "mix_loaded")
            load(bs_row[:, :, :], A["gmlp_b_s"], "consts_loaded")
            load(ws00[:, :], A["gmlp_w_s"][:, :, 0, 0], "consts_loaded")
            load(bf[:, :], A["fox_bf"][0].rearrange("(h o) -> h o", o=1), "consts_loaded")
            load(pt[:, :], A["page_table"].rearrange("(o b) n -> o (b n)", o=1), "consts_loaded")
            load(pt_col[:, :], A["page_table"].rearrange("b (n o) -> (b n) o", o=1), "consts_loaded")


        def load_cache(cache, n):
            pages = [sp.value_load(pt[0:1, (n % 16) * 4 + j:(n % 16) * 4 + j + 1], min_val=0,
                                   max_val=cache.shape[1] - 1) for j in range(4)]
            if n == 0:
                sp.wait_ge(sem("h_store"), 16)
            if n >= 2:
                sp.wait_ge(*told("kv_free", n - 1))
            for j, page in enumerate(pages):
                src = cache[0][ds(page, 1)].rearrange("o s h d -> (o s) (h d)")
                sp.dma_start(kv[:, n % 2, j, :], src).then_inc(sem(f"kv{n % 2}"), 16)

        hgrn_out = O["hgrn_sample"][0].rearrange("b h k v -> k (b h) v")

        def load_caches(n0, n1):
            for n in range(n0, n1):
                load_cache(A["cache_k"] if n < 16 else A["cache_v"], n)

        caches = [0]

        def load_due(n):
            due = sum(n >= at for at in CACHE_AT)
            load_caches(caches[0], due)
            caches[0] = due

        for p in range(PASSES_A):
            for kc in range(4):
                n, (col, cols) = 4 * p + kc, MIXER_COLS[p]
                load_chunk(n, n % RING, rows(w_in[kc * 512:(kc + 1) * 512, col:col + cols]), cols)
                if n == C_STATES:
                    sp.wait_ge(*told("s5_staged", 1))
                    for b in range(DEC):
                        sp.dma_start(s_smp[:, 4 * b:4 * b + 4, :],
                                     A["state_hgrn"][0, b].rearrange("h k v -> k h v")).then_inc(sem("s_smp"), 16)
                if n == C_STATES_OUT:
                    sp.wait_ge(*told("h_smp_done", 1))
                    sp.wait_ge(*made("h_os", 1))
                    sp.dma_start(hgrn_out, s_smp[:, :, :]).then_inc(sem("h_store"), 16)
                    sp.wait_ge(*told("consts_loaded", 16 * 5))
                if n == 1:
                    load_rest()
                load_due(n)

        def gate_passes(dg):
            for k in range(4):
                for half in range(2):
                    for kc in range(4):
                        n = C_GATE[dg] + 8 * k + 4 * half + kc
                        col = GT + k * D_MODEL + dg * 512 + half * COLS
                        load_chunk(n, n % RING, rows(w_in[kc * 512:(kc + 1) * 512, col:col + COLS]))
                        load_due(n)
                        if n == C_STATE_OUT:
                            sp.wait_ge(*told("h_done", 1))
                            sp.dma_start(O["hgrn_prompt"][0, 0].rearrange("h k v -> k h v"),
                                         s_prev[:, 1, :, :]).then_inc(sem("h_store"), 16)

        gate_passes(0)
        load_chunk(C_GLU, C_GLU % RING, rows(A["s5_w_glu"][0][:, 0:COLS]))
        load_chunk(C_GLU + 1, (C_GLU + 1) % RING, rows(A["s5_w_glu"][0][:, COLS:2 * COLS]))
        gate_passes(1)

        def load_merge(dg):
            for m, k in enumerate(MERGE_ORDER):
                for half in range(2):
                    n = C_MERGE[dg] + 2 * m + half
                    load_chunk(n, n % RING, rows(A["w_branch"][0, k][:, dg * 512 + half * COLS:dg * 512 + (half + 1) * COLS]))

        def load_gates(dg):
            base_c = C_GATE[dg]
            with nc.sync.Fori(0, 4) as k:
                for j in range(8):
                    n = base_c + j
                    src = w_in[(j % 4) * 512:(j % 4 + 1) * 512, ds(k * D_MODEL + (GT + dg * 512 + (j // 4) * COLS), COLS)]
                    load_chunk(None, n % RING, rows(src), freed=k * 8 + (n - RING - C_POOL_END + 1))

        def load_square(w, c0, count, tiles):
            with nc.sync.Fori(0, count) as i:
                for j in range(2 * tiles):
                    n = c0 + j
                    src = w[(j % tiles) * 512:(j % tiles + 1) * 512, ds(i * (2 * COLS) + (j // tiles) * COLS, COLS)]
                    load_chunk(None, n % RING, rows(src), freed=i * (2 * tiles) + (n - RING - C_POOL_END + 1))

        load_merge(0)
        load_merge(1)
        for dg in (2, 3):
            load_gates(dg)
            load_merge(dg)
        load_square(A["w_out"][0], C_OUT, 4, 4)
        w_up = A["w_ffn_up"][0]
        with nc.sync.Fori(0, UP_STEPS) as i:
            for j in range(8):
                n = C_UP + j
                src = w_up[(j % 4) * 512:(j % 4 + 1) * 512, ds(i * COLS + (j // 4) * D_FF, COLS)]
                load_chunk(None, n % RING, rows(src), freed=i * 8 + (n - RING - C_POOL_END + 1))
        w_down = A["w_ffn_down"][0]
        with nc.sync.Fori(0, 2) as i:
            for j in range(4 * DOWN_CHUNKS):
                n = C_DOWN + j
                ps, kc = j // DOWN_CHUNKS, j % DOWN_CHUNKS
                src = w_down[kc * 512:(kc + 1) * 512, ds(i * (4 * COLS) + ps * COLS, COLS)]
                load_chunk(None, n % RING, rows(src), freed=i * (4 * DOWN_CHUNKS) + (n - RING - C_POOL_END + 1))
        for half in range(4):
            sp.wait_ge(*told("y_copied", 3 * half + 3))
            c = slice(half * 512, half * 512 + 512)
            sp.dma_start(O["y_prompt"][0].rearrange("(n p) d -> p n d", p=P)[:, :, c], y_tok[:, :, c]).then_inc(sem("stored"), 16)
            sp.dma_start(O["y_sample"].rearrange("b o d -> (b o) d")[:, c], ys_tok[:, c]).then_inc(sem("stored"), 16)
        sp.wait_ge(*told("stored", 16 * 8))
        sp.wait_ge(*told("h_store", 16 * 2))

    @block.gpsimd
    def _(pool):
        steps = Steps(pool, sem("pool_steps"), tell)
        steps.do(pool.memset(ident[:, :], 0.0))
        steps.then(pool.memset(ones[:, :], 1.0))
        steps.then(pool.affine_select(out=ident[:, :], in_=ident[:, :], compare_op=ALU.not_equal, fill=1.0, base=0,
                                      pattern=[[-1, P]], channel_multiplier=1))
        tell(pool, "ident_ready")
        steps.do(pool.iota(iota16[:, :], [[1, 16]], base=0, channel_multiplier=0,
                           allow_small_or_imprecise_dtypes=True))
        steps.do(pool.iota(small[:, 0:1].bitcast(I32), [[0, 1]], base=0, channel_multiplier=1))
        steps.do(pool.iota(level_mask[:, 0, :], [[1, P]], base=0, channel_multiplier=0))
        steps.do(pool.iota(level_mask[:, 1, :], [[0, P]], base=0, channel_multiplier=1))
        steps.do(pool.memset(bd[:, :, :, :, :], 0.0))
        steps.then(pool.memset(eye8[:, :, :], 0.0))
        steps.do(pool.affine_select(out=eye8[:, :, :], in_=eye8[:, :, :], compare_op=ALU.not_equal, fill=1.0, base=0,
                                    pattern=[[1, DEC], [-1, DEC]], channel_multiplier=0))
        steps.tell("consts_ready")

        def low_parts(c0, c1):
            with nc.gpsimd.Fori(0, (c1 - c0) // RING) as i:
                for j in range(RING):
                    n = c0 + j
                    pool.wait_ge(*told("hi_done", i * RING + (n + 1)))
                    pool.tensor_tensor(w_lo[:, j, :, :], raw[:, j, :, :], w_hi[:, j, :, :],
                                       ALU.subtract).then_inc(sem("lo_pool"), 1)

        low_parts(0, 4)
        pool.wait_ge(*told("mix_loaded", 16 * 10))
        steps.do(pool.affine_select(out=ws_nat[:, :, :], in_=ws_nat[:, :, :], compare_op=ALU.is_ge, fill=0.0, base=0,
                                    pattern=[[0, MT], [-1, P]], channel_multiplier=1))
        steps.then(pool.memset(causal[:, :], 0.0))
        steps.do(pool.affine_select(out=causal[:, :], in_=causal[:, :], compare_op=ALU.is_ge, fill=NEG, base=0,
                                    pattern=[[-1, P]], channel_multiplier=1))
        steps.tell("mlp_ready")
        first = (H_AT + RING - 1) // RING * RING
        low_parts(4, first)
        for n in range(2, NL):
            pool.wait_ge(*told("h_qe", n - 1))
            steps.then(pool.tensor_tensor(*distances(n), ALU.subtract))
            steps.tell("p_dif")
            low_parts(first, first + H_GAP)
            first += H_GAP
        low_parts(first, 92)
        pool.wait_ge(*told("h_done", 1))
        steps.then(pool.memset(tri[:, :], 1.0))
        steps.then(pool.affine_select(out=tri[:, :], in_=tri[:, :], compare_op=ALU.is_gt, fill=0.0, base=0,
                                      pattern=[[-1, 64]], channel_multiplier=1))
        steps.then(pool.affine_select(out=tri[:, :].rearrange("k (b p) -> k b p", p=8),
                                      in_=tri[:, :].rearrange("k (b p) -> k b p", p=8), compare_op=ALU.is_ge,
                                      fill=0.0, base=7, pattern=[[8, 8], [0, 8]], channel_multiplier=-1))
        pool.wait_ge(*told("consts_loaded", 16 * 5))
        table = A["cache_logf"][0].rearrange("n s h -> n (s h)")
        pool.indirect_dma_start(out=lfp[:, :, :].rearrange("r s h -> r (s h)"), out_offset=None, in_=table,
                                in_offset=bass.IndirectOffsetOnAxis(ap=pt_col[:, 0:1], axis=0)).then_inc(sem("lfp"), 16)
        low_parts(92, 148)
        for n in (148, 149):
            pool.wait_ge(*told("hi_done", n + 1))
            pool.tensor_tensor(w_lo[:, n % RING, :, :], raw[:, n % RING, :, :], w_hi[:, n % RING, :, :],
                               ALU.subtract).then_inc(sem("lo_pool"), 1)


    targets = []
    for name in ("su", "hf", "hi", "hq", "fq", "hg", "fk", "fv"):
        targets += [(name, 0), (name, 1)]
    targets.append(("ff", 0))
    for name in ("gv", "gu"):
        targets += [(name, 0), (name, 1)]
    where = dict(su=su, hf=hf, hq=hq, hi=hi_, hg=hg, fq=fq, fk=fk, fv=fv, gv=gv, gu=gu)
    functions = dict(gv=ACT.Gelu_apprx_tanh, gu=ACT.Gelu_apprx_tanh, hg=ACT.Silu)

    def projected(engine, name):
        for p in range(PASSES_A):
            if targets[p][0] == name:
                engine.wait_ge(*told(f"evac{p % 2}", p // 2 + 1))

    BANK = lambda p: 2 * (p % 2)

    @block.tensor
    def _(pe):
        def products(slot, bank, right_h, right_l, k0, first, last, cols=COLS):
            for kk in range(CK):
                rh, rl = right_h[:, k0 + kk, :], right_l[:, k0 + kk, :]
                for half in range(cols // P):
                    out = PS[:, bank + half, 0:TOK]
                    c = slice(half * P, half * P + P)
                    nc.tensor.matmul(out, w_hi[:, slot, kk, c], rh, start=(first and kk == 0), stop=False)
                    nc.tensor.matmul(out, w_hi[:, slot, kk, c], rl, start=False, stop=False)
                    ins = nc.tensor.matmul(out, w_lo[:, slot, kk, c], rh, start=False, stop=(last and kk == CK - 1))
            ins.then_inc(sem("used"), 1)

        done = [0]

        def chunk(p, kc, chunks, right_h, right_l, cols=COLS):
            n = done[0]
            if kc == 0 and p >= 2:
                pe.wait_ge(*told(f"evac{p % 2}", p // 2))
            lo_done(pe, n)
            products(n % RING, BANK(p), right_h, right_l, CK * kc, kc == 0, kc == chunks - 1, cols)
            done[0] += 1

        def weights(upto):
            while done[0] < upto:
                n = done[0]
                if n < C_GATE[0]:
                    p = n // 4
                    if p == 0:
                        pe.wait_ge(sem("x_split"), CK * (n + 1))
                    chunk(p, n % 4, 4, xh, xl, MIXER_COLS[p][1])
                elif n < C_GLU:
                    chunk(P_GATE[0] + (n - C_GATE[0]) // 4, (n - C_GATE[0]) % 4, 4, xh, xl)
                elif n < C_GATE[1]:
                    if n == C_GLU:
                        pe.wait_ge(*told("g_split", 1))
                    chunk(P_GLU + n - C_GLU, 0, 1, gh1, gl1)
                else:
                    chunk(P_GATE[1] + (n - C_GATE[1]) // 4, (n - C_GATE[1]) % 4, 4, xh, xl)

        def transposes(name, index, parts):
            bank = claim(pe, name, index)[0]
            for col, src in parts:
                p, f = src.shape[0], src.shape[-1]
                ins = nc.tensor.transpose(PS[0:f, bank + col // 512, col % 512:col % 512 + p], src, ident[0:p, 0:p])
            ins.then_inc(sem("made"), 1)

        pe.wait_ge(*told("ident_ready", 1))
        pe.wait_ge(sem("xs_loaded"), 16)
        for k in range(KT):
            if k % 4 == 0:
                pe.wait_ge(sem(f"x_loaded{k // 4}"), 16)
            c = slice(k * P, k * P + P)
            transposes("x", k, [(0, x_nat[:, 0, c]), (P, x_nat[:, 1, c]), (SEQ, xs_nat[:, c])])

        pe.wait_ge(*told("s5_loaded", 16 * 9))
        transposes("s5_h0", 0, [(P * r, h0_nat[:, r, :]) for r in range(2)])
        weights(2)
        pe.wait_ge(*told("mix_loaded", 16 * 10))
        transposes("vecs", 0, [(0, vec_nat[:, :])])
        weights(4)
        pe.wait_ge(*told("s5_par", 1))
        transposes("s5_lam", 0, [(16 * k, s5p[:, 2 + k, :]) for k in range(6)])
        pe.wait_ge(*told("s5_cd", 1))
        for r in range(2):
            transposes("s5_ct", r, [(P * q, cd[:, r, q, :, :].rearrange("p a b -> p (a b)")) for q in range(MT)])
        pe.wait_ge(*told("mlp_ready", 1))
        transposes("g_ws", 0, [(P * g, ws_nat[:, g, :]) for g in range(MT)])
        weights(5)
        pe.wait_ge(*told("s5_bd", 1))
        for r in range(2):
            transposes("s5_bt", r, [(P * q, bd[:, r, 4 * q:4 * q + 4, :, :].rearrange("p i g h -> p (i g h)"))
                                    for q in range(MT)])
        weights(12)

        def s5_input(i, r):
            rows_ = slice(32 * (i % 4), 32 * (i % 4) + 32)
            return bt[rows_, r, i // 4, :], su[rows_, i // 4, :]

        projected(pe, "su")
        pe.wait_ge(*told("s5_bt_ready", 1))
        bank = claim(pe, "s5_bus")[0]
        for r in range(2):
            for i in range(S5_TILES):
                b, u = s5_input(i, r)
                col = (4 * r + i // 4) * DEC
                ins = nc.tensor.matmul(PS[:, bank + i % 4, col:col + DEC], b, u[:, SEQ:TOK], start=True, stop=True)
        ins.then_inc(sem("made"), 1)

        def s5_bu(b):
            bank = claim(pe, "s5_bu", b)[0]
            for t in range(2):
                for r in range(2):
                    w, u = s5_input(2 * b + t, r)
                    ins = nc.tensor.matmul(PS[:, bank + t, r * SEQ:r * SEQ + SEQ], w, u[:, 0:SEQ], start=True, stop=True)
            ins.then_inc(sem("made"), 1)

        def s5_y(b):
            bank = claim(pe, "s5_y", b)[0] if b % 2 == 0 else banks("s5_y", b)[0]
            pe.wait_ge(*told("s5_h", b + 1))
            for t in range(2):
                i = 2 * b + t
                q, j = i // 4, i % 4
                out = PS[32 * j:32 * j + 32, bank, :]
                for r, st in enumerate((hr, hm)):
                    ins = nc.tensor.matmul(out[:, 0:TOK], ct[:, r, q, 32 * j:32 * j + 32], st[:, t, :],
                                           start=(r == 0), stop=(r == 1), tile_position=(0, 32 * j))
            ins.then_inc(sem("made"), 1)

        s5_bu(0)
        for b in range(1, 8):
            weights(S5_AT[b] - 2)
            s5_bu(b)
            if b == H_SMP + 1:
                bank = claim(pe, "h_os")[0]
                pe.wait_ge(*told("h_smp_done", 1))
                for n in range(DEC):
                    ins = nc.tensor.matmul(PS[0:32, bank, :], qm[:, n, :, :].rearrange("p h m -> p (h m)"),
                                           s_smp[:, 4 * n:4 * n + 4, :].rearrange("p h v -> p (h v)"),
                                           start=(n == 0), stop=(n == DEC - 1))
                ins.then_inc(sem("made"), 1)
            weights(S5_AT[b] + 1)
            s5_y(b - 1)
            if b == H_SMP:
                projected(pe, "hi")
                transposes("h_vs", 0, [(P * h, hi_[:, h, SEQ:TOK]) for h in range(HEADS)])
                weights(done[0] + 1)
                pe.wait_ge(*told("h_vs_tok", 1))
                for n in range(DEC):
                    bank = claim(pe, "h_vb", n)[0]
                    nc.tensor.matmul(PS[:, bank, :], ident[0:DEC, n:n + 1].to_broadcast([DEC, P]), t8[:, 0, :],
                                     start=True, stop=True).then_inc(sem("made"), 1)
                    if n in (1, 3):
                        weights(done[0] + (2 if n == 1 else 1))
        weights(S5_AT[8])
        s5_y(7)
        weights(OUTS_AT)
        bank = claim(pe, "s5_out")[0]
        pe.wait_ge(*told("s5_sf", 1))
        for r in range(2):
            ins = nc.tensor.transpose(PS[0:S5_TILES, bank, r * P:r * P + P], sf[:, r, :], ident[:, :])
        ins.then_inc(sem("made"), 1)
        bank = claim(pe, "s5_outs")[0]
        for r in range(2):
            ins = nc.tensor.transpose(PS[:, bank, r * P:r * P + P], hs[:, r, :, :].rearrange("p b i -> p (b i)"), ident[:, :])
        ins.then_inc(sem("made"), 1)
        weights(OUTS_AT + 1)
        pe.wait_ge(*told("h_os_tok", 1))
        transposes("h_ost", 0, [((P - DEC) * h, ho[:, h * P:h * P + P]) for h in range(HEADS)])
        for c in range(2):
            transposes("h_v", c, [(P * h, hi_[:, h, c * P:c * P + P]) for h in range(HEADS)])
        weights(OUTS_AT + 2)
        projected(pe, "fq")
        transposes("f_tok", 0, [(P * h, fq[:, h, SEQ:TOK]) for h in range(HEADS)])
        for n in range(NL + 1):
            weights(H_AT + H_GAP * n)
            bank = claim(pe, "f_qb", n)[0]
            if n == 0:
                pe.wait_ge(*told("f_qtok", 1))
            nc.tensor.matmul(PS[:, bank, :], ident[0:DEC, n:n + 1].to_broadcast([DEC, P]), q8[:, :],
                             start=True, stop=True).then_inc(sem("made"), 1)
            bank = claim(pe, "h_att", n)[0]
            if n < NL:
                pe.wait_ge(*told("h_qe", n + 1))
            for hc in range(8):
                h, c = hc // 2, hc % 2
                t = slice(c * P, c * P + P)
                keys, queries = (ke[:, hc, :], qe[:, hc, :]) if n < NL else (kt_[:, h, t], hq[:, h, t])
                ins = nc.tensor.matmul(PS[:, bank + hc // 4, (hc % 4) * P:(hc % 4) * P + P], keys, queries,
                                       start=True, stop=True)
            ins.then_inc(sem("made"), 1)
        weights(H_END + 1)
        pe.wait_ge(*told("h_kd", 1))
        transposes("h_kd", 0, [(P * hc, qe[:, hc, :]) for hc in range(8)])
        weights(H_END + 3)
        pe.wait_ge(*told("h_kdt", 1))

        def h_state(c):
            bank = claim(pe, ("h_s", "h_last")[c])[0]
            for h in range(HEADS):
                ins = nc.tensor.matmul(PS[:, bank, h * P:h * P + P], ke[:, 2 * h + c, :],
                                       v_tok[:, c, h * P:h * P + P], start=True, stop=True)
            ins.then_inc(sem("made"), 1)

        h_state(0)
        weights(H_END + 5)
        bank = claim(pe, "h_o")[0]
        pe.wait_ge(*told("h_s0", 1))
        pe.wait_ge(*told("h_att_done", 1))
        for h in range(HEADS):
            out = PS[:, bank + h // 2, (h % 2) * SEQ:(h % 2) * SEQ + SEQ]
            v = slice(h * P, h * P + P)
            nc.tensor.matmul(out[:, 0:P], v_tok[:, 0, v], att[:, 2 * h, :], start=True, stop=True)
            nc.tensor.matmul(out[:, P:SEQ], v_tok[:, 1, v], att[:, 2 * h + 1, :], start=True, stop=False)
            ins = nc.tensor.matmul(out[:, P:SEQ], s_prev[:, 0, h, :], qb_h[:, h, :], start=False, stop=True)
        ins.then_inc(sem("made"), 1)
        h_state(1)
        weights(H_END + 6)
        weights(H_END + 7)
        bank = claim(pe, "h_ms")[0]
        pe.wait_ge(*told("h_sq", 1))
        for h in range(HEADS):
            ins = nc.tensor.matmul(PS[:, bank + h, 0:TOK], ones[:, :], lnt[:, h, :], start=True, stop=True)
        ins.then_inc(sem("made"), 1)

        def sums(name, index, src, tiles):
            bank = claim(pe, name, index)[0]
            for t in range(tiles):
                ins = nc.tensor.matmul(PS[:, bank, 0:TOK], ones[:, :], src[:, t, :], start=(t == 0), stop=(t == tiles - 1))
            ins.then_inc(sem("made"), 1)

        weights(89)
        projected(pe, "gv")
        sums("g_mu", 0, gv, MT)
        weights(91)
        pe.wait_ge(*told("g_sq", 1))
        sums("g_var", 0, gsq, MT)
        weights(93)
        pe.wait_ge(*told("g_vn", 1))
        for c in range(2):
            transposes("g_tok", c, [(P * g, gv[:, g, c * P:c * P + P]) for g in range(MT)])
        transposes("g_tok", 2, [(P * g, gv[:, g, SEQ:TOK]) for g in range(MT)])
        weights(95)
        pe.wait_ge(*told("g_tokens", 1))
        for n in range(2):
            bank = claim(pe, "g_mix", n)[0]
            for g in range(MT):
                out = PS[:, bank, g * P:g * P + P]
                nc.tensor.matmul(out, v_tok[:, n, g * P:g * P + P], ws_t[:, g, :], start=True, stop=False)
                ins = nc.tensor.matmul(out, ones[0:1, :], bs_row[0:1, g, :], start=False, stop=True)
            ins.then_inc(sem("made"), 1)
        bank = claim(pe, "g_ms")[0]
        pe.wait_ge(*told("consts_loaded", 16 * 5))
        nc.tensor.matmul(PS[:, bank, 0:MT], ones[0:1, :], ws00[0:1, :], start=True, stop=True)
        nc.tensor.matmul(PS[:, bank, MT:2 * MT], ones[0:1, :], bs_row[0:1, :, 0], start=True,
                         stop=True).then_inc(sem("made"), 1)

        weights(97)
        pe.wait_ge(*told("f_lf", 1))
        transposes("f_lf", 0, [(0, lf_t[:, 0:P]), (4, lf_t[:, P:SEQ]), (8, lf_t[:, SEQ:TOK])])
        bank = claim(pe, "f_suf")[0]
        pe.wait_ge(*told("f_rc", 1))
        nc.tensor.matmul(PS[0:64, bank, 0:HEADS], tri[:, :], rc[:, 0, :], start=True, stop=True).then_inc(sem("made"), 1)
        weights(98)
        bank = claim(pe, "f_suft")[0]
        pe.wait_ge(*told("f_suf_in", 1))
        for h in range(HEADS):
            ins = nc.tensor.transpose(PS[:, bank, h * 64:h * 64 + 64], rc[:, :, h], ident[0:64, 0:64])
        ins.then_inc(sem("made"), 1)
        bank = claim(pe, "f_new")[0]
        pe.wait_ge(*told("f_qk", 1))
        nc.tensor.matmul(PS[0:32, bank, 0:1], small[:, 8:40], ones[:, 0:1], start=True, stop=True)
        nc.tensor.matmul(PS[0:32, bank, 1:2], cum[:, 1, 0:32], ones[0:HEADS, 0:1], start=True,
                         stop=True).then_inc(sem("made"), 1)
        bank = claim(pe, "f_sct")[0]
        pe.wait_ge(*told("f_sc", 1))
        for pg in range(N_PAGES):
            ins = nc.tensor.transpose(PS[0:32, bank + pg // 4, (pg % 4) * P:(pg % 4) * P + P], sc[:, pg, :], ident[:, :])
        ins.then_inc(sem("made"), 1)
        weights(100)
        bank = claim(pe, "f_pt")[0]
        pe.wait_ge(*told("f_prob", 1))
        for pg in range(N_PAGES):
            ins = nc.tensor.transpose(PS[:, bank, pg * 32:pg * 32 + 32], ps_row[:, pg * P:pg * P + P], ident[0:32, 0:32])
        ins.then_inc(sem("made"), 1)
        bank = claim(pe, "f_pn")[0]
        nc.tensor.matmul(PS[:, bank, 0:32], ones[0:32, :], small[0:32, 0:32], start=True, stop=True).then_inc(sem("made"), 1)
        for n in range(1, 7):
            src, c = (fk, fv)[(n - 1) // 3], (n - 1) % 3
            t = slice(c * P, c * P + P) if c < 2 else slice(SEQ, TOK)
            transposes("f_tok", n, [(P * h, src[:, h, t]) for h in range(HEADS)])
        used_values = [0]

        def values(upto):
            while used_values[0] < upto:
                b = used_values[0]
                bank = claim(pe, "f_os")[0] if b == 0 else banks("f_os", 0)[0]
                pe.wait_ge(*told("f_vsum", b + 1))
                ins = nc.tensor.matmul(PS[0:DEC, bank, :], eye8[:, b, :], vacc[:, b % 2, :], start=(b == 0), stop=(b == 7))
                ins.then_inc(sem("values_used" if b < 7 else "made"), 1)
                used_values[0] += 1

        pe.wait_ge(*told("f_cum", 1))
        for i in range(2):
            weights(104 + 16 * i)
            values(2 * i)
            bank = claim(pe, "f_s", i)[0]
            t, keys = slice(i * P, i * P + P), (i + 1) * P
            for h in range(HEADS):
                out = PS[:, bank + h // 2, (h % 2) * SEQ:(h % 2) * SEQ + keys]
                nc.tensor.matmul(out, fq[:, h, t], fk[:, h, 0:keys], start=True, stop=False)
                nc.tensor.matmul(out, cum[:, 0, t], ident[0:HEADS, h:h + 1].to_broadcast([HEADS, keys]),
                                 start=False, stop=False)
                ins = nc.tensor.matmul(out, ident[0:HEADS, h:h + 1].to_broadcast([HEADS, P]), cum[:, 1, 0:keys],
                                       start=False, stop=True)
            ins.then_inc(sem("made"), 1)
            weights(109 + 16 * i)
            values(2 * i + 1)
            pbanks = claim(pe, "f_p", i)
            pe.wait_ge(*told("f_prompt", i + 1))
            for kb in range(i + 1):
                for h in range(HEADS):
                    ins = nc.tensor.transpose(PS[:, pbanks[kb], h * P:h * P + P], s_sb[:, h, kb * P:kb * P + P], ident[:, :])
            ins.then_inc(sem("made"), 1)
            weights(114 + 16 * i)
            bank = claim(pe, "f_o", i)[0]
            pe.wait_ge(*told("f_pt_sb", i + 1))
            for h in range(HEADS):
                for kb in range(i + 1):
                    ins = nc.tensor.matmul(PS[:, bank, h * P:h * P + P], v_tok[:, kb, h * P:h * P + P],
                                           pt_sb[:, kb, h, :], start=(kb == 0), stop=(kb == i))
            ins.then_inc(sem("made"), 1)
        for b in range(3, 8):
            weights(VALUES_AT[b - 3])
            values(b + 1)
        weights(149)
        pe.wait_ge(*told("f_ostok", 1))
        transposes("f_ost", 0, [(P * h, t8[:, 0, h * P:h * P + P]) for h in range(HEADS)])
        weights(150)

        def merge(dg):
            for m, k in enumerate(MERGE_ORDER):
                if dg == 0:
                    pe.wait_ge(*told(f"branch{k}", 1))
                for half in range(2):
                    chunk(P_MERGE[dg] + 2 * m + half, 0, 1, bh[k], bl[k])

        def loop(c0, p0, turns, chunks_of, right_h, right_l, passes, part=None):
            per = passes * chunks_of
            with nc.tensor.Fori(0, turns) as i:
                for j in range(per):
                    n, p, kc = c0 + j, p0 + j // chunks_of, j % chunks_of
                    if kc == 0:
                        pe.wait_ge(*told(f"evac{p % 2}", i * (passes // 2) + p // 2))
                    if part and j < chunks_of:
                        pe.wait_ge(*part(kc))
                    pe.wait_ge(*told("lo_dve", i * per + (n - C_POOL_END + 1)))
                    products(n % RING, BANK(p), right_h, right_l, CK * kc, kc == 0, kc == chunks_of - 1)
            done[0] = c0 + turns * per

        merge(0)
        merge(1)
        for dg in (2, 3):
            loop(C_GATE[dg], P_GATE[dg], 4, 4, xh, xl, 2)
            merge(dg)
        loop(C_OUT, P_OUT, 4, 4, mh, ml, 2, lambda kc: told("merged", kc + 1))

        def layer_sums(n, acc, squares):
            pe.wait_ge(sem("acc_done"), 8 * (n + 1))
            sums("l_mu", n, acc, 2)
            bank = claim(pe, "l_var", n)[0]
            for t in range(KT):
                if t in LN_PARTS:
                    pe.wait_ge(sem(f"sq{n}"), LN_PARTS.index(t) + 1)
                ins = nc.tensor.matmul(PS[:, bank, 0:TOK], ones[:, :], squares[:, t, :], start=(t == 0), stop=(t == KT - 1))
            ins.then_inc(sem("made"), 1)

        layer_sums(0, acc0, sq)
        loop(C_UP, P_UP, UP_STEPS, 4, xh, xl, 2, lambda kc: (sem("x1_ready"), kc + 1))
        loop(C_DOWN, P_DOWN, 2, DOWN_CHUNKS, hh, hl, 4, lambda kc: (sem("hl_done"), CK * (kc + 1) // 2))
        layer_sums(1, acc1, sq2)
        for t4 in range(4):
            pe.wait_ge(*told("y_ready", t4 + 1))
            for c in range(3):
                t = slice(c * P, c * P + P) if c < 2 else slice(SEQ, TOK)
                transposes("y", 3 * t4 + c, [(P * j, yp[:, 4 * t4 + j, t]) for j in range(4)])

    @block.scalar
    def _(act):
        steps = Steps(act, sem("act_steps"), tell)
        A_ = nc.scalar.activation

        for k in range(KT):
            act.wait_ge(*made("x", k + 1))
            A_(xh[:, k, :], PS[:, 4 + k % 4, 0:TOK], ACT.Copy).then_inc(sem("xh_done"), 1)

        done = [0]

        def split(n, slot, turn, used):
            act.wait_ge(*told(f"raw{slot}", turn))
            if used is not None:
                act.wait_ge(*told("used", used))
            A_(w_hi[:, slot, :, :], raw[:, slot, :, :], ACT.Copy).then_inc(sem("hi_done"), 1)

        def high(n):
            split(n, n % RING, 16 * (n // RING + 1), n - RING + 1 if n >= RING else None)
            done[0] = n + 1

        def evacuate(p):
            src = PS[:, BANK(p):BANK(p) + 2, 0:TOK]
            if p < PASSES_A:
                act.wait_ge(*told("used", 4 * p + 4))
                name, half = targets[p]
                if name == "ff":
                    ins = A_(lf_t[:, :], PS[0:HEADS, BANK(p), 0:TOK], ACT.Copy)
                else:
                    ins = A_(where[name][:, 2 * half:2 * half + 2, :], src, functions.get(name, ACT.Copy))
            else:
                dg = 0 if p < P_GLU else 1
                m = p - P_GATE[dg]
                act.wait_ge(*told("used", C_GATE[dg] + 4 * m + 4))
                if m == 0 and dg == 0:
                    act.wait_ge(*told("h_store", 32))
                    act.wait_ge(*told("h_done", 1))
                if m == 4 and dg == 1:
                    act.wait_ge(*made("f_o", 2))
                ins = A_(gates[:, 16 * dg + 2 * m:16 * dg + 2 * m + 2, :], src, ACT.Sigmoid)
            ins.then_inc(sem(f"evac{p % 2}"), 1)

        evacuated = [0]

        def weights(upto):
            while done[0] < upto:
                high(done[0])
                behind = done[0] - RING
                p = evacuated[0]
                end = 4 * p + 4 if p < P_GLU else C_GATE[1] + 4 * (p - P_GATE[1]) + 4
                if p < P_GLU or p >= P_GATE[1]:
                    if behind >= end and p < P_MERGE[0]:
                        evacuate(p)
                        evacuated[0] += 1
                elif behind >= C_GLU + 2:
                    glu_gate()
                    evacuated[0] += 2

        def glu_gate():
            act.wait_ge(*told("g_done", 1))
            act.wait_ge(sem("fox_stored"), 16 * 6)
            for half in range(2):
                p = P_GLU + half
                act.wait_ge(*told("used", C_GLU + half + 1))
                for t in range(2):
                    ins = A_(sgl[:, 2 * half + t, :], PS[:, BANK(p) + t, 0:TOK], ACT.Sigmoid,
                             bias=vecs[:, 1, 2 * half + t:2 * half + t + 1])
                ins.then_inc(sem(f"evac{p % 2}"), 1)

        def copied(name, index, dst, src, ready=None, release=1):
            act.wait_ge(*made(name, index + 1))
            steps.then(A_(dst, src, ACT.Copy))
            tell(act, "empty_" + name, release)
            if ready:
                tell(act, ready, 1)

        weights(4)
        act.wait_ge(*made("vecs", 1))
        steps.do(A_(lnv[:, :, :].rearrange("p a b -> p (a b)"), PS[:, 6, 0:4 * KT], ACT.Copy))
        steps.tell("vecs_lnv")
        copied("vecs", 0, vecs[:, :, :].rearrange("p a b -> p (a b)"), PS[:, 6, 4 * KT:4 * KT + 5 * MT], "vecs_ready")
        act.wait_ge(*told("d_turns", 1))
        steps.do(A_(s5p[:, 9, :], s5p[:, 3, :], ACT.Sin, scale=PI_))
        steps.do(A_(s5p[:, 10, :], s5p[:, 3, :], ACT.Sin, scale=2 * PI_))
        steps.tell("a_sin")
        copied("s5_h0", 0, h0[:, :, :, :].rearrange("p r i b -> p r b i"),
               PS[:, 5, 0:256].rearrange("p (r b i) -> p r b i", r=2, i=S5_TILES), "h0_ready")
        weights(5)
        copied("s5_lam", 0, lam_t[:, :, :].rearrange("p k i -> p (k i)"), PS[:, 4, 0:96], "lam_ready")
        for r in range(2):
            copied("s5_ct", r, ct[:, r, :, :].rearrange("p q c -> p (q c)"), PS[:, (7, 5)[r], :])
        copied("g_ws", 0, ws_t[:, :, :].rearrange("p q c -> p (q c)"), PS[:, 6, :])

        def s5_table(b):
            act.wait_ge(*told("d_angle", b + 1))
            steps.do(A_(er[:, b % 2, :, :], tab[:, :, :], ACT.Sin, scale=PI_))
            steps.then(A_(ei[:, b % 2, :, :], tab[:, :, :], ACT.Sin, scale=2 * PI_))
            steps.then(A_(er[:, b % 2, :, :], er[:, b % 2, :, :], ACT.Square))
            steps.then(A_(er[:, b % 2, :, :], er[:, b % 2, :, :], ACT.Copy, scale=-2.0, bias=1.0))
            tell(act, "a_table", 1)

        weights(8)
        for r in range(2):
            copied("s5_bt", r, bt[:, r, :, :].rearrange("p q c -> p (q c)"), PS[:, 4 + r, :])
        tell(act, "s5_bt_ready", 1)
        tell(act, "s5_staged", 1)
        weights(10)
        s5_table(0)
        weights(13)
        s5_table(1)
        weights(16)
        copied("s5_bus", 0, bus[:, :, :, :].rearrange("p r (q j) b -> p j (r q) b", j=4),
               PS[:, 4:8, 0:64].rearrange("p j (m b) -> p j m b", b=DEC), "bus_ready")
        for b in range(2, 8):
            weights(S5_AT[b])
            s5_table(b)
            if b == H_SMP - 1:
                projected(act, "hf")
                steps.do(A_(kt_[:, :, :], hf[:, :, :], ACT.Sigmoid, scale=-1.0))
                steps.then(A_(small[:, 8:40].rearrange("p (h b) -> p h b", h=HEADS), hf[:, :, SEQ:TOK], ACT.Sigmoid))
                tell(act, "a_smp", 1)
            if b == H_SMP:
                weights(S5_AT[b] + 2)
                copied("h_vs", 0, t8[:, 0, :], PS[0:DEC, 7, :], "h_vs_tok")
        copied("h_os", 0, ho[:, :], PS[0:32, 7, :], "h_os_tok")
        weights(S5_AT[8] + 4)
        act.wait_ge(*told("s5_yd", 1))
        steps.then(A_(su[:, :, :], su[:, :, :], ACT.Gelu_apprx_tanh))
        steps.then(A_(gh1[:, :, :], su[:, :, :], ACT.Copy))
        tell(act, "gh_done", 1)
        so = sc[0:S5_TILES, :, :].rearrange("i a b -> i (a b)")
        copied("s5_out", 0, so, PS[0:S5_TILES, 4, 0:256])
        for r, part in enumerate(("re", "im")):
            act.dma_start(O[f"s5_{part}_prompt"][0, 0].rearrange("(i g) p -> i (g p)", g=2),
                          so[:, r * P:(r + 1) * P]).then_inc(sem("so_stored"), 16)
        copied("s5_outs", 0, s5o[:, :, :].rearrange("p r s -> p (r s)"), PS[:, 5, 0:256])
        for r, part in enumerate(("re", "im")):
            act.dma_start(O[f"s5_{part}_sample"][0].rearrange("b (i g) p -> (b i) (g p)", g=2),
                          s5o[:, r, :]).then_inc(sem("so_stored"), 16)
        weights(OUTS_AT + 4)
        steps.then(A_(lnt[:, :, :], hf[:, :, :], ACT.Abs))
        steps.then(A_(lnt[:, :, :], lnt[:, :, :], ACT.Exp, scale=-1.0))
        steps.then(A_(lnt[:, :, :], lnt[:, :, :], ACT.Ln, bias=1.0))
        tell(act, "a_ln", 1)
        weights(OUTS_AT + 5)
        copied("h_ost", 0, hos[:, :].rearrange("p (h b) -> p h b", h=HEADS),
               PS[:, 7, :].rearrange("p (h b) -> p h b", h=HEADS)[:, :, 0:DEC])
        for c in range(2):
            copied("h_v", c, v_tok[:, c, :], PS[:, 4 + c, :])
        copied("f_tok", 0, q8[:, :], PS[0:DEC, 6, :], "f_qtok")
        for n in range(NL + 2):
            if n < NL:
                if n < 2:
                    act.wait_ge(*told("d_dif", n + 1))
                else:
                    act.wait_ge(*told("p_dif", n - 1))
                d = dif[:, n % 2, :, :]
                steps.then(A_(d, d, ACT.Abs))
                steps.then(A_(d, d, ACT.Exp, scale=-1.0))
                tell(act, "a_decay", 1)
            elif n == NL:
                act.wait_ge(*told("h_qe", NL - 1))
                steps.then(A_(dif[:, NL % 2, :, :], bc[:, :, :], ACT.Exp))
                tell(act, "a_decay", 1)
            else:
                act.wait_ge(*told("d_dif", 3))
                d = dif[:, (NL + 1) % 2, :, :]
                steps.then(A_(d, d, ACT.Exp))
                tell(act, "a_decay", 1)
            weights(min(H_AT + H_GAP * n + 3, H_END + 4))
        copied("h_kd", 0, ke[:, :, :].rearrange("p (a b) c -> p a (b c)", a=2), PS[:, 4:6, :], "h_kdt")
        weights(H_END + 6)
        copied("h_s", 0, s_prev[:, 0, :, :].rearrange("p h v -> p (h v)"), PS[:, 6, :], "h_s0")
        weights(H_END + 8)
        act.wait_ge(*made("h_o", 1))
        for pair in range(2):
            steps.do(A_(hf[:, 2 * pair:2 * pair + 2, 0:SEQ], PS[:, 4 + pair, :].rearrange("p (h t) -> p h t", h=2), ACT.Copy))
        steps.tell("empty_h_o")
        weights(H_END + 10)
        steps.then(A_(hf[:, :, SEQ:TOK], hos[:, :].rearrange("p (h b) -> p h b", h=HEADS), ACT.Copy))
        steps.then(A_(lnt[:, :, :], hf[:, :, :], ACT.Square))
        tell(act, "h_sq", 1)
        weights(H_END + 12)
        act.wait_ge(*told("h_var", 1))
        steps.then(A_(lnt[:, :, :], lnt[:, :, :], ACT.Sqrt))
        tell(act, "h_rstd", 1)
        weights(H_END + 15)
        act.wait_ge(*told("h_out", 1))
        steps.then(A_(bh2[:, :, :], hf[:, :, :], ACT.Copy))
        tell(act, "bh2_done", 1)
        projected(act, "ff")
        ab = cum[:, :, :].rearrange("h a t -> h (a t)")[:, 0:TOK]
        steps.then(A_(ab, lf_t[:, :], ACT.Abs, bias=bf[:, 0:1]))
        steps.then(A_(ab, ab, ACT.Exp, scale=-1.0))
        steps.then(A_(ab, ab, ACT.Ln, bias=1.0))
        tell(act, "a_lf", 1)
        weights(93)
        act.wait_ge(*told("g_cent", 1))
        steps.then(A_(gsq[:, :, :], gv[:, :, :], ACT.Square))
        tell(act, "g_sq", 1)
        weights(95)
        act.wait_ge(*told("g_rec", 1))
        steps.then(A_(gsq[:, 0, :], gsq[:, 0, :], ACT.Sqrt))
        tell(act, "g_rstd", 1)
        weights(96)
        for c in range(2):
            copied("g_tok", c, v_tok[:, c, :], PS[:, 6 + c, :])
        act.wait_ge(sem("so_stored"), 64)
        copied("g_tok", 2, t8[:, 1, :], PS[0:DEC, 6, :], "g_tokens")
        act.dma_start(O["gmlp_v_sample"][0].rearrange("b o c -> (b o) c"), t8[:, 1, :]).then_inc(sem("t8_stored1"), 16)
        weights(99)
        act.wait_ge(*told("g_mixed", 1))
        steps.then(A_(bh3[:, :, :], gu[:, :, :], ACT.Copy))
        tell(act, "bh3_done", 1)
        act.wait_ge(*made("f_lf", 1))
        steps.do(A_(small[:, 40:48], PS[:, 6, 0:8], ACT.Copy))
        steps.then(A_(small[0:DEC, 48:52], PS[0:DEC, 6, 8:12], ACT.Copy))
        tell(act, "empty_f_lf", 1)
        act.dma_start(O["fox_logf_prompt"][0, 0].rearrange("(n p) h -> p n h", p=P),
                      small[:, 40:48].rearrange("p (n h) -> p n h", n=2)).then_inc(sem("fox_stored"), 16)
        act.dma_start(O["fox_logf_sample"][0].rearrange("b o h -> (b o) h"), small[0:DEC, 48:52]).then_inc(sem("fox_stored"), 16)
        weights(102)
        act.wait_ge(*told("f_max", 1))
        steps.do(A_(ps_row[:, :].rearrange("r (a c) -> r a c", a=2), PS[0:32, 6:8, :], ACT.Exp, bias=small[0:32, 56:57],
                    accum_out=small[0:32, 57:58]))
        steps.then(A_(small[0:32, 58:59], small[0:32, 54:55], ACT.Exp, bias=small[0:32, 55:56]))
        tell(act, "empty_f_sct", 1)
        tell(act, "f_exp", 1)
        weights(103)
        copied("f_pt", 0, ptt[:, :, :].rearrange("p a b -> p (a b)"), PS[:, 4, 0:256], "f_ptt")
        act.wait_ge(*told("f_tok_free", 1))
        for n in range(1, 7):
            name, c = ("fox_k", "fox_v")[(n - 1) // 3], (n - 1) % 3
            buf = (k_tok, v_tok)[(n - 1) // 3]
            bank = 4 + n % 2
            if c < 2:
                copied("f_tok", n, buf[:, c, :], PS[:, bank, :], "f_vtok" if n == 5 else None)
                out = O[name + "_prompt"][0, 0].rearrange("(n p) h d -> n p (h d)", p=P)[c]
                act.dma_start(out, buf[:, c, :]).then_inc(sem("fox_stored"), 16)
            else:
                act.wait_ge(*told("t8_stored1", 16 * (1 if n == 3 else 2)))
                copied("f_tok", n, t8[:, 1, :], PS[0:DEC, bank, :])
                act.dma_start(O[name + "_sample"][0].rearrange("b o h d -> (b o) (h d)"),
                              t8[:, 1, :]).then_inc(sem("t8_stored1"), 16)
        for i in range(2):
            weights(107 + 16 * i)
            act.wait_ge(*told("f_pmax", i + 1))
            keys = (i + 1) * P
            for h in range(HEADS):
                steps.do(A_(s_sb[:, h, 0:keys], s_sb[:, h, 0:keys], ACT.Exp, scale=SCALE, bias=small[:, 4 + h:5 + h],
                            accum_out=small[:, h:h + 1]))
            steps.tell("f_pexp")
            weights(111 + 16 * i)
            act.wait_ge(*made("f_p", i + 1))
            pb = banks("f_p", i)
            for kb in range(i + 1):
                steps.do(A_(pt_sb[:, kb, :, :].rearrange("p h t -> p (h t)"), PS[:, pb[kb], :], ACT.Copy))
            steps.settle()
            tell(act, "empty_f_p", 1)
            tell(act, "f_pt_sb", 1)
        weights(136)
        act.wait_ge(*told("glu_done", 1))
        steps.then(A_(gh1[:, :, :], su[:, :, :], ACT.Copy))
        tell(act, "gh_done", 1)
        weights(150)
        copied("f_os", 0, t8[:, 0, :], PS[0:DEC, 6, :], "f_ostok")
        weights(154)
        act.wait_ge(*told("f_out", 1))
        steps.then(A_(bh0[:, :, :], fq[:, :, :], ACT.Copy))
        tell(act, "bh0_done", 1)

        def merged(dg):
            act.wait_ge(*told("sums", dg + 1))
            A_(mh[:, 4 * dg:4 * dg + 4, :], gates[:, (dg % 2) * 16:(dg % 2) * 16 + 4, :], ACT.Copy).then_inc(sem("mh_done"), 1)

        def highs(n0, n1):
            for n in range(n0, n1):
                high(n)

        def loop_highs(c0, i, per, j0, j1):
            for j in range(j0, j1):
                n = c0 + j
                split(None, n % RING, i * (4 * per) + 16 * (n // RING + 1), i * per + (n - RING + 1))

        highs(154, C_MERGE[1] + 6)
        merged(0)
        highs(C_MERGE[1] + 6, C_GATE[2])
        for dg in (2, 3):
            c0, p0 = C_GATE[dg], P_GATE[dg]

            def gate_pass(i, m):
                p = p0 + m
                act.wait_ge(*told("used", i * 8 + (c0 + 4 * m + 4)))
                dst = gates[:, ds(i * 4 + ((dg % 2) * 16 + 2 * m), 2), :]
                A_(dst, PS[:, BANK(p):BANK(p) + 2, 0:TOK], ACT.Sigmoid).then_inc(sem(f"evac{p % 2}"), 1)

            highs(c0, c0 + 4)
            merged(dg - 1)
            highs(c0 + 4, c0 + 8)
            act.wait_ge(*told("ml_done", dg - 1))
            act.wait_ge(*told("used", c0 + 4))
            A_(gates[:, (dg % 2) * 16:(dg % 2) * 16 + 2, :], PS[:, BANK(p0):BANK(p0) + 2, 0:TOK],
               ACT.Sigmoid).then_inc(sem(f"evac{p0 % 2}"), 1)
            with nc.scalar.Fori(1, 4) as i:
                loop_highs(c0, i, 8, 0, 4)
                gate_pass(i - 1, 1)
                loop_highs(c0, i, 8, 4, 8)
                gate_pass(i, 0)
            highs(C_MERGE[dg], C_MERGE[dg] + 4)
            act.wait_ge(*told("used", C_MERGE[dg]))
            A_(gates[:, (dg % 2) * 16 + 14:(dg % 2) * 16 + 16, :], PS[:, BANK(p0 + 7):BANK(p0 + 7) + 2, 0:TOK],
               ACT.Sigmoid).then_inc(sem(f"evac{(p0 + 7) % 2}"), 1)
            highs(C_MERGE[dg] + 4, C_MERGE[dg] + 8)
        highs(C_OUT, C_OUT + 4)
        merged(3)
        highs(C_OUT + 4, C_OUT + 8)
        with nc.scalar.Fori(1, 4) as i:
            loop_highs(C_OUT, i, 8, 0, 8)
        highs(C_UP, C_UP + 4)

        def squares(n, src, dst):
            A_(small[:, 63:64], ones[:, 0:1], ACT.Sqrt).then_inc(sem("sqrt_loaded"), 1)
            for m, (a, b) in enumerate(zip(LN_PARTS, LN_PARTS[1:] + [KT])):
                act.wait_ge(*told(f"centred{n}", m + 1))
                A_(dst[:, a:b, :], src[:, a:b, :], ACT.Square).then_inc(sem(f"sq{n}"), 1)
            act.wait_ge(*made("l_var", n + 1))
            A_(mu_r[:, 1, :], PS[:, 5 + 2 * n, 0:TOK], ACT.Sqrt, scale=1.0 / D_MODEL,
               bias=small[:, 62:63]).then_inc(sem(f"deviation{n}"), 1)

        squares(0, xp, sq)
        for t in range(KT):
            act.wait_ge(*told("x1_norm", t // 4 + 1))
            ins = A_(xh[:, t, :], xp[:, t, :], ACT.Identity, scale=lnv[:, 0, t:t + 1], bias=lnv[:, 1, t:t + 1])
            if t % 4 == 3:
                ins.then_inc(sem("x1_hi"), 1)

        bank_g = BANK(P_UP)

        def silu(i):
            act.wait_ge(*told("used", i * 8 + (C_UP + 4)))
            A_(sg[:, :, :], PS[:, bank_g:bank_g + 2, 0:TOK], ACT.Silu).then_inc(sem(f"evac{P_UP % 2}"), 1)

        def h_high(i):
            act.wait_ge(sem(f"evac{(P_UP + 1) % 2}"), i + ((P_UP + 1) // 2 + 1))
            A_(hh[:, ds(i * 2, 2), :], hx[:, :, :], ACT.Copy).then_inc(sem("hh_done"), 1)

        highs(C_UP + 4, C_UP + 8)
        silu(0)
        with nc.scalar.Fori(1, UP_STEPS) as i:
            loop_highs(C_UP, i, 8, 0, 6)
            h_high(i - 1)
            loop_highs(C_UP, i, 8, 6, 8)
            silu(i)
        highs(C_DOWN, C_DOWN + 4)
        act.wait_ge(sem(f"evac{(P_UP + 1) % 2}"), (UP_STEPS - 1) + ((P_UP + 1) // 2 + 1))
        A_(hh[:, 2 * UP_STEPS - 2:2 * UP_STEPS, :], hx[:, :, :], ACT.Copy).then_inc(sem("hh_done"), 1)
        highs(C_DOWN + 4, C_DOWN + 44)
        with nc.scalar.Fori(1, 2) as i:
            loop_highs(C_DOWN, i, 44, 0, 44)
        squares(1, yp, sq2)
        for n in range(12):
            act.wait_ge(*made("y", n + 1))
            t4, c = n // 3, n % 3
            dst = y_tok[:, c, t4 * 512:(t4 + 1) * 512] if c < 2 else ys_tok[:, t4 * 512:(t4 + 1) * 512]
            src = PS[:, 4 + n % 4, :] if c < 2 else PS[0:DEC, 4 + n % 4, :]
            steps.then(A_(dst, src, ACT.Copy))
            tell(act, "empty_y", 1)
            tell(act, "y_copied", 1)
        act.wait_ge(*told("so_stored", 64))
        act.wait_ge(*told("t8_stored1", 16 * 3))
        act.wait_ge(*told("fox_stored", 16 * 6))

    @block.vector
    def _(dve):
        V = nc.vector
        steps = Steps(dve, sem("dve_steps"), tell)
        do, then = steps.do, steps.then

        for k in range(KT):
            dve.wait_ge(*told("xh_done", k + 1))
            V.tensor_tensor(xl[:, k, :], PS[:, 4 + k % 4, 0:TOK], xh[:, k, :], ALU.subtract).then_inc(sem("x_split"), 1)
            dve.wait_ge(*told("x_split", k + 1))
            tell(dve, "empty_x", 1)

        S = lambda n: s5p[:, n, :]

        def exp_(dst, x, k, r):
            then(V.tensor_scalar(x, x, -87.0, 88.0, ALU.max, ALU.min))
            then(V.tensor_scalar(k, x, 1.0 / math.log(2.0), ROUND, ALU.mult, ALU.add))
            then(V.tensor_scalar(k, k, ROUND, None, ALU.subtract))
            then(V.scalar_tensor_tensor(r, k, -LN2_HIGH, x, ALU.mult, ALU.add))
            then(V.scalar_tensor_tensor(r, k, -LN2_LOW, r, ALU.mult, ALU.add))
            then(V.tensor_scalar(dst, r, 1.0 / 5040, None, ALU.mult))
            for c in (1.0 / 720, 1.0 / 120, 1.0 / 24, 1.0 / 6, 0.5, 1.0):
                then(V.scalar_tensor_tensor(dst, dst, c, r, ALU.add, ALU.mult))
            then(V.tensor_scalar(r.bitcast(I32), k, 127.0, 8388608.0, ALU.add, ALU.mult))
            then(V.scalar_tensor_tensor(dst, dst, 1.0, r, ALU.add, ALU.mult))

        dve.wait_ge(*told("s5_loaded", 16 * 9))
        exp_(s5p[:, 9, 0:2], dt2[:, :], s5p[:, 10, 0:2], s5p[:, 11, 0:2])
        step = s5p[:, 9, 0:2].unsqueeze(2).to_broadcast([S5_TILES, 2, 64])
        g2 = lambda n: s5p[:, n, :].rearrange("i (g p) -> i g p", g=2)
        do(V.tensor_tensor(g2(8), g2(0), step, ALU.mult))
        then(V.tensor_tensor(g2(3), g2(1), step, ALU.mult))
        then(V.tensor_scalar(S(11), S(3), 1.0 / (2 * math.pi), ROUND, ALU.mult, ALU.add))
        then(V.tensor_scalar(S(11), S(11), ROUND, None, ALU.subtract))
        then(V.scalar_tensor_tensor(S(3), S(11), -6.28125, S(3), ALU.mult, ALU.add))
        then(V.scalar_tensor_tensor(S(3), S(11), 6.28125 - 2 * math.pi, S(3), ALU.mult, ALU.add))
        then(V.tensor_scalar(S(3), S(3), 1.0 / (2 * math.pi), None, ALU.mult))
        do(V.tensor_scalar(S(3), S(3), 0.5, -0.5, ALU.min, ALU.max))
        steps.settle()
        tell(dve, "d_turns", 1)
        exp_(S(2), S(8), S(13), S(14))
        do(V.tensor_tensor(S(12), S(0), S(0), ALU.mult))
        then(V.tensor_tensor(S(13), S(1), S(1), ALU.mult))
        then(V.tensor_tensor(S(12), S(12), S(13), ALU.add))
        do(V.reciprocal(S(12), S(12)))
        dve.wait_ge(*told("a_sin", 1))
        then(V.tensor_tensor(S(9), S(9), S(9), ALU.mult))
        then(V.tensor_scalar(S(9), S(9), -2.0, 1.0, ALU.mult, ALU.add))
        do(V.tensor_tensor(S(4), S(2), S(9), ALU.mult))
        then(V.tensor_tensor(S(5), S(2), S(10), ALU.mult))
        then(V.tensor_scalar(S(9), S(4), 1.0, None, ALU.subtract))
        do(V.tensor_tensor(S(13), S(9), S(0), ALU.mult))
        do(V.tensor_tensor(S(14), S(5), S(1), ALU.mult))
        do(V.tensor_tensor(S(15), S(5), S(0), ALU.mult))
        then(V.tensor_tensor(S(11), S(9), S(1), ALU.mult))
        do(V.tensor_tensor(S(13), S(13), S(14), ALU.add))
        then(V.tensor_tensor(S(15), S(15), S(11), ALU.subtract))
        do(V.tensor_tensor(S(6), S(13), S(12), ALU.mult))
        do(V.tensor_tensor(S(7), S(15), S(12), ALU.mult))
        steps.tell("s5_par")
        dve.wait_ge(*told("consts_ready", 1))
        parity = small[:, 1:2].bitcast(I32)
        then(V.tensor_scalar(parity, small[:, 0:1].bitcast(I32), 4, 1, ALU.arith_shift_right, ALU.bitwise_and))
        then(V.tensor_copy(par[:, 1:2], parity))
        then(V.tensor_scalar(par[:, 0:1], par[:, 1:2], -1.0, 1.0, ALU.mult, ALU.add))
        dve.wait_ge(*told("s5_loaded", 16 * 9))
        for r in range(2):
            for g in range(2):
                do(V.tensor_scalar(cd[:, r, :, g, :], cn[:, r, :, :], par[:, g:g + 1], (1.0, -1.0)[r], ALU.mult, ALU.mult))
        steps.tell("s5_cd")
        t_s, s_s = level_mask[:, 0, :], level_mask[:, 1, :]
        then(V.tensor_tensor(level_mask[:, 2, :], t_s, s_s, ALU.bitwise_xor))
        then(V.tensor_tensor(level_mask[:, 3, :], t_s, s_s, ALU.is_gt))
        then(V.tensor_tensor(level_mask[:, NL, :], level_mask[:, 2, :], level_mask[:, 3, :], ALU.mult))
        for n, b in enumerate(HGRN_LEVELS):
            do(V.tensor_scalar(level_mask[:, n, :], level_mask[:, NL, :], b, None, ALU.is_ge))
        steps.settle()
        for n in range(NL - 1, 0, -1):
            then(V.tensor_tensor(level_mask[:, n, :], level_mask[:, n, :], level_mask[:, n - 1, :], ALU.subtract))
        then(V.tensor_copy(level_mask[:, NL, :], ident[:, :]))
        dve.wait_ge(*told("lam_ready", 1))
        co = [lam_t[:, 4 + r, :].unsqueeze(2).to_broadcast([P, S5_TILES, 16]) for r in range(2)]
        t1 = tab[:, 0, :].rearrange("p (i h) -> p i h", h=16)
        t2 = tab[:, 1, :].rearrange("p (i h) -> p i h", h=16)
        for r in range(2):
            do(V.tensor_tensor(t1, bn[:, r, :, :], co[0], ALU.mult))
            then(V.tensor_tensor(t2, bn[:, 1 - r, :, :], co[1], ALU.mult))
            for g in range(2):
                half = slice(64 * g, 64 * g + 64)
                do(V.tensor_tensor(bd[half, r, :, g, :], t1[half], t2[half], (ALU.subtract, ALU.add)[r]))
            steps.settle()
        tell(dve, "s5_bd", 1)

        def s5_angle(b):
            if b:
                dve.wait_ge(*told("a_table", b))
            two = slice(2 * b, 2 * b + 2)
            then(V.tensor_tensor(tab[:, :, :].rearrange("p t (a b) -> p t a b", b=16),
                                 rot_a[:, two, :].unsqueeze(3).to_broadcast([P, 2, 16, 16]),
                                 rot_b[:, two, :].unsqueeze(2).to_broadcast([P, 2, 16, 16]), ALU.add))
            then(V.tensor_scalar(rnd[:, :, :], tab[:, :, :], ROUND, ROUND, ALU.add, ALU.subtract))
            then(V.tensor_tensor(tab[:, :, :], tab[:, :, :], rnd[:, :, :], ALU.subtract))
            tell(dve, "d_angle", 1)

        wide = rnd[:, 0, :].rearrange("p (i a) -> p i a", a=16)
        for rot, factor in ((rot_b, 1.0), (rot_a, 16.0)):
            turns = rnd[:, 1, 0:S5_TILES]
            then(V.tensor_scalar(turns, lam_t[:, 1, :], factor, None, ALU.mult))
            then(V.tensor_scalar(wide[:, :, 0], turns, ROUND, ROUND, ALU.add, ALU.subtract))
            then(V.tensor_tensor(turns, turns, wide[:, :, 0], ALU.subtract))
            then(V.tensor_tensor(rot[:, :, :], iota16[:, :].unsqueeze(1).to_broadcast([P, S5_TILES, 16]),
                                 turns.unsqueeze(2).to_broadcast([P, S5_TILES, 16]), ALU.mult))
            then(V.tensor_scalar(wide, rot[:, :, :], ROUND, ROUND, ALU.add, ALU.subtract))
            then(V.tensor_tensor(rot[:, :, :], rot[:, :, :], wide, ALU.subtract))
        s5_angle(0)
        s5_angle(1)
        dve.wait_ge(*told("bus_ready", 1))
        dve.wait_ge(*told("h0_ready", 1))
        ab = [lam_t[:, 2 + r, :].unsqueeze(2).to_broadcast([P, S5_TILES, DEC]) for r in range(2)]
        t1 = gr[:, 0, 0:P].rearrange("p (i b) -> p i b", b=DEC)
        t2 = gr[:, 0, P:2 * P].rearrange("p (i b) -> p i b", b=DEC)
        for r in range(2):
            do(V.tensor_tensor(t1, h0[:, r, :, :], ab[0], ALU.mult))
            then(V.tensor_tensor(t2, h0[:, 1 - r, :, :], ab[1], ALU.mult))
            then(V.tensor_tensor(t1, t1, t2, (ALU.subtract, ALU.add)[r]))
            then(V.tensor_tensor(hs[:, r, :, :].rearrange("p b i -> p i b"), t1, bus[:, r, :, :], ALU.add))
        tell(dve, "s5_hs", 1)
        dve.wait_ge(*told("vecs_ready", 1))
        projected(dve, "su")
        states = s_smp[:, :, :].rearrange("p (b h) v -> p b h v", h=HEADS)

        def h_samples_decay():
            dve.wait_ge(*told("s_smp", 16 * DEC))
            dve.wait_ge(*told("a_smp", 1))
            for h in range(HEADS):
                do(V.tensor_tensor(states[:, :, h, :], states[:, :, h, :],
                                   small[:, 8 + 8 * h:16 + 8 * h].unsqueeze(2).to_broadcast([P, DEC, P]), ALU.mult))
            steps.settle()

        def h_samples():
            for b in range(DEC):
                dve.wait_ge(*made("h_vb", b + 1))
                for h in range(HEADS):
                    do(V.scalar_tensor_tensor(s_smp[:, 4 * b + h, :], PS[:, 4 + b % 2, h * P:h * P + P],
                                              kt_[:, h, SEQ + b:SEQ + b + 1], s_smp[:, 4 * b + h, :], ALU.mult, ALU.add))
                steps.settle()
                tell(dve, "empty_h_vb", 1)
            projected(dve, "hq")
            for h in range(HEADS):
                do(V.tensor_tensor(qm[:, :, h, :], hq[:, h, SEQ:TOK].unsqueeze(2).to_broadcast([P, DEC, DEC]),
                                   eye8[:, :, :], ALU.mult))
            steps.settle()
            tell(dve, "h_smp_done", 1)

        def s5_output(q):
            dve.wait_ge(*made("s5_y", 2 * q + 2))
            then(V.scalar_tensor_tensor(su[:, q, :], su[:, q, :], vecs[:, 0, q:q + 1], PS[:, 6 + q % 2, 0:TOK],
                                        ALU.mult, ALU.add))
            tell(dve, "empty_s5_y", 2)

        for b in range(8):
            dve.wait_ge(*told("a_table", b + 1))
            c_, s_ = er[:, b % 2, :, :], ei[:, b % 2, :, :]
            dve.wait_ge(*made("s5_bu", b + 1))
            br, bi = PS[:, 4:6, 0:SEQ], PS[:, 4:6, SEQ:2 * SEQ]
            hr_, hm_ = hr[:, :, 0:SEQ], hm[:, :, 0:SEQ]
            t1, t2 = rnd[:, :, :], tmp2[:, :, :]
            do(V.tensor_tensor(gr[:, :, :], c_, br, ALU.mult))
            do(V.tensor_tensor(t1, s_, bi, ALU.mult))
            do(V.tensor_tensor(gi[:, :, :], c_, bi, ALU.mult))
            then(V.tensor_tensor(t2, s_, br, ALU.mult))
            tell(dve, "empty_s5_bu", 1)
            do(V.tensor_tensor(gr[:, :, :], gr[:, :, :], t1, ALU.add))
            then(V.tensor_tensor(gi[:, :, :], gi[:, :, :], t2, ALU.subtract))
            for t in range(2):
                mag = lam_t[:, 0, 2 * b + t:2 * b + t + 1].to_broadcast([P, SEQ])
                do(V.tensor_tensor_scan(gr[:, t, :], mag, gr[:, t, :], 0.0, ALU.mult, ALU.add))
                do(V.tensor_tensor_scan(gi[:, t, :], mag, gi[:, t, :], 0.0, ALU.mult, ALU.add))
            steps.settle()
            if b:
                dve.wait_ge(*made("s5_y", b))
            do(V.tensor_tensor(hr_, c_, gr[:, :, :], ALU.mult))
            do(V.tensor_tensor(t1, s_, gi[:, :, :], ALU.mult))
            do(V.tensor_tensor(gi[:, :, :], c_, gi[:, :, :], ALU.mult))
            then(V.tensor_tensor(gr[:, :, :], s_, gr[:, :, :], ALU.mult))
            do(V.tensor_tensor(hr_, hr_, t1, ALU.subtract))
            do(V.tensor_tensor(hm_, gi[:, :, :], gr[:, :, :], ALU.add))
            do(V.tensor_copy(hr[:, :, SEQ:TOK], hs[:, 0, :, 2 * b:2 * b + 2].rearrange("p b i -> p i b")))
            then(V.tensor_copy(hm[:, :, SEQ:TOK], hs[:, 1, :, 2 * b:2 * b + 2].rearrange("p b i -> p i b")))
            tell(dve, "s5_h", 1)
            do(V.tensor_copy(sf[:, 0, 2 * b:2 * b + 2], hr[:, :, SEQ - 1]))
            do(V.tensor_copy(sf[:, 1, 2 * b:2 * b + 2], hm[:, :, SEQ - 1]))
            if b + 2 < 8:
                s5_angle(b + 2)
            if b == H_SMP - 1:
                h_samples_decay()
            if b == H_SMP:
                h_samples()
            if b and b % 2 == 0:
                s5_output(b // 2 - 1)
        steps.tell("s5_sf")
        s5_output(3)
        tell(dve, "s5_yd", 1)
        dve.wait_ge(*told("gh_done", 1))
        then(V.tensor_tensor(gl1[:, :, :], su[:, :, :], gh1[:, :, :], ALU.subtract))
        tell(dve, "g_split", 1)

        dve.wait_ge(*told("a_ln", 1))
        do(V.tensor_scalar(hf[:, :, :], hf[:, :, :], 0.0, None, ALU.min))
        steps.settle()
        then(V.tensor_tensor(hf[:, :, :], hf[:, :, :], lnt[:, :, :], ALU.subtract))
        tell(dve, "d_lf", 1)
        for hc in range(8):
            h, c = hc // 2, hc % 2
            do(V.tensor_tensor_scan(bc[:, hc, :], ones[:, :], hf[:, h, c * P:c * P + P], 0.0, ALU.mult, ALU.add))
        then(V.memset(att[:, :, :], 0.0))
        projected(dve, "hq")
        heads = lambda t: t.rearrange("p (h c) s -> p h (c s)", h=HEADS)

        def h_dif(n):
            then(V.tensor_tensor(*distances(n), ALU.subtract))
            tell(dve, "d_dif", 1)

        def keys_half(n):
            b = n // 2
            if n % 2 == 0:
                dve.wait_ge(*made("f_qb", b + 1))
            dve.wait_ge(sem(f"kv{n % 2}"), 64 * (n // 2 + 1))
            half = kv[:, n % 2, :, :]
            then(V.tensor_tensor(half, half, PS[:, 6 + b % 2, :].unsqueeze(1).to_broadcast([P, 4, MIX]), ALU.mult))
            if n % 2 == 1:
                tell(dve, "empty_f_qb", 1)
            then(V.tensor_reduce(sc[:, 4 * (n % 2):4 * (n % 2) + 4, 4 * b:4 * b + 4],
                                 half.rearrange("p j (h d) -> p j h d", h=HEADS), AX.X, ALU.add))
            tell(dve, "kv_free", 1)

        h_dif(0)
        h_dif(1)
        for n in range(NL):
            dve.wait_ge(*told("a_decay", n + 1))
            if n:
                dve.wait_ge(*made("h_att", n))
            d = heads(dif[:, n % 2, :, :])
            do(V.tensor_tensor(heads(qe[:, :, :]), d, hq[:, :, 0:SEQ], ALU.mult))
            then(V.tensor_tensor(heads(ke[:, :, :]), d, kt_[:, :, 0:SEQ], ALU.mult))
            tell(dve, "h_qe", 1)
            if n + 2 == NL + 1:
                h_dif(n + 2)
            if n == 0:
                dve.wait_ge(sem("so_stored"), 64)
            keys_half(2 * n)
            dve.wait_ge(*made("h_att", n + 1))
            bank = banks("h_att", n)[0]
            for part in range(2):
                mask = level_mask[:, n, :].unsqueeze(1).to_broadcast([P, 4, P])
                data = PS[:, bank + part, :].rearrange("p (a t) -> p a t", a=4)
                do(V.copy_predicated(att[:, 4 * part:4 * part + 4, :], mask, data))
            steps.settle()
            tell(dve, "empty_h_att", 1)
            keys_half(2 * n + 1)
        dve.wait_ge(*told("a_decay", NL + 1))
        eb = dif[:, NL % 2, :, :]
        do(V.tensor_tensor(qb_h[:, :, :], eb.rearrange("p (h c) s -> p h c s", h=HEADS)[:, :, 1, :], hq[:, :, P:SEQ], ALU.mult))
        do(V.tensor_copy(small[:, 2:6], eb.rearrange("p (h c) s -> p h c s", h=HEADS)[:, :, 1, P - 1]))
        dve.wait_ge(*made("h_att", NL + 1))
        bank = banks("h_att", NL)[0]
        for part in range(2):
            mask = level_mask[:, NL, :].unsqueeze(1).to_broadcast([P, 4, P])
            do(V.copy_predicated(att[:, 4 * part:4 * part + 4, :], mask, PS[:, bank + part, :].rearrange("p (a t) -> p a t", a=4)))
        steps.settle()
        tell(dve, "empty_h_att", 1)
        tell(dve, "h_att_done", 1)
        dve.wait_ge(*told("a_decay", NL + 2))
        then(V.tensor_tensor(heads(qe[:, :, :]), heads(dif[:, (NL + 1) % 2, :, :]), kt_[:, :, 0:SEQ], ALU.mult))
        tell(dve, "h_kd", 1)
        keys_half(14)
        keys_half(15)
        dve.wait_ge(*told("h_s0", 1))
        dve.wait_ge(*made("h_last", 1))
        for h in range(HEADS):
            do(V.scalar_tensor_tensor(s_prev[:, 1, h, :], s_prev[:, 0, h, :], small[:, 2 + h:3 + h],
                                      PS[:, 7, h * P:h * P + P], ALU.mult, ALU.add))
        steps.settle()
        tell(dve, "empty_h_last", 1)
        dve.wait_ge(*made("h_ms", 1))
        then(V.tensor_scalar(lnt[:, :, :], PS[:, 4:8, 0:TOK], 1.0 / P, RMS_EPS, ALU.mult, ALU.add))
        tell(dve, "empty_h_ms", 1)
        then(V.reciprocal(lnt[:, :, :], lnt[:, :, :]))
        tell(dve, "h_var", 1)
        projected(dve, "hg")
        dve.wait_ge(*told("h_rstd", 1))
        then(V.tensor_tensor(hf[:, :, :], hf[:, :, :], lnt[:, :, :], ALU.mult))
        then(V.tensor_tensor(hf[:, :, :], hf[:, :, :], vecs[:, 2, :].unsqueeze(2).to_broadcast([P, MT, TOK]), ALU.mult))
        then(V.tensor_tensor(hf[:, :, :], hf[:, :, :], hg[:, :, :], ALU.mult))
        tell(dve, "h_out", 1)
        dve.wait_ge(*told("bh2_done", 1))
        then(V.tensor_tensor(bl2[:, :, :], hf[:, :, :], bh2[:, :, :], ALU.subtract))
        tell(dve, "branch2", 1)
        tell(dve, "h_done", 2)

        projected(dve, "gv")
        projected(dve, "gu")
        dve.wait_ge(*made("g_mu", 1))
        then(V.tensor_scalar(gsq[:, 0, :], PS[:, 4, 0:TOK], 1.0 / MIX, None, ALU.mult))
        tell(dve, "empty_g_mu", 1)
        then(V.tensor_tensor(gv[:, :, :], gv[:, :, :], gsq[:, 0:1, :].to_broadcast([P, MT, TOK]), ALU.subtract))
        tell(dve, "g_cent", 1)
        dve.wait_ge(*told("a_lf", 1))
        ab = cum[:, :, :].rearrange("h a t -> h (a t)")[:, 0:TOK]
        then(V.tensor_scalar(lf_t[:, :], lf_t[:, :], bf[:, 0:1], 0.0, ALU.add, ALU.min))
        then(V.tensor_tensor(lf_t[:, :], lf_t[:, :], ab, ALU.subtract))
        tell(dve, "f_lf", 1)
        dve.wait_ge(*made("g_var", 1))
        then(V.tensor_scalar(gsq[:, 0, :], PS[:, 5, 0:TOK], 1.0 / MIX, LN_EPS, ALU.mult, ALU.add))
        tell(dve, "empty_g_var", 1)
        then(V.reciprocal(gsq[:, 0, :], gsq[:, 0, :]))
        tell(dve, "g_rec", 1)
        dve.wait_ge(*told("g_rstd", 1))
        then(V.tensor_tensor(gv[:, :, :], gv[:, :, :], gsq[:, 0:1, :].to_broadcast([P, MT, TOK]), ALU.mult))
        for t in range(MT):
            do(V.tensor_scalar(gv[:, t, :], gv[:, t, :], vecs[:, 3, t:t + 1], vecs[:, 4, t:t + 1], ALU.mult, ALU.add))
        steps.tell("g_vn")
        for n in range(2):
            dve.wait_ge(*made("g_mix", n + 1))
            then(V.tensor_tensor(gu[:, :, n * P:n * P + P], gu[:, :, n * P:n * P + P],
                                 PS[:, 4 + n, :].rearrange("p (g t) -> p g t", g=MT), ALU.mult))
            tell(dve, "empty_g_mix", 1)
        dve.wait_ge(*made("g_ms", 1))
        t1 = gsq[:, 1, 0:32].rearrange("p (g b) -> p g b", g=MT)
        then(V.tensor_tensor(t1, gv[:, :, SEQ:TOK], PS[:, 6, 0:MT].unsqueeze(2).to_broadcast([P, MT, DEC]), ALU.mult))
        then(V.tensor_tensor(t1, t1, PS[:, 6, MT:2 * MT].unsqueeze(2).to_broadcast([P, MT, DEC]), ALU.add))
        tell(dve, "empty_g_ms", 1)
        then(V.tensor_tensor(gu[:, :, SEQ:TOK], gu[:, :, SEQ:TOK], t1, ALU.mult))
        tell(dve, "g_mixed", 1)
        dve.wait_ge(*told("bh3_done", 1))
        then(V.tensor_tensor(bl3[:, :, :], gu[:, :, :], bh3[:, :, :], ALU.subtract))
        tell(dve, "branch3", 1)
        tell(dve, "g_done", 1)

        dve.wait_ge(*told("lfp", 16))
        for h in range(HEADS):
            do(V.tensor_tensor_scan(rc[:, ::-1, h], ones[0:64, :], lfp[:, ::-1, h], 0.0, ALU.mult, ALU.add))
        steps.tell("f_rc")
        dve.wait_ge(*made("f_suf", 1))
        then(V.tensor_tensor(rc[:, :, :], rc[:, :, :], lfp[:, :, :], ALU.subtract))
        then(V.tensor_tensor(rc[:, :, :], rc[:, :, :], PS[0:64, 7, 0:HEADS].unsqueeze(1).to_broadcast([64, PAGE, HEADS]), ALU.add))
        tell(dve, "empty_f_suf", 1)
        tell(dve, "f_suf_in", 1)
        projected(dve, "fq")
        projected(dve, "fk")
        do(V.tensor_tensor(small[:, 8:40].rearrange("p (b h) -> p h b", h=HEADS), fq[:, :, SEQ:TOK], fk[:, :, SEQ:TOK], ALU.mult))
        do(V.tensor_tensor(cum[:, 1, 0:32].rearrange("k (b h) -> k b h", h=HEADS),
                           lf_t[:, SEQ:TOK].unsqueeze(2).to_broadcast([HEADS, DEC, HEADS]),
                           ident[0:HEADS, 0:HEADS].unsqueeze(1).to_broadcast([HEADS, DEC, HEADS]), ALU.mult))
        steps.tell("f_qk")
        then(V.tensor_scalar(sc[:, :, :], sc[:, :, :], SCALE, None, ALU.mult))
        dve.wait_ge(*made("f_suft", 1))
        for h in range(HEADS):
            do(V.tensor_tensor(sc[:, :, h::HEADS], sc[:, :, h::HEADS],
                               PS[:, 6, h * 64:h * 64 + 64].rearrange("p (b g) -> p g b", g=N_PAGES), ALU.add))
        steps.settle()
        tell(dve, "empty_f_suft", 1)
        tell(dve, "f_sc", 1)
        col = lambda n: small[0:32, n:n + 1]
        dve.wait_ge(*made("f_new", 1))
        do(V.tensor_scalar(col(54), PS[0:32, 5, 0:1], SCALE, None, ALU.mult))
        then(V.tensor_copy(col(53), PS[0:32, 5, 1:2]))
        tell(dve, "empty_f_new", 1)
        dve.wait_ge(*made("f_sct", 1))
        then(V.tensor_reduce(col(60), PS[0:32, 6:8, :], AX.XY, ALU.max))
        then(V.tensor_tensor(col(60), col(60), col(53), ALU.add))
        then(V.tensor_tensor(col(60), col(60), col(54), ALU.max))
        do(V.tensor_tensor(col(56), col(53), col(60), ALU.subtract))
        then(V.tensor_scalar(col(55), col(60), -1.0, None, ALU.mult))
        tell(dve, "f_max", 1)
        dve.wait_ge(*told("f_exp", 1))
        then(V.tensor_tensor(col(60), col(57), col(58), ALU.add))
        then(V.reciprocal(col(60), col(60)))
        do(V.tensor_scalar(ps_row[:, :], ps_row[:, :], col(60), None, ALU.mult))
        then(V.tensor_tensor(col(58), col(58), col(60), ALU.mult))
        then(V.tensor_scalar(small[0:32, 0:32], ident[0:32, 0:32], col(58), None, ALU.mult))
        tell(dve, "f_prob", 1)
        tell(dve, "f_tok_free", 1)
        projected(dve, "fv")
        dve.wait_ge(*made("f_pn", 1))
        new = osmp[:, :].rearrange("p (h b) -> p h b", h=HEADS)
        dve.wait_ge(*made("f_pt", 1))
        then(V.tensor_tensor(new, fv[:, :, SEQ:TOK], PS[:, 5, 0:32].rearrange("p (b h) -> p h b", h=HEADS), ALU.mult))
        tell(dve, "empty_f_pn", 1)
        dve.wait_ge(*told("mlp_ready", 1))
        then(V.tensor_tensor_scan(cum[:, 0, :], ones[0:HEADS, 0:1].to_broadcast([HEADS, SEQ]),
                                  lf_t[:, 0:SEQ], 0.0, ALU.mult, ALU.add))
        do(V.tensor_scalar(cum[:, 1, :], cum[:, 0, :], -1.0 / SCALE, None, ALU.mult))
        steps.settle()
        then(V.tensor_scalar(cum[:, 0, :], cum[:, 0, :], 1.0 / SCALE, None, ALU.mult))
        tell(dve, "f_cum", 1)

        def values_half(n):
            b, half = n // 2, n % 2
            if n == 0:
                dve.wait_ge(*told("f_ptt", 1))
            dve.wait_ge(sem(f"kv{half}"), 64 * (8 + b + 1))
            v = kv[:, half, :, :]
            w = ptt[:, 4 * half:4 * half + 4, 4 * b:4 * b + 4].unsqueeze(3).to_broadcast([P, 4, HEADS, P])
            vh = v.rearrange("p j (h d) -> p j h d", h=HEADS)
            then(V.tensor_tensor(vh, vh, w, ALU.mult))
            then(V.tensor_tensor(v[:, 0:2, :], v[:, 0:2, :], v[:, 2:4, :], ALU.add))
            acc = vacc[:, b % 2, :]
            if half == 0:
                if b >= 2:
                    dve.wait_ge(sem("values_used"), b - 1)
                then(V.tensor_tensor(acc, v[:, 0, :], v[:, 1, :], ALU.add))
            else:
                then(V.tensor_tensor(v[:, 0, :], v[:, 0, :], v[:, 1, :], ALU.add))
                then(V.tensor_tensor(acc, acc, v[:, 0, :], ALU.add))
            if n < 14:
                tell(dve, "kv_free", 1)
            if half:
                tell(dve, "f_vsum", 1)

        for i in range(2):
            keys = (i + 1) * P
            values_half(4 * i)
            values_half(4 * i + 1)
            dve.wait_ge(*made("f_s", i + 1))
            b0 = banks("f_s", i)[0]
            src = lambda a, c: PS[:, b0:b0 + 2, :].rearrange("p n (h k) -> p (n h) k", h=2)[:, :, a:c]
            if i:
                dve.wait_ge(*made("f_p", 1))
                do(V.tensor_copy(s_sb[:, :, 0:P], src(0, P)))
            else:
                dve.wait_ge(*made("f_pt", 1))
            then(V.tensor_tensor(s_sb[:, :, keys - P:keys], src(keys - P, keys),
                                 causal[:, :].unsqueeze(1).to_broadcast([P, HEADS, P]), ALU.add))
            tell(dve, "empty_f_s", 1)
            then(V.tensor_reduce(small[:, 8:12], s_sb[:, :, 0:keys], AX.X, ALU.max))
            then(V.tensor_scalar(small[:, 4:8], small[:, 8:12], -SCALE, None, ALU.mult))
            tell(dve, "f_pmax", 1)
            values_half(4 * i + 2)
            dve.wait_ge(*told("f_pexp", i + 1))
            then(V.reciprocal(small[:, 0:4], small[:, 0:4]))
            then(V.tensor_tensor(s_sb[:, :, 0:keys], s_sb[:, :, 0:keys],
                                 small[:, 0:4].unsqueeze(2).to_broadcast([P, HEADS, keys]), ALU.mult))
            tell(dve, "f_prompt", 1)
            values_half(4 * i + 3)
            dve.wait_ge(*made("f_o", i + 1))
            then(V.tensor_copy(fq[:, :, i * P:i * P + P], PS[:, banks("f_o", i)[0], :].rearrange("p (h t) -> p h t", h=HEADS)))
            tell(dve, "empty_f_o", 1)
        dve.wait_ge(*told(f"evac{P_GLU % 2}", P_GLU // 2 + 1))
        dve.wait_ge(sem(f"evac{(P_GLU + 1) % 2}"), (P_GLU + 1) // 2 + 1)
        then(V.tensor_tensor(su[:, :, :], su[:, :, :], sgl[:, :, :], ALU.mult))
        tell(dve, "glu_done", 1)
        for n in range(8, 16):
            values_half(n)
        dve.wait_ge(*told("gh_done", 2))
        then(V.tensor_tensor(gl1[:, :, :], su[:, :, :], gh1[:, :, :], ALU.subtract))
        tell(dve, "branch1", 1)
        dve.wait_ge(*made("f_ost", 1))
        then(V.tensor_tensor(fq[:, :, SEQ:TOK], PS[:, 7, :].rearrange("p (h b) -> p h b", h=HEADS)[:, :, 0:DEC],
                             osmp[:, :].rearrange("p (h b) -> p h b", h=HEADS), ALU.add))
        tell(dve, "empty_f_ost", 1)
        tell(dve, "f_out", 1)

        done = [C_POOL_END]

        def low(n, slot, count):
            dve.wait_ge(*told("hi_done", count))
            V.tensor_tensor(w_lo[:, slot, :, :], raw[:, slot, :, :], w_hi[:, slot, :, :], ALU.subtract).then_inc(sem("lo_dve"), 1)

        def lows(n0, n1):
            for n in range(n0, n1):
                low(n, n % RING, n + 1)

        def loop_lows(c0, i, per, j0, j1):
            for j in range(j0, j1):
                low(None, (c0 + j) % RING, i * per + (c0 + j + 1))

        lows(150, 154)
        dve.wait_ge(*told("bh0_done", 1))
        then(V.tensor_tensor(bl0[:, :, :], fq[:, :, :], bh0[:, :, :], ALU.subtract))
        tell(dve, "branch0", 1)

        def merge(dg):
            g0 = (dg % 2) * 16
            last_gate = P_GATE[dg] + 7
            dve.wait_ge(*told(f"evac{last_gate % 2}", last_gate // 2 + 1))
            dve.wait_ge(sem(f"evac{(last_gate - 1) % 2}"), (last_gate - 1) // 2 + 1)
            for m in range(8):
                k, half = MERGE_ORDER[m // 2], m % 2
                p, n = P_MERGE[dg] + m, C_MERGE[dg] + m
                dve.wait_ge(*told("used", n + 1))
                g = gates[:, g0 + 4 * k + 2 * half:g0 + 4 * k + 2 * half + 2, :]
                V.tensor_tensor(g, g, PS[:, BANK(p):BANK(p) + 2, 0:TOK], ALU.mult).then_inc(sem(f"evac{p % 2}"), 1)
                if m < 7:
                    lows(n + RING, n + RING + 1)
            for par_ in range(2):
                p = P_MERGE[dg] + 6 + par_
                dve.wait_ge(*told(f"evac{p % 2}", p // 2 + 1))
            G = lambda k: gates[:, g0 + 4 * k:g0 + 4 * k + 4, :]
            then(V.tensor_tensor(G(0), G(0), G(1), ALU.add))
            lows(C_MERGE[dg] + 7 + RING, C_MERGE[dg] + 8 + RING)
            then(V.tensor_tensor(G(2), G(2), G(3), ALU.add))
            then(V.tensor_tensor(G(0), G(0), G(2), ALU.add))
            tell(dve, "sums", 1)

        def merged_low(dg):
            dve.wait_ge(*told("mh_done", dg + 1))
            V.tensor_tensor(ml[:, 4 * dg:4 * dg + 4, :], gates[:, (dg % 2) * 16:(dg % 2) * 16 + 4, :],
                            mh[:, 4 * dg:4 * dg + 4, :], ALU.subtract).then_inc(sem("ml_done"), 1)
            dve.wait_ge(*told("ml_done", dg + 1))
            tell(dve, "merged", 1)

        dve.wait_ge(*told("t8_stored1", 16 * 3))
        dve.wait_ge(*told("fox_stored", 16 * 6))
        merge(0)
        merge(1)
        merged_low(0)
        for dg in (2, 3):
            c0 = C_GATE[dg]
            lows(c0 + 4, c0 + 6)
            merged_low(dg - 1)
            lows(c0 + 6, c0 + 8)
            with nc.vector.Fori(1, 4) as i:
                loop_lows(c0, i, 8, 0, 8)
            lows(C_MERGE[dg], C_MERGE[dg] + 4)
            merge(dg)
        merged_low(3)
        lows(C_OUT + 4, C_OUT + 6)

        def out_pass(c0, p0, dst, i, m, per, passes, first=False):
            acc, before_it = (acc0, 0) if dst is xp else (acc1, 8)
            tiles = ds(i * (2 * passes) + 2 * m, 2)
            p = p0 + m
            dve.wait_ge(*told("used", i * (passes * per) + (c0 + per * (m + 1))))
            V.scalar_tensor_tensor(dst[:, tiles, :], xl[:, tiles, :], ALPHA, PS[:, BANK(p):BANK(p) + 2, 0:TOK],
                                   ALU.mult, ALU.add).then_inc(sem(f"evac{p % 2}"), 1)
            dve.wait_ge(*told(f"evac{p % 2}", i * (passes // 2) + (p // 2 + 1)))
            V.scalar_tensor_tensor(dst[:, tiles, :], xh[:, tiles, :], ALPHA, dst[:, tiles, :],
                                   ALU.mult, ALU.add).then_inc(sem("res_done"), 1)
            dve.wait_ge(sem("res_done"), i * passes + (m + 1 + before_it))
            if first:
                V.tensor_copy(acc[:, :, :], dst[:, tiles, :]).then_inc(sem("acc_done"), 1)
            else:
                dve.wait_ge(sem("acc_done"), i * passes + (m + before_it))
                V.tensor_tensor(acc[:, :, :], acc[:, :, :], dst[:, tiles, :], ALU.add).then_inc(sem("acc_done"), 1)

        lows(C_OUT + 6, C_OUT + 7)
        out_pass(C_OUT, P_OUT, xp, 0, 0, 4, 2, first=True)
        lows(C_OUT + 7, C_OUT + 8)
        with nc.vector.Fori(1, 4) as i:
            loop_lows(C_OUT, i, 8, 0, 3)
            out_pass(C_OUT, P_OUT, xp, i - 1, 1, 4, 2)
            loop_lows(C_OUT, i, 8, 3, 7)
            out_pass(C_OUT, P_OUT, xp, i, 0, 4, 2)
            loop_lows(C_OUT, i, 8, 7, 8)
        lows(C_UP, C_UP + 3)
        out_pass(C_OUT, P_OUT, xp, 3, 1, 4, 2)
        lows(C_UP + 3, C_UP + 4)

        def layer_norm(n, src, finish):
            dve.wait_ge(*made("l_mu", n + 1))
            then(V.tensor_scalar(mu_r[:, 0, :], PS[:, 4 + 2 * n, 0:TOK], 1.0 / D_MODEL, None, ALU.mult))
            tell(dve, "empty_l_mu", 1)
            part = lambda t4: src[:, 4 * t4:4 * t4 + 4, :]
            spread = lambda r: mu_r[:, r:r + 1, :].to_broadcast([P, 4, TOK])
            for a, b in zip(LN_PARTS, LN_PARTS[1:] + [KT]):
                then(V.tensor_tensor(src[:, a:b, :], src[:, a:b, :],
                                     mu_r[:, 0:1, :].to_broadcast([P, b - a, TOK]), ALU.subtract))
                tell(dve, f"centred{n}", 1)
            dve.wait_ge(sem(f"deviation{n}"), 1)
            then(V.reciprocal(mu_r[:, 1, :], mu_r[:, 1, :]))
            tell(dve, "empty_l_var", 1)
            for t4 in range(4):
                then(V.tensor_tensor(part(t4), part(t4), spread(1), ALU.mult))
                if n == 0:
                    tell(dve, "x1_norm", 1)
                dst = sq if n == 0 else src
                for t in range(4 * t4, 4 * t4 + 4):
                    do(V.tensor_scalar(dst[:, t, :], src[:, t, :], lnv[:, 2 * n, t:t + 1], lnv[:, 2 * n + 1, t:t + 1],
                                       ALU.mult, ALU.add))
                steps.settle()
                finish(t4)

        def x1_low(t4):
            dve.wait_ge(sem("x1_hi"), t4 + 1)
            c = slice(4 * t4, 4 * t4 + 4)
            V.tensor_tensor(xl[:, c, :], sq[:, c, :], xh[:, c, :], ALU.subtract).then_inc(sem("x1_ready"), 1)

        then(V.memset(small[:, 62:63], LN_EPS))
        layer_norm(0, xp, x1_low)
        dve.wait_ge(*told("x1_ready", 4))

        pg, pu = P_UP, P_UP + 1

        def h_product(i, hh_count):
            dve.wait_ge(*told("used", i * 8 + (C_UP + 8)))
            dve.wait_ge(*told(f"evac{pg % 2}", i + (pg // 2 + 1)))
            if hh_count is not None:
                dve.wait_ge(*told("hl_done", hh_count))
            V.tensor_tensor(hx[:, :, :], sg[:, :, :], PS[:, BANK(pu):BANK(pu) + 2, 0:TOK], ALU.mult).then_inc(sem(f"evac{pu % 2}"), 1)

        def h_low(i):
            dve.wait_ge(*told("hh_done", i + 1))
            V.tensor_tensor(hl[:, ds(i * 2, 2), :], hx[:, :, :], hh[:, ds(i * 2, 2), :], ALU.subtract).then_inc(sem("hl_done"), 1)

        lows(C_UP + 4, C_UP + 8)
        loop_lows(C_UP, 1, 8, 0, 3)
        h_product(0, None)
        loop_lows(C_UP, 1, 8, 3, 7)
        h_low(0)
        loop_lows(C_UP, 1, 8, 7, 8)
        with nc.vector.Fori(2, UP_STEPS) as i:
            loop_lows(C_UP, i, 8, 0, 3)
            h_product(i - 1, i - 1)
            loop_lows(C_UP, i, 8, 3, 7)
            h_low(i - 1)
            loop_lows(C_UP, i, 8, 7, 8)
        lows(C_DOWN, C_DOWN + 3)
        h_product(UP_STEPS - 1, UP_STEPS - 1)
        lows(C_DOWN + 3, C_DOWN + 4)
        h_low(UP_STEPS - 1)

        def down_turn(i, last):
            for m in range(4):
                a, b = 11 * m, 11 * m + 11
                loop_lows(C_DOWN, i, 44, a + (4 if (m == 0) else 3), b)
                if last and m == 3:
                    out_pass(C_DOWN, P_DOWN, yp, i, m, 11, 4)
                    break
                if m == 3:
                    loop_lows(C_DOWN, i + 1, 44, 0, 3)
                    out_pass(C_DOWN, P_DOWN, yp, i, m, 11, 4)
                    loop_lows(C_DOWN, i + 1, 44, 3, 4)
                else:
                    loop_lows(C_DOWN, i, 44, b, b + 3)
                    out_pass(C_DOWN, P_DOWN, yp, i, m, 11, 4, first=(i == 0 and m == 0))

        down_turn(0, False)
        down_turn(1, True)
        layer_norm(1, yp, lambda t4: tell(dve, "y_ready", 1))

    ctx.close()


_INS = ("x_prompt x_sample cache_k cache_v cache_logf page_table state_s5_re state_s5_im state_hgrn w_in fox_bf "
        "s5_lambda_re s5_lambda_im s5_log_dt s5_b_re s5_b_im s5_c_re s5_c_im s5_d s5_w_glu s5_b_glu hgrn_lb "
        "hgrn_norm_g gmlp_ln_g gmlp_ln_b gmlp_w_s gmlp_b_s w_branch w_out ln1_g ln1_b w_ffn_up w_ffn_down ln2_g "
        "ln2_b").split()
_OUTS = {
    "y_prompt": (1, SEQ, D_MODEL), "y_sample": (DEC, 1, D_MODEL),
    "fox_k_prompt": (1, 1, SEQ, HEADS, P), "fox_v_prompt": (1, 1, SEQ, HEADS, P), "fox_logf_prompt": (1, 1, SEQ, HEADS),
    "fox_k_sample": (1, DEC, 1, HEADS, P), "fox_v_sample": (1, DEC, 1, HEADS, P), "fox_logf_sample": (1, DEC, 1, HEADS),
    "s5_re_prompt": (1, 1, 32, 64), "s5_im_prompt": (1, 1, 32, 64), "s5_re_sample": (1, DEC, 32, 64),
    "s5_im_sample": (1, DEC, 32, 64), "hgrn_prompt": (1, 1, HEADS, P, P), "hgrn_sample": (1, DEC, HEADS, P, P),
    "gmlp_v_sample": (1, DEC, 1, MIX),
}


def kernel(**inputs):
    import numpy as np
    import concourse.bacc as bacc
    from concourse.bass_utils import run_bass_kernel_spmd

    nc = bacc.Bacc("TRN2", target_bir_lowering=False, num_devices=1)
    arrays, A = {}, {}
    for name in _INS:
        a = np.ascontiguousarray(inputs[name])
        arrays["in_" + name] = a
        A[name] = nc.dram_tensor("in_" + name, a.shape, mybir.dt.from_np(a.dtype), kind="ExternalInput").ap()
    O = {name: nc.dram_tensor("out_" + name, shape, F32, kind="ExternalOutput").ap() for name, shape in _OUTS.items()}
    trunk(nc, A, O)
    r = run_bass_kernel_spmd(nc, [arrays], core_ids=[0])
    return tuple(r.results[0]["out_" + name] for name in _OUTS)
```
